# Optimizing a Trainium2 kernel written in Bass

```python
import jax
import jax.numpy as jnp
from jax import lax
import numpy as np

D_MODEL = 1024
BATCH = 1
SEQ = 512
DEPTH = 1

GLA_HEADS = 4
GLA_DK = D_MODEL // (2 * GLA_HEADS)
GLA_DV = D_MODEL // GLA_HEADS
GLA_LOWRANK = 16
GLA_TAU = 16.0
GLA_CHUNK = 16

ATTN_GROUPS = ((128, 1), (512, 4), (2048, 16))
ATTN_HEADS_PER_GROUP = 4
ATTN_HEAD_DIM = 64
ATTN_HEADS = ATTN_HEADS_PER_GROUP * len(ATTN_GROUPS)
ROPE_THETA = 10000.0

D_FF = 2816
CONV_WIDTH = 3
EPS = 1e-6

GLA_QK_WIDTH = GLA_HEADS * GLA_DK
GLA_V_WIDTH = GLA_HEADS * GLA_DV
ATTN_WIDTH = ATTN_HEADS * ATTN_HEAD_DIM
ATTN_OUT_WIDTH = ATTN_HEADS_PER_GROUP * ATTN_HEAD_DIM
IN_WIDTHS = (GLA_QK_WIDTH, GLA_QK_WIDTH, GLA_V_WIDTH, GLA_V_WIDTH, GLA_LOWRANK,
             ATTN_WIDTH, ATTN_WIDTH, ATTN_WIDTH, D_MODEL, D_MODEL)
D_IN = sum(IN_WIDTHS)

kernel_name = "hybrid_gla_dilated_attn_convffn_block"

def rmsnorm(x, w):
    xf = x.astype(jnp.float32)
    y = xf * lax.rsqrt(jnp.mean(xf * xf, axis=-1, keepdims=True) + EPS)
    return (y * w.astype(jnp.float32)).astype(x.dtype)

def rotary(t, positions):
    half = t.shape[-1] // 2
    inv_freq = ROPE_THETA ** (-jnp.arange(half, dtype=jnp.float32) / half)
    ang = positions.astype(jnp.float32)[..., None] * inv_freq
    cos = jnp.cos(ang)[:, :, None, :]
    sin = jnp.sin(ang)[:, :, None, :]
    tf = t.astype(jnp.float32)
    t1, t2 = tf[..., :half], tf[..., half:]
    return jnp.concatenate([t1 * cos - t2 * sin, t2 * cos + t1 * sin], axis=-1).astype(t.dtype)

def gla_chunked(q, k, v, log_a):
    B, S, H, dk = q.shape
    dv = v.shape[-1]
    C = GLA_CHUNK
    N = S // C

    def chunks(t):
        return t.astype(jnp.float32).reshape(B, N, C, H, -1).transpose(0, 3, 1, 2, 4)

    qc = chunks(q) * (dk ** -0.5)
    kc, vc, lac = chunks(k), chunks(v), chunks(log_a)
    b = jnp.cumsum(lac, axis=3)
    b_last = b[:, :, :, -1:, :]
    qg = qc * jnp.exp(b)
    kg = kc * jnp.exp(-b)
    kd = kc * jnp.exp(b_last - b)

    causal = jnp.tril(jnp.ones((C, C), dtype=bool))
    attn = jnp.where(causal, jnp.einsum('bhnid,bhnjd->bhnij', qg, kg), 0.0)
    o_intra = jnp.einsum('bhnij,bhnjv->bhniv', attn, vc)

    def step(state, xs):
        qg_n, kd_n, v_n, dec_n = xs
        o_n = jnp.einsum('bhcd,bhdv->bhcv', qg_n, state)
        state = dec_n[..., None] * state + jnp.einsum('bhcd,bhcv->bhdv', kd_n, v_n)
        return state, o_n

    xs = (qg.transpose(2, 0, 1, 3, 4), kd.transpose(2, 0, 1, 3, 4), vc.transpose(2, 0, 1, 3, 4),
          jnp.exp(b_last[:, :, :, 0, :]).transpose(2, 0, 1, 3))
    state0 = jnp.zeros((B, H, dk, dv), jnp.float32)
    _, o_inter = lax.scan(step, state0, xs)
    o = o_intra + o_inter.transpose(1, 2, 0, 3, 4)
    return o.transpose(0, 2, 3, 1, 4).reshape(B, S, H, dv)

def dilated_group_attention(q, k, v, window, dilation):
    B, S, H, Dh = q.shape
    r = dilation
    L = S // r
    blk = window // dilation
    nblk = -(-L // blk)
    Lp = nblk * blk

    def to_sub(t):
        t = t.reshape(B, L, r, H, Dh).transpose(0, 2, 3, 1, 4)
        t = jnp.pad(t, ((0, 0), (0, 0), (0, 0), (0, Lp - L), (0, 0)))
        return t.reshape(B, r, H, nblk, blk, Dh)

    def with_prev(t):
        prev = jnp.pad(t, ((0, 0), (0, 0), (0, 0), (1, 0), (0, 0), (0, 0)))[:, :, :, :-1]
        return jnp.concatenate([prev, t], axis=-2)

    qb = to_sub(q)
    kc = with_prev(to_sub(k))
    vc = with_prev(to_sub(v))
    s = jnp.einsum('brhnid,brhnjd->brhnij', qb, kc).astype(jnp.float32) * (Dh ** -0.5)
    i_idx = jnp.arange(blk)[:, None]
    j_idx = jnp.arange(2 * blk)[None, :]
    dist = i_idx + blk - j_idx
    band = (dist >= 0) & (dist <= blk)
    n_idx = jnp.arange(nblk)[:, None, None]
    valid = band[None] & ((n_idx > 0) | (j_idx >= blk)[None])
    s = jnp.where(valid, s, -jnp.inf)
    m = jnp.max(s, axis=-1, keepdims=True)
    p = jnp.exp(s - m)
    denom = jnp.sum(p, axis=-1, keepdims=True)
    o = jnp.einsum('brhnij,brhnjd->brhnid', p, vc.astype(jnp.float32)) / denom
    lse = (m + jnp.log(denom))[..., 0]
    o = o.reshape(B, r, H, Lp, Dh)[:, :, :, :L].transpose(0, 3, 1, 2, 4).reshape(B, S, H, Dh)
    lse = lse.reshape(B, r, H, Lp)[..., :L].transpose(0, 3, 1, 2).reshape(B, S, H)
    return o, lse

def dilated_attention(aq, ak, av, positions):
    B, S, _ = aq.shape
    q = rotary(aq.reshape(B, S, ATTN_HEADS, ATTN_HEAD_DIM), positions)
    k = rotary(ak.reshape(B, S, ATTN_HEADS, ATTN_HEAD_DIM), positions)
    v = av.reshape(B, S, ATTN_HEADS, ATTN_HEAD_DIM)
    outs, lses = [], []
    for g, (window, dilation) in enumerate(ATTN_GROUPS):
        sl = slice(g * ATTN_HEADS_PER_GROUP, (g + 1) * ATTN_HEADS_PER_GROUP)
        o_g, lse_g = dilated_group_attention(q[:, :, sl], k[:, :, sl], v[:, :, sl], window, dilation)
        outs.append(o_g)
        lses.append(lse_g)
    wts = jax.nn.softmax(jnp.stack(lses, axis=0), axis=0)
    o = jnp.sum(wts[..., None] * jnp.stack(outs, axis=0), axis=0)
    return o.reshape(B, S, ATTN_OUT_WIDTH).astype(aq.dtype)

def causal_conv_ffn_hidden(h, w_up, conv_w, conv_b):
    S = h.shape[1]
    u = h @ w_up
    up = jnp.pad(u, ((0, 0), (CONV_WIDTH - 1, 0), (0, 0)))
    u = conv_b + sum(conv_w[i] * up[:, i:i + S] for i in range(CONV_WIDTH))
    value, gate = jnp.split(u, 2, axis=-1)
    return jax.nn.gelu(gate, approximate=False) * value

def setup_inputs(seed: int = 0) -> dict:
    key = jax.random.key(seed)
    ks = jax.random.split(key, 20)
    f32 = jnp.float32

    def nrm(k, shape, scale):
        return jax.random.normal(k, shape, f32) * scale

    def gain(k, shape):
        return 1.0 + 0.02 * jax.random.normal(k, shape, f32)

    L = DEPTH
    x = nrm(ks[0], (BATCH, SEQ, D_MODEL), 1.0)
    c = nrm(ks[1], (BATCH, D_MODEL), 1.0)
    positions = (jax.random.randint(ks[2], (BATCH, 1), 0, 1024, dtype=jnp.int32)
                 + jnp.arange(SEQ, dtype=jnp.int32)[None, :])
    return {
        'x': x,
        'c': c,
        'positions': positions,
        'ada_w': nrm(ks[3], (L, D_MODEL, 6 * D_MODEL), D_MODEL ** -0.5),
        'ada_b': nrm(ks[4], (L, 6 * D_MODEL), 0.02),
        'norm1_w': gain(ks[5], (L, D_MODEL)),
        'w_in': nrm(ks[6], (L, D_MODEL, D_IN), D_MODEL ** -0.5),
        'gla_gate_w2': nrm(ks[7], (L, GLA_LOWRANK, GLA_QK_WIDTH), GLA_LOWRANK ** -0.5),
        'gla_gate_b': nrm(ks[8], (L, GLA_QK_WIDTH), 0.1),
        'gla_norm_w': gain(ks[9], (L, GLA_DV)),
        'w_gla_branch': nrm(ks[10], (L, GLA_V_WIDTH, D_MODEL), GLA_V_WIDTH ** -0.5),
        'w_attn_branch': nrm(ks[11], (L, ATTN_OUT_WIDTH, D_MODEL), ATTN_OUT_WIDTH ** -0.5),
        'w_out': nrm(ks[12], (L, D_MODEL, D_MODEL), D_MODEL ** -0.5),
        'norm2_w': gain(ks[13], (L, D_MODEL)),
        'w_up': nrm(ks[14], (L, D_MODEL, 2 * D_FF), D_MODEL ** -0.5),
        'conv_w': nrm(ks[15], (L, CONV_WIDTH, 2 * D_FF), CONV_WIDTH ** -0.5),
        'conv_b': nrm(ks[16], (L, 2 * D_FF), 0.01),
        'w_down': nrm(ks[17], (L, D_FF, D_MODEL), D_FF ** -0.5),
        'final_norm_w': gain(ks[18], (D_MODEL,)),
    }

def reference(x, c, positions, ada_w, ada_b, norm1_w, w_in, gla_gate_w2, gla_gate_b, gla_norm_w,
              w_gla_branch, w_attn_branch, w_out, norm2_w, w_up, conv_w, conv_b, w_down, final_norm_w):
    B, S, _ = x.shape
    split_at = np.cumsum(IN_WIDTHS)[:-1].tolist()
    for layer in range(DEPTH):
        mod = jax.nn.silu(c) @ ada_w[layer] + ada_b[layer]
        shift1, scale1, gate1, shift2, scale2, gate2 = jnp.split(mod[:, None, :], 6, axis=-1)

        h = rmsnorm(x, norm1_w[layer]) * (1 + scale1) + shift1
        gq, gk, gv, gr, g_lr, aq, ak, av, merge_a, merge_b = jnp.split(h @ w_in[layer], split_at, axis=-1)

        log_a = jax.nn.log_sigmoid((g_lr @ gla_gate_w2[layer] + gla_gate_b[layer]).astype(jnp.float32)) / GLA_TAU
        o_gla = gla_chunked(gq.reshape(B, S, GLA_HEADS, GLA_DK), gk.reshape(B, S, GLA_HEADS, GLA_DK),
                            gv.reshape(B, S, GLA_HEADS, GLA_DV), log_a.reshape(B, S, GLA_HEADS, GLA_DK))
        o_gla = rmsnorm(o_gla.astype(x.dtype), gla_norm_w[layer]).reshape(B, S, GLA_V_WIDTH) * jax.nn.silu(gr)
        y_gla = o_gla @ w_gla_branch[layer]

        y_attn = dilated_attention(aq, ak, av, positions) @ w_attn_branch[layer]

        mixed = jax.nn.sigmoid(merge_a) * y_gla + jax.nn.sigmoid(merge_b) * y_attn
        x = x + gate1 * (mixed @ w_out[layer])

        h2 = rmsnorm(x, norm2_w[layer]) * (1 + scale2) + shift2
        hidden = causal_conv_ffn_hidden(h2, w_up[layer], conv_w[layer], conv_b[layer])
        x = x + gate2 * (hidden @ w_down[layer])
    return rmsnorm(x, final_norm_w)


_drawn_inputs = setup_inputs


def setup_inputs(seed=0):
    import zlib

    import numpy as np

    out = dict(_drawn_inputs(seed))
    spreads = {}
    factors = {'norm1_w': 4.355,
     'gla_gate_b': 3.168,
     'gla_norm_w': 8.0,
     'norm2_w': 12.655,
     'conv_b': 29.22,
     'final_norm_w': 8.609}
    for name, (base, spread) in spreads.items():
        noise = np.random.default_rng([zlib.crc32(name.encode()), seed]).standard_normal(out[name].shape)
        drawn = base * np.exp(spread * noise) if base else spread * noise
        out[name] = jnp.asarray(drawn.astype(out[name].dtype))
    for name, factor in factors.items():
        out[name] = (out[name] * factor).astype(out[name].dtype)
    return out
```

```python
from contextlib import ExitStack

import numpy as np

import concourse.bass as bass
from concourse import mybir

F32 = mybir.dt.float32
F32R = mybir.dt.float32r
I32 = mybir.dt.int32
U32 = mybir.dt.uint32
ACT = mybir.ActivationFunctionType
ALU = mybir.AluOpType
AX = mybir.AxisListType

P = 128
SEQ = 512
D = 1024
KT = D // P
NB = SEQ // P
HEADS = 4
DV = 256
LOWRANK = 16
CHUNK = 16
NCH = P // CHUNK
DH = 64
GROUPS = 3
DIL = 4
D_FF = 2816
FT = D_FF // P
EPS = 1e-6
NEG = -3.0e38
ROUND = 1.5 * 2.0 ** 23
TWO_PI = (6.28125, 0.0019350051879882812, 3.0199159795074593e-07)

GLA_QK = HEADS * P
COL_GQ = 0
COL_GK = COL_GQ + GLA_QK
COL_GV = COL_GK + GLA_QK
COL_GR = COL_GV + HEADS * DV
COL_LR = COL_GR + HEADS * DV
COL_AQ = COL_LR + LOWRANK
COL_AK = COL_AQ + GROUPS * HEADS * DH
COL_AV = COL_AK + GROUPS * HEADS * DH
COL_MA = COL_AV + GROUPS * HEADS * DH
COL_MB = COL_MA + D
UW = 256
UE = KT * UW

C_ID = 0
C_TRI = C_ID + P
C_KEEP = C_TRI + P + NCH + 1
C_MSK = C_KEEP + P
C_MOD = C_MSK + 3 * P
C_FRQ = C_MOD + P
C_ALL = C_FRQ + 1

V_C, V_N1, V_N2, V_FN, V_GN, V_AB = 0, 8, 16, 24, 32, 34
ROWS_A = V_AB + 6 * KT
ROWS_B = 4 * FT
V_CW0 = ROWS_A
V_CW1 = V_CW0 + 2 * FT
V_CW2 = V_CW1 + 2 * FT
V_CB = V_CW2 + 2 * FT
V_ALL = V_CB + 2 * FT


def shape_constants():
    c = np.zeros((P, C_ALL), np.float32)
    row, col = np.arange(P)[:, None], np.arange(P)[None, :]
    c[:, C_ID:C_ID + P] = row == col
    same = row // CHUNK == col // CHUNK
    c[:, C_TRI:C_TRI + P] = np.where(same & (row <= col), -1.0 / 16.0, 0.0)
    for n in range(NCH + 1):
        c[:, C_TRI + P + n] = np.where(row[:, 0] < CHUNK * n, -1.0 / 16.0, 0.0)
    c[:, C_KEEP:C_KEEP + P] = col >= row
    c[:, C_MSK:C_MSK + P] = np.where(col >= row, 0.0, NEG)
    c[:, C_MSK + P:C_MSK + 2 * P] = np.where(col <= row, 0.0, NEG)
    c[:, C_MSK + 2 * P:C_MSK + 3 * P] = np.where(col <= row, 0.0, NEG)
    c[:, C_MOD:C_MOD + P] = np.where((col <= row) & ((row - col) % 4 == 0), 0.0, NEG)
    half = DH // 2
    freq = np.float32(10000.0) ** (-np.arange(half, dtype=np.float32) / np.float32(half))
    c[:, C_FRQ] = np.tile(freq.astype(np.float32), P // half)
    return c


UNITS = ([("v", g, 0) for g in range(GROUPS)]
         + [("qk", p, g) for p in range(2) for g in range(GROUPS)]
         + [("lr", 0, 0)]
         + [(kind, h, 0) for h in range(HEADS) for kind in ("gqk", "gv", "gr")]
         + [("ma", u, 0) for u in range(4)]
         + [("mb", u, 0) for u in range(4)]
         + [("wa", 0, 0)]
         + [("wg", u, 0) for u in range(4)]
         + [("wo", u, 0) for u in range(4)])
N_UNITS = len(UNITS)
UNIT = {u: n for n, u in enumerate(UNITS)}


def tiles_of(unit):
    return {"lr": 1, "wa": 8}.get(unit[0], 2)


TILES = []
for _u in UNITS:
    TILES += [(_u, t) for t in range(tiles_of(_u))]
    if _u == ("gqk", 0, 0):
        TILES += [("z", b) for b in range(NB)]
    if _u == ("qk", 1, 1):
        TILES += [("ada", 0)]
    if _u == ("gv", 2, 0):
        TILES += [("ada", 1)]
TILE = {t: n for n, t in enumerate(TILES)}
N_TILES = len(TILES)

RAW = []
for _n in range(N_UNITS):
    RAW.append(("w", _n))
    if _n < 16:
        RAW.append(("ada", _n))
RAW_AT = {r: q for q, r in enumerate(RAW)}
N_RAW = len(RAW)


def dmas_of(raw):
    return 2 if raw[0] == "w" and UNITS[raw[1]][0] in ("qk", "gqk") else 1


LANDED = []
_count = [0, 0]
for _q, _r in enumerate(RAW):
    _count[_q % 2] += 16 * dmas_of(_r)
    LANDED.append(_count[_q % 2])
LANDED_END = tuple(_count)
FIRST_FFN = N_RAW
DOWN_UNITS = FT // 2


def hybrid_block_kernel(nc, x, c, positions, ada_w, ada_b, norm1_w, w_in, gate_w2, gate_b, gla_norm_w,
                        w_gla, w_attn, w_out, norm2_w, w_up, conv_w, conv_b, w_down, final_w, consts, out):
    assert N_UNITS % 2 == 1 and N_RAW % 2 == 1
    ctx = ExitStack()
    with ctx:
        def sb(name, shape, dt=F32):
            return ctx.enter_context(nc.sbuf_tensor(name, shape, dt))

        def sem(name):
            return ctx.enter_context(nc.semaphore(name))

        x_spill = nc.dram_tensor("x_spill", [P, KT * SEQ], F32, kind="Internal").ap()

        raw = sb("raw", [P, 2, UE])
        w_hi = sb("w_hi", [P, 2, UE], F32R)
        w_lo = sb("w_lo", [P, 2, UE], F32R)
        h_hi = sb("h_hi", [P, KT, SEQ], F32R)
        h_lo = sb("h_lo", [P, KT, SEQ], F32R)
        cst = sb("cst", [P, C_ALL])
        ones = sb("ones", [P, P])
        vecs = sb("vecs", [P, V_ALL])
        rows_a = sb("rows_a", [ROWS_A, P])
        rows_b = sb("rows_b", [ROWS_B, 2, P])
        c_silu = sb("c_silu", [P, KT])
        mod = sb("mod", [P, 6 * KT])
        gain = sb("gain", [P, 2, KT])
        ada_acc = sb("ada_acc", [P, 2 * D])

        def region(*places):
            got = []
            with ExitStack() as scope:
                at = 0
                for n, (name, kb, shape, dt) in enumerate(sorted(places, key=lambda p: p[1])):
                    off = int(kb * 1024)
                    assert off >= at, name
                    if off > at:
                        scope.enter_context(nc.sbuf_tensor(f"gap_{name}", [P, (off - at) // 4], F32))
                    got.append(scope.enter_context(nc.sbuf_tensor(name, shape, dt)))
                    size = 4
                    for s in shape[1:]:
                        size *= s
                    at = off + (size + 31) // 32 * 32
            order = sorted(range(len(places)), key=lambda i: places[i][1])
            back = [None] * len(places)
            for i, t in zip(order, got):
                back[i] = t
            return back

        ada_in, x_tok, xT0, sq, sq_sum, rstd, ntmp, ada_in7, cs = region(
            ("ada_in", 0, [P, 7, 2 * D], F32), ("x_tok", 56, [P, NB, D], F32), ("xT0", 72, [P, KT, SEQ], F32),
            ("sq", 88, [P, 2, SEQ], F32), ("sq_sum", 92, [P, SEQ], F32), ("rstd", 94, [P, SEQ], F32),
            ("ntmp", 96, [P, 2, SEQ], F32), ("ada_in7", 100, [P, 2 * D], F32), ("cs", 108, [P, 2, SEQ], F32))
        qk, rope, oa_hi, oa_lo, ocomb, osum, orec, oa32, v_ext, S, PT, mx, mg, rowm, negm = region(
            ("qk", 0, [DH, GROUPS, 2, 2, SEQ], F32), ("rope", 24, [P, 4, SEQ], F32),
            ("oa_hi", 32, [P, 2, SEQ], F32R), ("oa_lo", 36, [P, 2, SEQ], F32R),
            ("ocomb", 40, [P, SEQ], F32), ("osum", 42, [P, SEQ], F32), ("orec", 44, [P, SEQ], F32),
            ("oa32", 46, [P, SEQ], F32),
            ("v_ext", 56, [P, NB, GROUPS, HEADS, P], F32), ("S", 80, [P, 2, 1920], F32),
            ("PT", 95, [P, 1920], F32), ("mx", 102.5, [P, 8, 2], F32), ("mg", 102.75, [P, 2, 4], F32),
            ("rowm", 103, [2, 2, SEQ], F32), ("negm", 107, [P, 8, 2], F32))
        q_in, k_in, gv, gr, logs, za, lrT, w2b, og_hi, og_lo, kk, at_sb, kt_sb, ke, state, eb, enb, ed, qB, o_sb, osq, ors = region(
            ("q_in", 0, [P, 2, SEQ], F32), ("k_in", 4, [P, 2, SEQ], F32), ("gv_sb", 8, [P, 2, NB, DV], F32),
            ("gr_sb", 16, [P, 2, 2, SEQ], F32), ("logs", 24, [P, NB, SEQ], F32),
            ("za", 48, [P, 2, SEQ], F32), ("lrT", 52, [32, SEQ], F32), ("w2b", 54, [LOWRANK + 1, SEQ], F32),
            ("og_hi", 56, [P, KT, SEQ], F32R), ("og_lo", 72, [P, KT, SEQ], F32R),
            ("kk", 88, [P, NCH, P], F32), ("at_sb", 92, [P, 2, P], F32), ("kt_sb", 93, [P, 2, P], F32),
            ("ke", 94, [P, P], F32), ("state", 94.5, [P, DV], F32), ("eb", 95.5, [P, SEQ], F32),
            ("enb", 97.5, [P, SEQ], F32), ("ed", 99.5, [P, NB, NCH + 1], F32), ("qB", 99.75, [P, SEQ], F32),
            ("o_sb", 101.75, [P, 2, SEQ], F32), ("osq", 105.75, [P, 2, SEQ], F32), ("ors", 109.75, [P, SEQ], F32))
        mix_hi, mix_lo, sA, sB, mtmp = region(
            ("mix_hi", 0, [P, KT, SEQ], F32R), ("mix_lo", 16, [P, KT, SEQ], F32R),
            ("sA", 40, [P, KT, SEQ], F32), ("sB", 88, [P, KT, SEQ], F32), ("mtmp", 104, [P, 2, SEQ], F32))
        hid, x1, conv, sq2, sq_sum2, rstd2, ntmp2, hs_hi, hs_lo = region(
            ("hid", 0, [P, FT, SEQ], F32), ("x1", 56, [P, KT, SEQ], F32), ("conv", 72, [P, 2, 2, SEQ], F32),
            ("sq2", 80, [P, 2, SEQ], F32), ("sq_sum2", 84, [P, SEQ], F32), ("rstd2", 86, [P, SEQ], F32),
            ("ntmp2", 88, [P, 2, SEQ], F32),
            ("hs_hi", 92, [P, 2, 2, SEQ], F32R), ("hs_lo", 100, [P, 2, 2, SEQ], F32R))
        y_tok, = region(("y_tok", 0, [P, NB, D], F32))
        pos_i = ada_acc[:, 0:SEQ].bitcast(I32)
        ang, turns, ang_abs = (ada_acc[:, i * SEQ:(i + 1) * SEQ] for i in range(1, 4))

        bank = [ctx.enter_context(nc.psum_tensor(f"bank{i}", [P, SEQ], F32)) for i in range(8)]
        side = bank[2:]

        landed = [sem(f"raw_landed{i}") for i in range(2)]
        raw_used = sem("raw_used")
        hi_done = sem("hi_done")
        acc_ready = sem("acc_ready")
        acc_free = [sem(f"acc_free{i}") for i in range(2)]
        rows_in, conv_in, cst_in, x_in, pos_in = (sem(n) for n in ("rows_in", "conv_in", "cst_in", "x_in", "pos_in"))
        ada_landed = [sem(f"ada_landed{i}") for i in range(KT)]
        w2_in = sem("w2_in")
        ones_set = sem("ones_set")
        vec_ps, vec_sb, silu_done = sem("vec_ps"), sem("vec_sb"), sem("silu_done")
        xt_ps, xt_sb, spilled, x_back = sem("xt_ps"), sem("xt_sb"), sem("spilled"), sem("x_back")
        mod1_ps, mod_done, gain_done = sem("mod1_ps"), sem("mod_done"), sem("gain_done")
        sq_done, sum_done, ssq_ps, root_done, rstd_done = (sem(n) for n in (
            "sq_done", "sum_done", "ssq_ps", "root_done", "rstd_done"))
        nt_done, hh_done, hl_done = sem("nt_done"), sem("hh_done"), sem("hl_done")
        rot_dve, rot_sum, rot_act = sem("rot_dve"), sem("rot_sum"), sem("rot_act")
        v_ones = sem("v_ones")
        rope_sum, qk_in = sem("rope_sum"), sem("qk_in")
        sc_done, msk_done, mx1_done, mx_done = sem("sc_done"), sem("msk_done"), sem("mx1_done"), sem("mx_done")
        mxr_ps, rowmax_done, mxc_ps, negm_done = (sem(n) for n in ("mxr_ps", "rowmax_done", "mxc_ps", "negm_done"))
        exp_done, tr_ps, pt_act, pt_dve, pv_done = (sem(n) for n in ("exp_done", "tr_ps", "pt_act", "pt_dve", "pv_done"))
        perm_sb, osum_done, orec_done, oa32_done, oahi_done, oalo_done = (sem(n) for n in (
            "perm_sb", "osum_done", "orec_done", "oa32_done", "oahi_done", "oalo_done"))
        lr_ones, z_abs, z_exp, z_ln, logs_done = (sem(n) for n in (
            "lr_ones", "z_abs", "z_exp", "z_ln", "logs_done"))
        b_ps, gexp_done, qg_done, qB_done, kk_step, kk_done = (sem(n) for n in (
            "b_ps", "gexp_done", "qg_done", "qB_done", "kk_step", "kk_done"))
        at_zero, at_ps, at_done, kt_done, p3_done, st_done = (sem(n) for n in (
            "at_zero", "at_ps", "at_done", "kt_done", "p3_done", "st_done"))
        o_done, osq_done, osum2_done, gssq_ps, groot_done, grstd_done, on_done, og32_done, oghi_done, oglo_done = (
            sem(n) for n in ("o_done", "osq_done", "osqsum_done", "gssq_ps", "groot_done", "grstd_done", "on_done",
                             "og32_done", "oghi_done", "oglo_done"))
        mix32_done, mixhi_done, mixlo_done = sem("mix32_done"), sem("mixhi_done"), sem("mixlo_done")
        ffn_ready, tap2_done, tap_done, gelu_done, hid_done = (sem(n) for n in (
            "ffn_ready", "tap2_done", "tap_done", "gelu_done", "hid_done"))
        hs_hi_done, hs_lo_done, down_done, down_tile = (sem(n) for n in (
            "hs_hi_done", "hs_lo_done", "down_done", "down_tile"))
        x2_done, y_done, yt_ps, yt_act, yt_dve, stored = (sem(n) for n in (
            "x2_done", "y_done", "yt_ps", "yt_act", "yt_dve", "stored"))

        block = ctx.enter_context(nc.Block())

        def yt_bank(i):
            return i

        def last_tile(n):
            return TILE[(UNITS[n], tiles_of(UNITS[n]) - 1)]

        def views(n):
            rs, ws = RAW_AT[("w", n)] % 2, n % 2
            kind = UNITS[n][0]
            if kind == "qk":
                r = raw[:, rs, :].rearrange("p (k a t f) -> p t k a f", k=KT, a=4, t=2)
                hv = w_hi[:, ws, :].rearrange("p (k t a f) -> p t k a f", k=KT, t=2, a=4)
                lv = w_lo[:, ws, :].rearrange("p (k t a f) -> p t k a f", k=KT, t=2, a=4)
                return [(r[:, t], hv[:, t], lv[:, t]) for t in range(2)]
            size = KT * LOWRANK if kind == "lr" else UE
            return [(raw[:, rs, 0:size], w_hi[:, ws, 0:size], w_lo[:, ws, 0:size])]

        def evacuated(eng, tile):
            i = TILE[tile]
            eng.wait_ge(acc_free[i % 2], i // 2 + 1)

        BANK_AT = [0, 512, 896, 1408]
        BANK_W = [512, 384, 512, 512]

        def score_blocks(bk):
            if bk == 0:
                return [(0, 2 * P, 1), (2 * P, 2 * P, 2)]
            if bk == 1:
                return [(0, 2 * P, 3), (2 * P, P, 0)]
            return [(r * P, P, NB + r) for r in range(DIL)]

        @block.sync
        def _(sp):
            sp.dma_start(rows_a[V_C:V_C + KT, :], c.rearrange("a (k p) -> (a k) p", p=P)).then_inc(rows_in, 16)
            sp.dma_start(rows_a[V_N1:V_N1 + KT, :], norm1_w.rearrange("a (k p) -> (a k) p", p=P)).then_inc(rows_in, 16)
            sp.dma_start(rows_a[V_AB:ROWS_A, :], ada_b.rearrange("a (k p) -> (a k) p", p=P)).then_inc(rows_in, 16)
            sp.dma_start(rows_a[V_N2:V_N2 + KT, :], norm2_w.rearrange("a (k p) -> (a k) p", p=P)).then_inc(rows_in, 16)
            sp.dma_start(rows_a[V_FN:V_FN + KT, :], final_w.rearrange("(k p) -> k p", p=P)).then_inc(rows_in, 16)
            sp.dma_start(rows_a[V_GN:V_GN + 2, :], gla_norm_w.rearrange("a (k p) -> (a k) p", p=P)).then_inc(rows_in, 16)
            ada_v = ada_w.rearrange("a (k p) n -> (a k) p n", p=P)
            for k in range(KT):
                dst = ada_in[:, k, :] if k < 7 else ada_in7[:, :]
                sp.dma_start(dst, ada_v[k, :, 0:2 * D]).then_inc(ada_landed[k], 16)

            w_in_v = w_in.rearrange("a (k p) n -> p (a k) n", p=P)

            def cols(view, at, width=UW):
                return view[:, :, at:at + width]

            wg_v = w_gla.rearrange("a (k p) n -> p (a k) n", p=P)
            wo_v = w_out.rearrange("a (k p) n -> p (a k) n", p=P)
            wa_v = w_attn.rearrange("a (k p) n -> p (a k) n", p=P)

            def load(q):
                what, n = RAW[q]
                slot = q % 2
                done = landed[slot]
                if q >= 2:
                    sp.wait_ge(raw_used, q - 1)
                if what == "ada":
                    r, k = n // KT, n % KT
                    sp.dma_start(raw[:, slot, :], ada_v[k, :, 2 * D * (r + 1):2 * D * (r + 2)]).then_inc(done, 16)
                    return
                kind, a, b = UNITS[n]
                dst = raw[:, slot, :].rearrange("p (k n) -> p k n", k=KT)
                if kind == "qk":
                    off = b * HEADS * DH + a * 2 * DH
                    sp.dma_start(dst[:, :, 0:P], cols(w_in_v, COL_AQ + off, P)).then_inc(done, 16)
                    sp.dma_start(dst[:, :, P:UW], cols(w_in_v, COL_AK + off, P)).then_inc(done, 16)
                elif kind == "gqk":
                    sp.dma_start(dst[:, :, 0:P], cols(w_in_v, COL_GQ + a * P, P)).then_inc(done, 16)
                    sp.dma_start(dst[:, :, P:UW], cols(w_in_v, COL_GK + a * P, P)).then_inc(done, 16)
                elif kind == "lr":
                    small = raw[:, slot, 0:KT * LOWRANK].rearrange("p (k n) -> p k n", k=KT)
                    sp.dma_start(small, cols(w_in_v, COL_LR, LOWRANK)).then_inc(done, 16)
                elif kind == "wa":
                    sp.dma_start(raw[:, slot, :].rearrange("p (k n) -> p k n", k=2), wa_v).then_inc(done, 16)
                else:
                    src = {"v": cols(w_in_v, COL_AV + a * UW), "gv": cols(w_in_v, COL_GV + a * DV),
                           "gr": cols(w_in_v, COL_GR + a * DV), "ma": cols(w_in_v, COL_MA + a * UW),
                           "mb": cols(w_in_v, COL_MB + a * UW),
                           "wg": wg_v[:, :, (a % 4) * UW:(a % 4 + 1) * UW],
                           "wo": wo_v[:, :, (a % 4) * UW:(a % 4 + 1) * UW]}[kind]
                    sp.dma_start(dst, src).then_inc(done, 16)

            def shuffle(j):
                p, g = divmod(j, GROUPS)
                sp.wait_ge(rope_sum, 2 * j + 2)
                if p == 1:
                    sp.wait_ge(sc_done, 8)
                for half in range(2):
                    for a in range(4):
                        sp.dma_start(qk[32 * half:32 * half + 32, g, a // 2, a % 2, :],
                                     rope[32 * a:32 * a + 32, half, :]).then_inc(qk_in, 16)

            for q in range(N_RAW):
                load(q)
                if q == 1:
                    sp.dma_start(rows_b[:, 0, :], conv_w[0, 0:2, :].rearrange("i (k p) -> (i k) p", p=P)).then_inc(conv_in, 16)
                    sp.dma_start(rows_b[0:2 * FT, 1, :], conv_w[0, 2:3, :].rearrange("i (k p) -> (i k) p", p=P)).then_inc(conv_in, 16)
                    sp.dma_start(rows_b[2 * FT:ROWS_B, 1, :], conv_b.rearrange("i (k p) -> (i k) p", p=P)).then_inc(conv_in, 16)
                    sp.wait_ge(xt_sb, KT)
                    sp.dma_start(x_spill, xT0[:, :, :].rearrange("p k n -> p (k n)")).then_inc(spilled, 16)
                what, n = RAW[q]
                if what == "w" and 6 <= n < 12:
                    shuffle(n - 6)
                if q == 2:
                    sp.wait_ge(mod1_ps, 1)
                    sp.dma_start(w2b[0:LOWRANK, :], gate_w2.rearrange("a r n -> (a r) n")).then_inc(w2_in, 16)
                    sp.dma_start(w2b[LOWRANK:LOWRANK + 1, :], gate_b).then_inc(w2_in, 16)
                if what == "w" and n == UNIT[("wo", 0, 0)]:
                    sp.wait_ge(spilled, 16)
                if what == "w" and n == UNIT[("wo", 1, 0)]:
                    sp.wait_ge(acc_ready, last_tile(UNIT[("wg", 3, 0)]) + 1)
                    sp.dma_start(x1[:, :, :].rearrange("p k n -> p (k n)"), x_spill).then_inc(x_back, 16)

            up_v = w_up.rearrange("a (k p) n -> p (a k) n", p=P)

            def load_up(i, s):
                slot = (s + 1) % 2
                dst = raw[:, slot, :].rearrange("p (k t n) -> p k t n", k=KT, t=2)
                sp.wait_ge(raw_used, i + (FIRST_FFN - 1))
                for t in range(2):
                    sp.dma_start(dst[:, :, t, :], up_v[:, :, bass.ds(i * P + t * D_FF, P)]).then_inc(landed[slot], 16)

            with sp.Fori(0, FT // 2) as a:
                for s in range(2):
                    load_up(2 * a + s, s)

            down_v = w_down.rearrange("a (k p) n -> p (a k) n", p=P)

            def load_down(j, s):
                slot = (s + 1) % 2
                sp.wait_ge(raw_used, j + (FIRST_FFN + FT - 1))
                for t in range(2):
                    sp.dma_start(raw[:, slot, t * D:(t + 1) * D].rearrange("p (k n) -> p k n", k=1),
                                 down_v[:, bass.ds(2 * j + t, 1), :]).then_inc(landed[slot], 16)

            with sp.Fori(0, DOWN_UNITS // 2) as a:
                for s in range(2):
                    load_down(2 * a + s, s)
            load_down(DOWN_UNITS - 1, 0)

            out_v = out.rearrange("a (b p) n -> p (a b) n", p=P)
            for i in range(8):
                half, b = divmod(i, NB)
                sp.wait_ge(yt_act if i % 2 == 0 else yt_dve, i // 2 + 1)
                sp.dma_start(out_v[:, b, half * SEQ:(half + 1) * SEQ], y_tok[:, b, half * SEQ:(half + 1) * SEQ]).then_inc(stored, 16)
            sp.wait_ge(stored, 8 * 16)

        @block.gpsimd
        def _(pool):
            pool.memset(ones[:, :], 1.0).then_inc(ones_set, 1)

            def sum_squares(part, sq_t, sum_t):
                for k in range(KT):
                    i = part * KT + k
                    pool.wait_ge(sq_done, i + 1)
                    if k == 0 and part > 0:
                        pool.wait_ge(ssq_ps, part)
                    if k > 0:
                        pool.wait_ge(sum_done, i)
                    if k == 0:
                        pool.tensor_copy(sum_t[:, :], sq_t[:, k % 2, :]).then_inc(sum_done, 1)
                    else:
                        pool.tensor_tensor(sum_t[:, :], sum_t[:, :], sq_t[:, k % 2, :], ALU.add).then_inc(sum_done, 1)

            sum_squares(0, sq, sq_sum)
            pool.wait_ge(xt_ps, KT)
            pool.wait_ge(hl_done, KT)
            pool.wait_ge(spilled, 16)
            for hd in range(2):
                part = v_ext[:, :, :, hd::2, (1 - hd) * DH:(2 - hd) * DH]
                pool.memset(part.rearrange("p b g h n -> p (b g) h n"), 1.0).then_inc(v_ones, 1)
            for j in range(2 * GROUPS):
                for t in range(2):
                    evacuated(pool, (("qk", *divmod(j, GROUPS)), t))
                pool.tensor_tensor(rope[:, 0, :], rope[:, 0, :], rope[:, 2, :], ALU.subtract).then_inc(rope_sum, 1)
                pool.tensor_tensor(rope[:, 1, :], rope[:, 1, :], rope[:, 3, :], ALU.add).then_inc(rope_sum, 1)
            pool.memset(lrT[:, :], 1.0).then_inc(lr_ones, 1)
            for h in range(HEADS):
                pool.wait_ge(osq_done, h + 1)
                pool.tensor_tensor(osq[:, 0, :], osq[:, 0, :], osq[:, 1, :], ALU.add).then_inc(osum2_done, 1)
            for m in range(KT):
                evacuated(pool, (("wg", m // 2, 0), m % 2))
                pool.tensor_tensor(sB[:, m, :], sB[:, m, :], mtmp[:, m % 2, :], ALU.add).then_inc(mix32_done, 1)
            sum_squares(1, sq2, sq_sum2)
            sum_squares(2, sq2, sq_sum2)

        @block.scalar
        def _(act):
            act.dma_start(cst[:, :], consts).then_inc(cst_in, 16)
            x_v = x.rearrange("a (b p) n -> p (a b) n", p=P)
            for b in range(NB):
                act.dma_start(x_tok[:, b, :], x_v[:, b, :]).then_inc(x_in, 16)
            act.dma_start(pos_i, positions.broadcast_to((P, SEQ))).then_inc(pos_in, 16)

            def split_hi(n):
                if n == N_UNITS:
                    return split_hi_ffn(0, 0, acc_ready, last_tile(n - 2) + 1)
                q = RAW_AT[("w", n)]
                act.wait_ge(landed[q % 2], LANDED[q])
                if n >= 2:
                    act.wait_ge(acc_ready, last_tile(n - 2) + 1)
                for r, hv, _ in views(n):
                    last = act.activation(hv, r, ACT.Copy)
                last.then_inc(hi_done, 1)

            def split_hi_ffn(pair, odd, used, value):
                slot = 1 - odd
                act.wait_ge(landed[slot], pair * 32 + (LANDED_END[slot] + 32))
                act.wait_ge(used, value)
                act.activation(w_hi[:, slot, :], raw[:, slot, :], ACT.Copy).then_inc(hi_done, 1)

            def square(part, k, sq_t, src):
                if k >= 2:
                    act.wait_ge(sum_done, part * KT + k - 1)
                elif part > 0:
                    act.wait_ge(sum_done, part * KT)
                act.activation(sq_t[:, k % 2, :], src[:, k, :], ACT.Square).then_inc(sq_done, 1)

            def root(part, dst, src):
                act.wait_ge(ssq_ps, part + 1)
                act.activation(dst[:, :], src[:, :], ACT.Sqrt, scale=1.0 / D, bias=EPS).then_inc(root_done, 1)

            def shifted(part, k, tmp, shift_col):
                act.wait_ge(nt_done, part * KT + k + 1)
                act.activation(h_hi[:, k, :], tmp[:, k % 2, :], ACT.Identity,
                               bias=mod[:, shift_col + k:shift_col + k + 1]).then_inc(hh_done, 1)

            act.wait_ge(vec_sb, 1)
            act.activation(c_silu[:, :], vecs[:, V_C:V_C + KT], ACT.Silu).then_inc(silu_done, 1)
            for k in range(KT):
                act.wait_ge(xt_ps, k + 1)
                act.activation(xT0[:, k, :], bank[3 + k % 4][:, :], ACT.Copy).then_inc(xt_sb, 1)
                act.wait_ge(xt_sb, k + 1)
                square(0, k, sq, xT0)
            act.wait_ge(rot_dve, 7)
            act.activation(cs[:, 1, :], ang, ACT.Sin).then_inc(rot_act, 1)
            act.activation(ang_abs, ang, ACT.Abs).then_inc(rot_act, 1)
            act.wait_ge(rot_act, 2)
            act.activation(cs[:, 0, :], ang_abs, ACT.Sin, scale=-1.0, bias=float(np.pi / 2)).then_inc(rot_act, 1)
            root(0, rstd, bank[0])
            split_hi(0)
            for k in range(KT):
                shifted(0, k, ntmp, 0)

            def acc(tile):
                i = TILE[tile]
                act.wait_ge(acc_ready, i + 1)
                return bank[i % 2]

            def free(tile, ins):
                ins.then_inc(acc_free[TILE[tile] % 2], 1)

            def exps(hh):
                p, hd = divmod(hh, 2)
                act.wait_ge(negm_done, p + 1)
                for bk in range(4):
                    for col, width, i in score_blocks(bk):
                        at = BANK_AT[bk] + col
                        last = act.activation(S[:, hd, at:at + width], S[:, hd, at:at + width], ACT.Exp,
                                              bias=negm[:, i, hd:hd + 1], scale=DH ** -0.5)
                    last.then_inc(exp_done, 1)

            def attention(p, i):
                if i in (4, 5):
                    hh = 2 * p + i - 4
                    for bk in range(2):
                        act.wait_ge(tr_ps, 4 * hh + bk + 1)
                        if hh >= 1:
                            act.wait_ge(pv_done, hh)
                        at = BANK_AT[bk]
                        act.activation(PT[:, at:at + BANK_W[bk]], side[bk][:, 0:BANK_W[bk]],
                                       ACT.Copy).then_inc(pt_act, 1)
                if i in (3, 4):
                    exps(2 * p + i - 3)
                if i in (5, 6):
                    hh = 2 * p + i - 5
                    act.wait_ge(pv_done, hh + 1)
                    if hh >= 1:
                        act.wait_ge(osum_done, hh)
                    act.activation(ocomb[:, :].rearrange("p (l r) -> p r l", r=DIL),
                                   side[5][:, :].rearrange("p (r l) -> p r l", r=DIL),
                                   ACT.Copy).then_inc(perm_sb, 1)
                if i == 6:
                    act.wait_ge(oa32_done, 2 * p + 2)
                    act.activation(oa_hi[:, p, :], oa32[:, :], ACT.Copy).then_inc(oahi_done, 1)

            def gates():
                for b in range(NB):
                    z = acc(("z", b))
                    if b >= 2:
                        act.wait_ge(logs_done, 2 * (b - 1))
                    act.activation(za[:, b % 2, :], z[:, :], ACT.Abs).then_inc(z_abs, 1)
                    act.wait_ge(z_abs, b + 1)
                    act.activation(za[:, b % 2, :], za[:, b % 2, :], ACT.Exp, scale=-1.0).then_inc(z_exp, 1)
                    act.wait_ge(z_exp, b + 1)
                    act.activation(za[:, b % 2, :], za[:, b % 2, :], ACT.Ln, bias=1.0).then_inc(z_ln, 1)

            def gla(h, i):
                if i == 0:
                    act.wait_ge(b_ps, h + 1)
                    if h > 0:
                        act.wait_ge(kk_done, NB * h)
                        act.wait_ge(st_done, 3 * h)
                    act.activation(eb[:, :], side[0][:, :], ACT.Exp).then_inc(gexp_done, 1)
                    act.activation(enb[:, :], side[0][:, :], ACT.Exp, scale=-1.0).then_inc(gexp_done, 1)
                    act.activation(ed[:, :, :].rearrange("p b n -> p (b n)"), side[1][:, 0:NB * (NCH + 1)],
                                   ACT.Exp).then_inc(gexp_done, 1)
                if 2 <= i <= 5:
                    u = NB * h + i - 2
                    act.wait_ge(at_ps, u + 1)
                    if u >= 2:
                        act.wait_ge(p3_done, u - 1)
                    act.activation(kt_sb[:, u % 2, :], side[3][:, 0:P], ACT.Copy).then_inc(kt_done, 1)
                if i == 6:
                    act.wait_ge(o_done, 2 * h + 2)
                    if h > 0:
                        act.wait_ge(gssq_ps, h)
                    act.activation(osq[:, :, :], o_sb[:, :, :], ACT.Square).then_inc(osq_done, 1)
                if i == 8:
                    act.wait_ge(gssq_ps, h + 1)
                    if h > 0:
                        act.wait_ge(on_done, h)
                    act.activation(ors[:, :], side[0][:, :], ACT.Sqrt, scale=1.0 / DV, bias=EPS).then_inc(groot_done, 1)
                if i == 9:
                    act.wait_ge(og32_done, 2 * h + 2)
                    act.activation(og_hi[:, 2 * h:2 * h + 2, :], o_sb[:, :, :], ACT.Copy).then_inc(oghi_done, 1)

            def evac(n, t):
                kind, a, _ = UNITS[n]
                tile = (UNITS[n], t)
                src = acc(tile)
                if kind == "v":
                    act.wait_ge(v_ones, 2)
                    v = src[:, :].rearrange("p (b h n) -> p b h n", b=2, h=HEADS)
                    for hd in range(2):
                        last = act.activation(v_ext[:, 2 * t:2 * t + 2, a, hd::2, hd * DH:(hd + 1) * DH],
                                              v[:, :, hd::2, :], ACT.Copy)
                    free(tile, last)
                if kind == "lr":
                    act.wait_ge(lr_ones, 1)
                    free(tile, act.activation(lrT[0:LOWRANK, :], src[0:LOWRANK, :], ACT.Copy))
                if kind == "gqk":
                    if a < 2:
                        act.wait_ge(sc_done, 16)
                    else:
                        act.wait_ge(p3_done, NB * (a - 1))
                    dst, scale = ((q_in, float(P) ** -0.5), (k_in, 1.0))[t]
                    free(tile, act.activation(dst[:, a % 2, :], src[:, :], ACT.Copy, scale=scale))
                if kind == "gv":
                    if a >= 2:
                        act.wait_ge(p3_done, NB * (a - 1))
                    free(tile, act.activation(gv[:, a % 2, 2 * t:2 * t + 2, :].rearrange("p b n -> p (b n)"),
                                              src[:, :], ACT.Copy))
                if kind == "gr":
                    if a >= 2:
                        act.wait_ge(og32_done, 2 * (a - 1))
                    free(tile, act.activation(gr[:, a % 2, t, :], src[:, :], ACT.Silu))
                if kind == "ma":
                    if a == 0 and t == 0:
                        act.wait_ge(oalo_done, 2)
                        act.wait_ge(logs_done, 2 * NB)
                    free(tile, act.activation(sA[:, 2 * a + t, :], src[:, :], ACT.Sigmoid))
                if kind == "mb":
                    if a == 0 and t == 0:
                        act.wait_ge(p3_done, NB * HEADS)
                        act.wait_ge(st_done, 3 * HEADS)
                        act.wait_ge(o_done, 2 * HEADS)
                    if a == 3 and t == 0:
                        act.wait_ge(oglo_done, HEADS)
                    free(tile, act.activation(sB[:, 2 * a + t, :], src[:, :], ACT.Sigmoid))

            for g in range(GROUPS):
                n = UNIT[("v", g, 0)]
                split_hi(n + 1)
                for t in range(2):
                    evac(n, t)
            for g in range(GROUPS):
                split_hi(UNIT[("qk", 0, g)] + 1)
            for g in range(GROUPS):
                split_hi(UNIT[("qk", 1, g)] + 1)
                for t in range(2):
                    attention(0, 2 * g + t)
            split_hi(UNIT[("lr", 0, 0)] + 1)
            evac(UNIT[("lr", 0, 0)], 0)
            attention(0, 6)
            for h in range(HEADS):
                for u, kind in enumerate(("gqk", "gv", "gr")):
                    n = UNIT[(kind, h, 0)]
                    split_hi(n + 1)
                    for t in range(2):
                        i = 2 * u + t
                        evac(n, t)
                        if h == 0:
                            attention(1, i)
                        if h == 1 and i == 0:
                            attention(1, 6)
                        if h >= 2 and i in (0, 2, 3):
                            gla(h - 2, 6 + i)
                        if h >= 1:
                            gla(h - 1, i)
                    if kind == "gqk" and h == 0:
                        gates()
            for u in range(4):
                n = UNIT[("ma", u, 0)]
                split_hi(n + 1)
                for t in range(2):
                    i = 2 * u + t
                    evac(n, t)
                    if i in (0, 2, 3):
                        gla(2, 6 + i)
                    gla(3, i)
            for u in range(4):
                n = UNIT[("mb", u, 0)]
                split_hi(n + 1)
                for t in range(2):
                    if u == 0:
                        gla(3, 8 + t)
                    evac(n, t)
            split_hi(UNIT[("wa", 0, 0)] + 1)
            for u in range(4):
                split_hi(UNIT[("wg", u, 0)] + 1)
                for m in (2 * u, 2 * u + 1):
                    act.wait_ge(mix32_done, m + 1)
                    act.activation(mix_hi[:, m, :], sB[:, m, :], ACT.Copy).then_inc(mixhi_done, 1)
            for u in range(4):
                split_hi(UNIT[("wo", u, 0)] + 1)
                for m in (2 * u, 2 * u + 1):
                    evacuated(act, (("wo", u, 0), m % 2))
                    square(1, m, sq2, x1)
            root(1, rstd2, side[0])
            for k in range(KT):
                shifted(1, k, ntmp2, 3 * KT)

            def up(a, s, used, value, first=False):
                i = 2 * a + s
                split_hi_ffn(a + s, 1 - s, used, value)
                for t in range(2):
                    act.wait_ge(ffn_ready, 2 * i + (t + 1))
                    if not first:
                        act.wait_ge(hid_done, i - 1)
                    act.activation(conv[:, s, t, :], bank[2 * s + t][:, :], ACT.Identity,
                                   scale=vecs[:, bass.ds(i + (V_CW2 + t * FT), 1)],
                                   bias=vecs[:, bass.ds(i + (V_CB + t * FT), 1)]).then_inc(tap2_done, 1)
                act.wait_ge(tap_done, 4 * i + 4)
                act.activation(conv[:, s, 1, :], conv[:, s, 1, :], ACT.Gelu).then_inc(gelu_done, 1)

            up(0, 0, acc_ready, N_TILES, first=True)
            up(0, 1, ffn_ready, 2, first=True)
            with act.Fori(1, FT // 2) as a:
                for s in range(2):
                    up(a, s, ffn_ready, 4 * a + 2 * s)

            def hidden_hi(j, s):
                act.activation(hs_hi[:, s, :, :], hid[:, bass.ds(2 * j, 2), :], ACT.Copy).then_inc(hs_hi_done, 1)

            act.wait_ge(hid_done, 2)
            hidden_hi(0, 0)

            def down(a, s, used, value):
                j = 2 * a + s
                split_hi_ffn(a + (FT // 2 + s), 1 - s, used, value)
                act.wait_ge(hid_done, 2 * j + 4)
                hidden_hi(j + 1, 1 - s)

            down(0, 0, ffn_ready, 2 * FT)
            down(0, 1, down_done, 1)
            with act.Fori(1, DOWN_UNITS // 2) as a:
                for s in range(2):
                    down(a, s, down_done, 2 * a + s)
            for m in range(KT):
                act.wait_ge(x2_done, m + 1)
                square(2, m, sq2, x1)
            root(2, rstd2, bank[0])
            for i in range(0, 8, 2):
                half, b = divmod(i, NB)
                act.wait_ge(yt_ps, i + 1)
                act.activation(y_tok[:, b, half * SEQ:(half + 1) * SEQ], bank[yt_bank(i)][:, :],
                               ACT.Copy).then_inc(yt_act, 1)

        @block.vector
        def _(dve):
            dve.wait_ge(vec_ps, 1)
            dve.tensor_copy(vecs[:, 0:ROWS_A], bank[2][:, 0:ROWS_A]).then_inc(vec_sb, 1)
            dve.wait_ge(pos_in, 16)
            dve.tensor_copy(ang, pos_i).then_inc(rot_dve, 1)
            dve.wait_ge(cst_in, 16)
            dve.wait_ge(rot_dve, 1)
            dve.tensor_scalar(ang, ang, cst[:, C_FRQ:C_FRQ + 1], None, ALU.mult).then_inc(rot_dve, 1)
            dve.wait_ge(rot_dve, 2)
            dve.tensor_scalar(turns, ang, float(1.0 / (2 * np.pi)), ROUND, ALU.mult, ALU.add).then_inc(rot_dve, 1)
            dve.wait_ge(rot_dve, 3)
            dve.tensor_scalar(turns, turns, ROUND, None, ALU.subtract).then_inc(rot_dve, 1)
            for n, part in enumerate(TWO_PI):
                dve.wait_ge(rot_dve, 4 + n)
                last = dve.scalar_tensor_tensor(ang, turns, -part, ang, ALU.mult, ALU.add)
                if n < 2:
                    last.then_inc(rot_dve, 1)
                else:
                    last.then_inc(rot_sum, 1)
            dve.wait_ge(rot_sum, 1)
            dve.tensor_scalar(ang, ang, 3.1415925, -3.1415925, ALU.min, ALU.max).then_inc(rot_dve, 1)
            dve.wait_ge(mod1_ps, 1)
            dve.wait_ge(vec_sb, 1)
            dve.tensor_tensor(mod[:, 0:2 * KT], bank[7][:, 0:2 * KT], vecs[:, V_AB:V_AB + 2 * KT], ALU.add).then_inc(mod_done, 1)
            dve.wait_ge(mod_done, 1)
            dve.scalar_tensor_tensor(gain[:, 0, :], mod[:, KT:2 * KT], 1.0, vecs[:, V_N1:V_N1 + KT],
                                     ALU.add, ALU.mult).then_inc(gain_done, 1)

            def normalise(part, src, tmp, rs, shift_col):
                dve.wait_ge(root_done, part + 1)
                dve.reciprocal(rs[:, :], rs[:, :]).then_inc(rstd_done, 1)
                dve.wait_ge(rstd_done, part + 1)
                dve.wait_ge(gain_done, part + 1)
                for k in range(KT):
                    if k >= 2:
                        dve.wait_ge(hh_done, part * KT + k - 1)
                        dve.wait_ge(hl_done, part * KT + k - 1)
                    dve.scalar_tensor_tensor(tmp[:, k % 2, :], src[:, k, :], gain[:, part, k:k + 1], rs[:, :],
                                             ALU.mult, ALU.mult).then_inc(nt_done, 1)
                    if k >= 1:
                        lower(part, k - 1, tmp, shift_col)
                lower(part, KT - 1, tmp, shift_col)

            def lower(part, k, tmp, shift_col):
                dve.wait_ge(hh_done, part * KT + k + 1)
                dve.scalar_tensor_tensor(h_lo[:, k, :], tmp[:, k % 2, :], mod[:, shift_col + k:shift_col + k + 1],
                                         h_hi[:, k, :].bitcast(F32), ALU.add, ALU.subtract).then_inc(hl_done, 1)

            dve.wait_ge(xt_sb, KT)
            normalise(0, xT0, ntmp, rstd, 0)
            dve.wait_ge(vec_ps, 3)
            for half in range(2):
                dve.tensor_copy(vecs[:, ROWS_A + half * ROWS_B:ROWS_A + (half + 1) * ROWS_B],
                                bank[2][:, P * (half + 1):P * (half + 1) + ROWS_B]).then_inc(vec_sb, 1)
            dve.wait_ge(rot_act, 3)

            def split_lo(n):
                if n == N_UNITS:
                    return split_lo_ffn(0, 0)
                dve.wait_ge(hi_done, n + 1)
                for r, hv, lv in views(n):
                    last = dve.tensor_tensor(lv, r, hv.bitcast(F32), ALU.subtract)
                last.then_inc(raw_used, 1)

            def split_lo_ffn(pair, odd):
                slot = 1 - odd
                dve.wait_ge(hi_done, pair * 2 + (odd + N_UNITS + 1))
                dve.tensor_tensor(w_lo[:, slot, :], raw[:, slot, :], w_hi[:, slot, :].bitcast(F32),
                                  ALU.subtract).then_inc(raw_used, 1)

            def modulate(n):
                if n >= 2 * KT:
                    return
                r, k = divmod(n, KT)
                q = RAW_AT[("ada", n)]
                dve.wait_ge(landed[q % 2], LANDED[q])
                if k > 0:
                    dve.wait_ge(raw_used, RAW_AT[("ada", n - 1)] + 1)
                src = raw[:, q % 2, :]
                if k == 0:
                    if r == 1:
                        dve.wait_ge(acc_ready, TILE[("ada", 0)] + 1)
                    ins = dve.tensor_scalar(ada_acc[:, :], src, c_silu[:, 0:1], None, ALU.mult)
                else:
                    ins = dve.scalar_tensor_tensor(ada_acc[:, :], src, c_silu[:, k:k + 1], ada_acc[:, :],
                                                   ALU.mult, ALU.add)
                ins.then_inc(raw_used, 1)

            def acc(tile):
                i = TILE[tile]
                dve.wait_ge(acc_ready, i + 1)
                return bank[i % 2]

            def free(tile, ins):
                ins.then_inc(acc_free[TILE[tile] % 2], 1)

            def ada_tile(r):
                src = acc(("ada", r))
                at = 2 * KT * (r + 1)
                free(("ada", r), dve.tensor_tensor(mod[:, at:at + 2 * KT], src[:, 0:2 * KT],
                                                   vecs[:, V_AB + at:V_AB + at + 2 * KT], ALU.add))
                if r == 1:
                    evacuated(dve, ("ada", 1))
                    dve.scalar_tensor_tensor(gain[:, 1, :], mod[:, 4 * KT:5 * KT], 1.0, vecs[:, V_N2:V_N2 + KT],
                                             ALU.add, ALU.mult).then_inc(gain_done, 1)

            def rotate(j):
                p, g = divmod(j, GROUPS)
                if j > 0:
                    dve.wait_ge(qk_in, 16 * 8 * j)
                unit = ("qk", p, g)
                first = acc((unit, 0))
                dve.tensor_tensor(rope[:, 0, :], first[:, :], cs[:, 0, :], ALU.mult)
                free((unit, 0), dve.tensor_tensor(rope[:, 3, :], first[:, :], cs[:, 1, :], ALU.mult))
                second = acc((unit, 1))
                dve.tensor_tensor(rope[:, 2, :], second[:, :], cs[:, 1, :], ALU.mult)
                free((unit, 1), dve.tensor_tensor(rope[:, 1, :], second[:, :], cs[:, 0, :], ALU.mult))

            def mask_and_max(hh):
                p, hd = divmod(hh, 2)
                prev_own, own = cst[:, C_MSK:C_MSK + 2 * P], cst[:, C_MSK + P:C_MSK + 2 * P]
                own4 = own.rearrange("p (a n) -> p a n", a=1).broadcast_to((P, DIL, P))
                mod4 = cst[:, C_MOD:C_MOD + P].rearrange("p (a n) -> p a n", a=1).broadcast_to((P, DIL, P))
                two = prev_own.rearrange("p (a n) -> p a n", a=1).broadcast_to((P, 2, 2 * P))
                for bk in range(4):
                    dve.wait_ge(sc_done, 4 * hh + bk + 1)
                    if hh >= 2:
                        dve.wait_ge(tr_ps, 4 * (hh - 2) + bk + 1)
                    at, w = BANK_AT[bk], BANK_W[bk]
                    dst, src = S[:, hd, at:at + w], side[bk][:, 0:w]
                    if bk == 1:
                        m = cst[:, C_MSK:C_MSK + 3 * P]
                    else:
                        m = (two, None, own4, mod4)[bk]
                        n_b = 2 if bk == 0 else DIL
                        dst, src = (v.rearrange("p (a n) -> p a n", a=n_b) for v in (dst, src))
                    dve.tensor_tensor(dst, src, m, ALU.add).then_inc(msk_done, 1)
                for bk in range(4):
                    dve.wait_ge(msk_done, 4 * hh + bk + 1)
                    at = BANK_AT[bk]
                    if hd == 0 and bk == 0 and p > 0:
                        dve.wait_ge(mxr_ps, p)
                    if bk == 0:
                        dve.tensor_reduce(mx[:, 1:3, hd], S[:, hd, 0:4 * P].rearrange("p (a n) -> p a n", a=2),
                                          AX.X, ALU.max)
                    elif bk == 1:
                        dve.tensor_reduce(mx[:, 3:4, hd], S[:, hd, at:at + 2 * P], AX.X, ALU.max)
                        dve.tensor_reduce(mx[:, 0:1, hd], S[:, hd, at + 2 * P:at + 3 * P], AX.X, ALU.max)
                    else:
                        dve.tensor_reduce(mg[:, bk - 2, :], S[:, hd, at:at + 4 * P].rearrange("p (a n) -> p a n", a=DIL),
                                          AX.X, ALU.max).then_inc(mx1_done, 1)
                dve.wait_ge(mx1_done, 2 * hh + 2)
                dve.tensor_tensor(mx[:, NB:2 * NB, hd], mg[:, 0, :], mg[:, 1, :], ALU.max).then_inc(mx_done, 1)
                dve.wait_ge(mx_done, hh + 1)

            def attention(p, i):
                if i in (0, 1):
                    mask_and_max(2 * p + i)
                if i == 2:
                    dve.wait_ge(mxr_ps, p + 1)
                    if p > 0:
                        dve.wait_ge(mxc_ps, p)
                    dve.tensor_copy(rowm[:, 0, :], side[0][0:2, :]).then_inc(rowmax_done, 1)
                    dve.wait_ge(rowmax_done, 2 * p + 1)
                    dve.tensor_tensor(rowm[:, 1, :], side[1][0:2, :], rowm[:, 0, :], ALU.max).then_inc(rowmax_done, 1)
                if i == 3:
                    dve.wait_ge(mxc_ps, p + 1)
                    if p > 0:
                        dve.wait_ge(exp_done, 8 * p)
                    dve.tensor_scalar(negm[:, :, :].rearrange("p a b -> p (a b)"), side[0][:, 0:16],
                                      -DH ** -0.5, None, ALU.mult).then_inc(negm_done, 1)
                if i in (4, 5):
                    hh = 2 * p + i - 4
                    for bk in (2, 3):
                        dve.wait_ge(tr_ps, 4 * hh + bk + 1)
                        if hh >= 1:
                            dve.wait_ge(pv_done, hh)
                        at = BANK_AT[bk]
                        dve.tensor_copy(PT[:, at:at + BANK_W[bk]], side[bk][:, 0:BANK_W[bk]]).then_inc(pt_dve, 1)
                if i in (5, 6):
                    hh = 2 * p + i - 5
                    hd = hh % 2
                    top, bottom = slice(0, DH), slice(DH, P)
                    num, den = (top, bottom) if hd == 0 else (bottom, top)
                    dve.wait_ge(perm_sb, hh + 1)
                    if hh > 0:
                        dve.wait_ge(oa32_done, hh)
                    dve.tensor_tensor(osum[:, :], side[4][:, :], ocomb[:, :], ALU.add).then_inc(osum_done, 1)
                    dve.wait_ge(osum_done, hh + 1)
                    dve.reciprocal(orec[num, :], osum[den, :]).then_inc(orec_done, 1)
                    dve.wait_ge(orec_done, hh + 1)
                    if p > 0:
                        dve.wait_ge(oalo_done, p)
                    dve.tensor_tensor(oa32[num, :], osum[num, :], orec[num, :], ALU.mult).then_inc(oa32_done, 1)
                if i == 6:
                    dve.wait_ge(oa32_done, 2 * p + 2)
                    dve.wait_ge(oahi_done, p + 1)
                    dve.tensor_tensor(oa_lo[:, p, :], oa32[:, :], oa_hi[:, p, :].bitcast(F32),
                                      ALU.subtract).then_inc(oalo_done, 1)
                    dve.wait_ge(oalo_done, p + 1)

            def gates():
                dve.wait_ge(sc_done, 16)
                for b in range(NB):
                    z = acc(("z", b))
                    dve.wait_ge(z_abs, b + 1)
                    free(("z", b), dve.tensor_scalar(logs[:, b, :], z[:, :], -1.0, 0.0, ALU.mult, ALU.max))
                    evacuated(dve, ("z", b))
                    dve.wait_ge(z_ln, b + 1)
                    dve.tensor_tensor(logs[:, b, :], logs[:, b, :], za[:, b % 2, :], ALU.add).then_inc(logs_done, 2)

            def keys(h, b):
                u = NB * h + b
                if u >= 1:
                    dve.wait_ge(at_ps, u)
                    dve.wait_ge(kk_done, u)
                own = k_in[:, h % 2, b * P:(b + 1) * P]
                dve.tensor_copy(kk[:, :, :], own.rearrange("p (a n) -> p a n", a=1).broadcast_to((P, NCH, P))).then_inc(kk_step, 1)
                for n in range(NCH):
                    w = CHUNK * (n + 1)
                    decay = eb[:, b * P + w - 1:b * P + w]
                    dve.wait_ge(kk_step, NCH * u + n + 1)
                    dst = kk[:, n + 1, 0:w] if n < NCH - 1 else ke[:, :]
                    dve.tensor_scalar(dst, kk[:, n, 0:w], decay, None,
                                      ALU.mult).then_inc(kk_step if n < NCH - 1 else kk_done, 1)

            def gla(h, i):
                if i == 0:
                    q, k = q_in[:, h % 2, :], k_in[:, h % 2, :]
                    evacuated(dve, (("gqk", h, 0), 0))
                    evacuated(dve, (("gqk", h, 0), 1))
                    dve.wait_ge(gexp_done, 3 * h + 3)
                    dve.tensor_tensor(k, k, enb[:, :], ALU.mult).then_inc(qg_done, 1)
                    dve.tensor_tensor(q, q, eb[:, :], ALU.mult).then_inc(qg_done, 1)
                    if h > 0:
                        dve.wait_ge(p3_done, NB * h)
                    dve.wait_ge(qg_done, 2 * h + 2)
                    keys(h, 0)
                    chunks = q.rearrange("p (b n c) -> p b n c", b=NB, n=NCH)
                    start = ed[:, :, 0:NCH].rearrange("p b (n o) -> p b n o", o=1).broadcast_to((P, NB, NCH, CHUNK))
                    dve.tensor_tensor(qB[:, :].rearrange("p (b n c) -> p b n c", b=NB, n=NCH), chunks, start,
                                      ALU.mult).then_inc(qB_done, 1)
                if 2 <= i <= 5:
                    b = i - 2
                    u = NB * h + b
                    dve.wait_ge(at_ps, u + 1)
                    if u >= 2:
                        dve.wait_ge(p3_done, u - 1)
                    dve.copy_predicated(at_sb[:, u % 2, :], cst[:, C_KEEP:C_KEEP + P].bitcast(U32),
                                        side[2][:, 0:P]).then_inc(at_done, 1)
                    if b + 1 < NB:
                        keys(h, b + 1)
                if 3 <= i <= 5:
                    b = i - 3
                    dve.wait_ge(p3_done, NB * h + b + 1)
                    new = side[1][:, 64:64 + DV]
                    if b == 0:
                        if h > 0:
                            dve.wait_ge(st_done, 3 * h)
                        ins = dve.tensor_copy(state[:, :], new)
                    else:
                        dve.wait_ge(st_done, 3 * h + b)
                        ins = dve.scalar_tensor_tensor(state[:, :], state[:, :], ed[:, b, NCH:NCH + 1], new,
                                                       ALU.mult, ALU.add)
                    ins.then_inc(st_done, 1)
                if i == 6:
                    dve.wait_ge(p3_done, NB * h + NB)
                    if h > 0:
                        dve.wait_ge(oglo_done, h)
                    for v in range(2):
                        dve.tensor_copy(o_sb[:, v, :], side[4 + v][:, :]).then_inc(o_done, 1)
                if i == 8:
                    dve.wait_ge(groot_done, h + 1)
                    dve.reciprocal(ors[:, :], ors[:, :]).then_inc(grstd_done, 1)
                    dve.wait_ge(grstd_done, h + 1)
                    dve.wait_ge(osq_done, h + 1)
                    dve.tensor_tensor(o_sb[:, :, :], o_sb[:, :, :],
                                      ors[:, :].rearrange("p (a n) -> p a n", a=1).broadcast_to((P, 2, SEQ)),
                                      ALU.mult).then_inc(on_done, 1)
                    dve.wait_ge(on_done, h + 1)
                    evacuated(dve, (("gr", h, 0), 0))
                    evacuated(dve, (("gr", h, 0), 1))
                    for v in range(2):
                        dve.scalar_tensor_tensor(o_sb[:, v, :], o_sb[:, v, :], vecs[:, V_GN + v:V_GN + v + 1],
                                                 gr[:, h % 2, v, :], ALU.mult, ALU.mult).then_inc(og32_done, 1)
                if i == 9:
                    dve.wait_ge(og32_done, 2 * h + 2)
                    dve.wait_ge(oghi_done, h + 1)
                    dve.tensor_tensor(og_lo[:, 2 * h:2 * h + 2, :], o_sb[:, :, :],
                                      og_hi[:, 2 * h:2 * h + 2, :].bitcast(F32), ALU.subtract).then_inc(oglo_done, 1)

            split_lo(0)
            for n in range(GROUPS):
                modulate(n)
                split_lo(n + 1)
            for p in range(2):
                for g in range(GROUPS):
                    n = UNIT[("qk", p, g)]
                    modulate(n)
                    split_lo(n + 1)
                    if p == 1:
                        attention(0, 2 * g)
                    rotate(GROUPS * p + g)
                    if p == 1:
                        attention(0, 2 * g + 1)
                    if (p, g) == (1, 1):
                        ada_tile(0)
            n = UNIT[("lr", 0, 0)]
            modulate(n)
            split_lo(n + 1)
            attention(0, 6)
            for h in range(HEADS):
                for u, kind in enumerate(("gqk", "gv", "gr")):
                    n = UNIT[(kind, h, 0)]
                    modulate(n)
                    split_lo(n + 1)
                    for t in range(2):
                        i = 2 * u + t
                        if h == 0:
                            attention(1, i)
                        if h == 1 and i == 0:
                            attention(1, 6)
                            dve.memset(at_sb[:, :, :], 0.0).then_inc(at_zero, 1)
                            dve.wait_ge(at_zero, 1)
                        if h >= 2 and i in (0, 2, 3):
                            gla(h - 2, 6 + i)
                        if h >= 1:
                            gla(h - 1, i)
                    if kind == "gqk" and h == 0:
                        gates()
                    if (kind, h) == ("gv", 2):
                        ada_tile(1)
            for u in range(4):
                split_lo(UNIT[("ma", u, 0)] + 1)
                for t in range(2):
                    i = 2 * u + t
                    if i in (0, 2, 3):
                        gla(2, 6 + i)
                    gla(3, i)
            for u in range(4):
                split_lo(UNIT[("mb", u, 0)] + 1)
                if u == 0:
                    for i in (8, 9):
                        gla(3, i)
            n = UNIT[("wa", 0, 0)]
            split_lo(n + 1)
            for m in range(KT):
                tile = (UNITS[n], m)
                evacuated(dve, (("mb", m // 2, 0), m % 2))
                free(tile, dve.tensor_tensor(sB[:, m, :], acc(tile)[:, :], sB[:, m, :], ALU.mult))
            for u in range(4):
                split_lo(UNIT[("wg", u, 0)] + 1)
                for t in range(2):
                    m = 2 * u + t
                    tile = (("wg", u, 0), t)
                    if m >= 2:
                        dve.wait_ge(mix32_done, m - 1)
                    evacuated(dve, (("wa", 0, 0), m))
                    evacuated(dve, (("ma", m // 2, 0), m % 2))
                    src = acc(tile)
                    free(tile, dve.tensor_tensor(mtmp[:, m % 2, :], src[:, :], sA[:, m, :], ALU.mult))
                    dve.wait_ge(mixhi_done, m + 1)
                    dve.tensor_tensor(mix_lo[:, m, :], sB[:, m, :], mix_hi[:, m, :].bitcast(F32),
                                      ALU.subtract).then_inc(mixlo_done, 1)
            for u in range(4):
                split_lo(UNIT[("wo", u, 0)] + 1)
                for t in range(2):
                    m = 2 * u + t
                    tile = (("wo", u, 0), t)
                    dve.wait_ge(x_back, 16)
                    src = acc(tile)
                    free(tile, dve.scalar_tensor_tensor(x1[:, m, :], src[:, :], mod[:, 2 * KT + m:2 * KT + m + 1],
                                                        x1[:, m, :], ALU.mult, ALU.add))
            for t in range(2):
                evacuated(dve, (("wo", 3, 0), t))
            normalise(1, x1, ntmp2, rstd2, 3 * KT)

            def up(a, s):
                i = 2 * a + s
                split_lo_ffn(a + s, 1 - s)
                for t in range(2):
                    dve.wait_ge(tap2_done, 2 * i + (t + 1))
                    src = bank[2 * s + t]
                    for tap, col in ((1, V_CW1), (2, V_CW0)):
                        if tap == 2:
                            dve.wait_ge(tap_done, 4 * i + (2 * t + 1))
                        ins = dve.scalar_tensor_tensor(conv[:, s, t, tap:SEQ], src[:, 0:SEQ - tap],
                                                       vecs[:, bass.ds(i + (col + t * FT), 1)],
                                                       conv[:, s, t, tap:SEQ], ALU.mult, ALU.add)
                        ins.then_inc(tap_done, 1)
                dve.wait_ge(gelu_done, i + 1)
                dve.tensor_tensor(hid[:, bass.ds(i, 1), :].rearrange("p a n -> p (a n)"), conv[:, s, 0, :],
                                  conv[:, s, 1, :], ALU.mult).then_inc(hid_done, 1)

            with dve.Fori(0, FT // 2) as a:
                for s in range(2):
                    up(a, s)

            def hidden_lo(j, s):
                dve.wait_ge(hs_hi_done, j + 1)
                dve.tensor_tensor(hs_lo[:, s, :, :], hid[:, bass.ds(2 * j, 2), :], hs_hi[:, s, :, :].bitcast(F32),
                                  ALU.subtract).then_inc(hs_lo_done, 1)

            hidden_lo(0, 0)
            with dve.Fori(0, DOWN_UNITS // 2) as a:
                for s in range(2):
                    split_lo_ffn(a + (FT // 2 + s), 1 - s)
                    hidden_lo(2 * a + s + 1, 1 - s)
            for m in range(KT):
                dve.wait_ge(down_tile, m + 1)
                dve.scalar_tensor_tensor(x1[:, m, :], bank[m][:, :], mod[:, 5 * KT + m:5 * KT + m + 1], x1[:, m, :],
                                         ALU.mult, ALU.add).then_inc(x2_done, 1)
            dve.wait_ge(root_done, 3)
            dve.reciprocal(rstd2[:, :], rstd2[:, :]).then_inc(rstd_done, 1)
            dve.wait_ge(rstd_done, 3)
            for m in range(KT):
                dve.scalar_tensor_tensor(x1[:, m, :], x1[:, m, :], vecs[:, V_FN + m:V_FN + m + 1], rstd2[:, :],
                                         ALU.mult, ALU.mult).then_inc(y_done, 1)
            for i in range(1, 8, 2):
                half, b = divmod(i, NB)
                dve.wait_ge(yt_ps, i + 1)
                dve.tensor_copy(y_tok[:, b, half * SEQ:(half + 1) * SEQ], bank[yt_bank(i)][:, :]).then_inc(yt_dve, 1)

        @block.tensor
        def _(pe):
            ident = cst[:, C_ID:C_ID + P]

            def three(out_ap, w, x_, first, last):
                (wh, wl), (xh, xl) = w, x_
                pe.matmul(out_ap, wh, xh, start=first, stop=False, skip_group_check=True)
                pe.matmul(out_ap, wh, xl, start=False, stop=False, skip_group_check=True)
                return pe.matmul(out_ap, wl, xh, start=False, stop=last, skip_group_check=True)

            pe.wait_ge(cst_in, 16)
            pe.wait_ge(rows_in, 6 * 16)
            pe.transpose(bank[2][:, 0:ROWS_A], rows_a[:, :], ident[0:ROWS_A, 0:ROWS_A]).then_inc(vec_ps, 1)
            pe.wait_ge(x_in, NB * 16)
            for k in range(KT):
                if k >= 4:
                    pe.wait_ge(xt_sb, k - 3)
                for b in range(NB):
                    last = pe.transpose(bank[3 + k % 4][:, b * P:(b + 1) * P], x_tok[:, b, k * P:(k + 1) * P], ident)
                last.then_inc(xt_ps, 1)
            pe.wait_ge(ones_set, 1)
            pe.wait_ge(silu_done, 1)
            for k in range(KT):
                pe.wait_ge(ada_landed[k], 16)
                src = ada_in[:, k, :] if k < KT - 1 else ada_in7[:, :]
                for j in range(2 * KT):
                    last = pe.matmul(bank[7][:, j:j + 1], src[:, j * P:(j + 1) * P], c_silu[:, k:k + 1],
                                     start=(k == 0 and j == 0), stop=(k == KT - 1), skip_group_check=True)
                if k == 3:
                    pe.wait_ge(sum_done, KT)
                    pe.matmul(bank[0][:, :], ones[:, :], sq_sum[:, :], start=True, stop=True).then_inc(ssq_ps, 1)
            last.then_inc(mod1_ps, 1)
            pe.wait_ge(conv_in, 3 * 16)
            pe.wait_ge(vec_sb, 1)
            for half in range(2):
                pe.transpose(bank[2][:, P * (half + 1):P * (half + 1) + ROWS_B], rows_b[:, half, :],
                             ident[0:ROWS_B, 0:ROWS_B]).then_inc(vec_ps, 1)
            pe.wait_ge(root_done, 1)

            def take(i):
                if i >= 2:
                    pe.wait_ge(acc_free[i % 2], i // 2)
                return bank[i % 2]

            def product(n, t):
                kind, a, _ = UNITS[n]
                slot = n % 2
                i = TILE[(UNITS[n], t)]
                dst = take(i)
                if t == 0:
                    pe.wait_ge(raw_used, RAW_AT[("w", n)] + 1)
                if kind in ("v", "gv"):
                    for half in range(2):
                        blk = 2 * t + half
                        tok = slice(blk * P, (blk + 1) * P) if kind == "gv" or a == 0 else slice(blk, SEQ, DIL)
                        for k in range(KT):
                            if n == 0 and t == 0 and half == 0:
                                pe.wait_ge(hl_done, k + 1)
                            w = tuple(v[:, slot, k * UW:(k + 1) * UW] for v in (w_hi, w_lo))
                            s = tuple(v[:, k, tok] for v in (h_hi, h_lo))
                            last = three(dst[:, half * UW:(half + 1) * UW], s, w, k == 0, k == KT - 1)
                else:
                    if kind == "wa":
                        nk, width, at, src = 2, D, t * P, (oa_hi, oa_lo)
                    elif kind == "lr":
                        nk, width, at, src = KT, LOWRANK, 0, (h_hi, h_lo)
                    else:
                        nk, width, at = KT, UW, t * P
                        src = {"wg": (og_hi, og_lo), "wo": (mix_hi, mix_lo)}.get(kind, (h_hi, h_lo))
                    m = LOWRANK if kind == "lr" else P
                    if kind == "wa" and t == 0:
                        pe.wait_ge(oalo_done, 2)
                    if kind == "wg" and a == 0 and t == 0:
                        pe.wait_ge(oglo_done, HEADS)
                    for k in range(nk):
                        if kind == "wo" and a == 0 and t == 0:
                            pe.wait_ge(mixlo_done, k + 1)
                        w = tuple(v[:, slot, k * width + at:k * width + at + m] for v in (w_hi, w_lo))
                        last = three(dst[0:m, :], w, tuple(v[:, k, :] for v in src), k == 0, k == nk - 1)
                last.then_inc(acc_ready, 1)

            def ada_tile(r):
                dst = take(TILE[("ada", r)])
                pe.wait_ge(raw_used, RAW_AT[("ada", KT * (r + 1) - 1)] + 1)
                for j in range(2 * KT):
                    last = pe.matmul(dst[:, j:j + 1], ada_acc[:, j * P:(j + 1) * P], ones[:, 0:1],
                                     start=(j == 0), stop=True, skip_group_check=True)
                last.then_inc(acc_ready, 1)

            def scores(hh):
                p, hd = divmod(hh, 2)
                if hd == 0:
                    pe.wait_ge(qk_in, 16 * 8 * GROUPS * (p + 1))
                for bk in range(4):
                    if hh >= 1:
                        pe.wait_ge(msk_done, 4 * (hh - 1) + bk + 1)
                    if hd == 0 and p > 0:
                        pe.wait_ge(pt_act if bk < 2 else pt_dve, 4 * p)
                    if bk < 2:
                        blocks = [(0, 1), (2 * P, 2)] if bk == 0 else [(0, 3), (2 * P, 0)]
                        for col, b in blocks:
                            lo = max(b - 1, 0) * P
                            keys = slice(lo, (b + 1) * P)
                            last = pe.matmul(side[bk][:, col:col + (b + 1) * P - lo], qk[:, 0, 0, hd, b * P:(b + 1) * P],
                                             qk[:, 0, 1, hd, keys], start=True, stop=True, skip_group_check=True)
                    else:
                        for r in range(DIL):
                            tok = slice(r, SEQ, DIL)
                            last = pe.matmul(side[bk][:, r * P:(r + 1) * P], qk[:, bk - 1, 0, hd, tok],
                                             qk[:, bk - 1, 1, hd, tok], start=True, stop=True, skip_group_check=True)
                    last.then_inc(sc_done, 1)

            def transposes(hh):
                hd = hh % 2
                for bk in range(4):
                    pe.wait_ge(exp_done, 4 * hh + bk + 1)
                    if hd == 1:
                        pe.wait_ge(pt_act if bk < 2 else pt_dve, 2 * hh - (1 - bk % 2))
                    for col in range(0, BANK_W[bk], P):
                        last = pe.transpose(side[bk][:, col:col + P], S[:, hd, BANK_AT[bk] + col:BANK_AT[bk] + col + P], ident)
                    last.then_inc(tr_ps, 1)

            def values(hh):
                pe.wait_ge(pt_act, 2 * hh + 2)
                pe.wait_ge(pt_dve, 2 * hh + 2)
                if hh >= 1:
                    pe.wait_ge(osum_done, hh)
                if hh == 0:
                    evacuated(pe, (("v", GROUPS - 1, 0), 0))
                    evacuated(pe, (("v", GROUPS - 1, 0), 1))
                at = {1: 0, 2: 2 * P, 3: 4 * P}
                for b in range(NB):
                    dst = side[4][:, b * P:(b + 1) * P]
                    if b == 0:
                        pe.matmul(dst, v_ext[:, 0, 0, hh, :], PT[:, 6 * P:7 * P], start=True, stop=True, skip_group_check=True)
                    else:
                        for j in range(2):
                            pe.matmul(dst, v_ext[:, b - 1 + j, 0, hh, :], PT[:, at[b] + j * P:at[b] + (j + 1) * P],
                                      start=(j == 0), stop=(j == 1), skip_group_check=True)
                for r in range(DIL):
                    for g in (1, 2):
                        col = BANK_AT[g + 1] + r * P
                        last = pe.matmul(side[5][:, r * P:(r + 1) * P], v_ext[:, r, g, hh, :], PT[:, col:col + P],
                                         start=(g == 1), stop=(g == 2), skip_group_check=True)
                last.then_inc(pv_done, 1)

            def attention(p, i):
                if i in (0, 1):
                    scores(2 * p + i)
                if i == 2:
                    pe.wait_ge(mx_done, 2 * p + 2)
                    for b in range(NB):
                        pe.transpose(side[0][0:2, b * P:(b + 1) * P], mx[:, b, :], ident)
                    for r in range(DIL):
                        last = pe.transpose(side[1][0:2, r::DIL], mx[:, NB + r, :], ident)
                    last.then_inc(mxr_ps, 1)
                if i == 3:
                    pe.wait_ge(rowmax_done, 2 * p + 2)
                    for b in range(NB):
                        pe.transpose(side[0][:, 2 * b:2 * b + 2], rowm[:, 1, b * P:(b + 1) * P], ident[0:2, 0:2])
                    for r in range(DIL):
                        c0 = 2 * (NB + r)
                        last = pe.transpose(side[0][:, c0:c0 + 2], rowm[:, 1, r::DIL], ident[0:2, 0:2])
                    last.then_inc(mxc_ps, 1)
                if i == 4:
                    transposes(2 * p)
                if i == 5:
                    values(2 * p)
                    transposes(2 * p + 1)
                if i == 6:
                    values(2 * p + 1)

            def gate_tiles():
                pe.wait_ge(w2_in, 32)
                evacuated(pe, (("lr", 0, 0), 0))
                for b in range(NB):
                    dst = take(TILE[("z", b)])
                    pe.matmul(dst[:, :], lrT[0:LOWRANK + 1, b * P:(b + 1) * P], w2b[:, :],
                              start=True, stop=True).then_inc(acc_ready, 1)

            def within(h, b):
                u = NB * h + b
                pe.wait_ge(kk_done, u + 1)
                if u >= 1:
                    pe.wait_ge(at_done, u)
                    pe.wait_ge(kt_done, u)
                for n in range(NCH):
                    at = CHUNK * n
                    pe.matmul(side[2][:, at:at + CHUNK], kk[:, n, :], q_in[:, h % 2, b * P + at:b * P + at + CHUNK],
                              start=True, stop=True, skip_group_check=True)
                pe.transpose(side[3][:, 0:P], ke[:, :], ident).then_inc(at_ps, 1)

            def outputs(h, b):
                u = NB * h + b
                pe.wait_ge(at_done, u + 1)
                pe.wait_ge(kt_done, u + 1)
                if b == 0:
                    if h == 0:
                        pe.wait_ge(osum_done, 4)
                    else:
                        pe.wait_ge(o_done, 2 * h)
                    evacuated(pe, (("gv", h, 0), 0))
                    evacuated(pe, (("gv", h, 0), 1))
                else:
                    pe.wait_ge(st_done, 3 * h + b)
                    pe.wait_ge(qB_done, h + 1)
                for v in range(2):
                    dst = side[4 + v][:, b * P:(b + 1) * P]
                    last = pe.matmul(dst, gv[:, h % 2, b, v * P:(v + 1) * P], at_sb[:, u % 2, :],
                                     start=True, stop=(b == 0), skip_group_check=True)
                    if b > 0:
                        last = pe.matmul(dst, state[:, v * P:(v + 1) * P], qB[:, b * P:(b + 1) * P],
                                         start=False, stop=True, skip_group_check=True)
                if b < NB - 1:
                    last = pe.matmul(side[1][:, 64:64 + DV], kt_sb[:, u % 2, :], gv[:, h % 2, b, :],
                                     start=True, stop=True, skip_group_check=True)
                last.then_inc(p3_done, 1)

            def gla(h, i):
                if i == 0:
                    pe.wait_ge(logs_done, 2 * NB)
                    if h >= 1:
                        pe.wait_ge(gexp_done, 3 * h)
                        pe.wait_ge(st_done, 3 * h)
                    if h >= 2:
                        pe.wait_ge(groot_done, h - 1)
                    for b in range(NB):
                        g = logs[:, b, h * P:(h + 1) * P]
                        pe.matmul(side[0][:, b * P:(b + 1) * P], g, cst[:, C_TRI:C_TRI + P],
                                  start=True, stop=True, skip_group_check=True)
                        c0 = b * (NCH + 1)
                        last = pe.matmul(side[1][:, c0:c0 + NCH + 1], g, cst[:, C_TRI + P:C_TRI + P + NCH + 1],
                                         start=True, stop=True, skip_group_check=True)
                    last.then_inc(b_ps, 1)
                if 2 <= i <= 5:
                    within(h, i - 2)
                if 3 <= i <= 6:
                    outputs(h, i - 3)
                if i == 8:
                    pe.wait_ge(osum2_done, h + 1)
                    pe.wait_ge(gexp_done, 3 * min(h + 2, HEADS))
                    pe.matmul(side[0][:, :], ones[:, :], osq[:, 0, :], start=True, stop=True,
                              skip_group_check=True).then_inc(gssq_ps, 1)

            for n in range(GROUPS):
                for t in range(2):
                    product(n, t)
            for p in range(2):
                for g in range(GROUPS):
                    for t in range(2):
                        product(UNIT[("qk", p, g)], t)
                        if p == 1:
                            attention(0, 2 * g + t)
                    if (p, g) == (1, 1):
                        ada_tile(0)
            product(UNIT[("lr", 0, 0)], 0)
            attention(0, 6)
            for h in range(HEADS):
                for u, kind in enumerate(("gqk", "gv", "gr")):
                    for t in range(2):
                        i = 2 * u + t
                        product(UNIT[(kind, h, 0)], t)
                        if h == 0:
                            attention(1, i)
                        if h == 1 and i == 0:
                            attention(1, 6)
                        if h >= 2 and i in (0, 2, 3):
                            gla(h - 2, 6 + i)
                        if h >= 1:
                            gla(h - 1, i)
                    if kind == "gqk" and h == 0:
                        gate_tiles()
                    if (kind, h) == ("gv", 2):
                        ada_tile(1)
            for u in range(4):
                for t in range(2):
                    i = 2 * u + t
                    product(UNIT[("ma", u, 0)], t)
                    if i in (0, 2, 3):
                        gla(2, 6 + i)
                    gla(3, i)
            for u in range(4):
                for t in range(2):
                    product(UNIT[("mb", u, 0)], t)
                    if u == 0:
                        gla(3, 8 + t)
            for m in range(KT):
                product(UNIT[("wa", 0, 0)], m)
            for kind in ("wg", "wo"):
                for u in range(4):
                    for t in range(2):
                        product(UNIT[(kind, u, 0)], t)
            pe.wait_ge(sum_done, 2 * KT)
            pe.matmul(side[0][:, :], ones[:, :], sq_sum2[:, :], start=True, stop=True).then_inc(ssq_ps, 1)

            def up(a, s, first=False):
                i = 2 * a + s
                slot = 1 - s
                for t in range(2):
                    if first and s == 0:
                        last_in_bank = N_TILES - 1 - (N_TILES - 1 - t) % 2
                        pe.wait_ge(acc_free[t], last_in_bank // 2 + 1)
                    if not first:
                        pe.wait_ge(tap_done, 4 * i + (2 * t - 6))
                    if t == 0:
                        pe.wait_ge(raw_used, i + (N_RAW + 1))
                    for k in range(KT):
                        if first and s == 0 and t == 0:
                            pe.wait_ge(hl_done, KT + k + 1)
                        at = k * UW + t * P
                        w = tuple(v[:, slot, at:at + P] for v in (w_hi, w_lo))
                        last = three(bank[2 * s + t][:, :], w, (h_hi[:, k, :], h_lo[:, k, :]), k == 0, k == KT - 1)
                    last.then_inc(ffn_ready, 1)

            for s in range(2):
                up(0, s, first=True)
            with pe.Fori(1, FT // 2) as a:
                for s in range(2):
                    up(a, s)

            def down(a, s, first=False, final=False):
                j = 2 * a + s
                slot = 1 - s
                pe.wait_ge(raw_used, j + (N_RAW + FT + 1))
                pe.wait_ge(hs_lo_done, j + 1)
                for m in range(KT):
                    if first and m < 4:
                        pe.wait_ge(tap_done, 4 * FT - 6 + 2 * m)
                    for k in range(2):
                        at = k * D + m * P
                        w = tuple(v[:, slot, at:at + P] for v in (w_hi, w_lo))
                        last = three(bank[m][:, :], w, (hs_hi[:, s, k, :], hs_lo[:, s, k, :]),
                                     first and k == 0, final and k == 1)
                    if final:
                        last.then_inc(down_tile, 1)
                if not final:
                    last.then_inc(down_done, 1)

            down(0, 0, first=True)
            down(0, 1)
            with pe.Fori(1, DOWN_UNITS // 2) as a:
                for s in range(2):
                    down(a, s)
            down(DOWN_UNITS // 2, 0, final=True)
            pe.wait_ge(sum_done, 3 * KT)
            pe.matmul(bank[0][:, :], ones[:, :], sq_sum2[:, :], start=True, stop=True).then_inc(ssq_ps, 1)
            pe.wait_ge(root_done, 3)
            for i in range(8):
                half, b = divmod(i, NB)
                for m in range(4):
                    if b == 0:
                        pe.wait_ge(y_done, 4 * half + m + 1)
                    last = pe.transpose(bank[yt_bank(i)][:, m * P:(m + 1) * P], x1[:, 4 * half + m, b * P:(b + 1) * P], ident)
                last.then_inc(yt_ps, 1)


_INS = ["x", "c", "positions", "ada_w", "ada_b", "norm1_w", "w_in", "gla_gate_w2", "gla_gate_b", "gla_norm_w",
        "w_gla_branch", "w_attn_branch", "w_out", "norm2_w", "w_up", "conv_w", "conv_b", "w_down", "final_norm_w"]


def kernel(**inputs):
    import concourse.bacc as _bacc
    from concourse.bass_utils import run_bass_kernel_spmd as _run

    nc = _bacc.Bacc("TRN2", target_bir_lowering=False, num_devices=1)
    arrays, args = {}, []
    for name in _INS + ["shape_constants"]:
        a = np.ascontiguousarray(inputs[name]) if name in inputs else shape_constants()
        arrays[f"in_{name}_dram"] = a
        args.append(nc.dram_tensor(f"in_{name}_dram", a.shape, mybir.dt.from_np(a.dtype), kind="ExternalInput").ap())
    args.append(nc.dram_tensor("out_0_dram", (1, SEQ, D), F32, kind="ExternalOutput").ap())
    hybrid_block_kernel(nc, *args)
    r = _run(nc, [arrays], core_ids=[0])
    return r.results[0]["out_0_dram"]
```

```python
from contextlib import ExitStack

import numpy as np

import concourse.bass as bass
from concourse import mybir

F32 = mybir.dt.float32
F32R = mybir.dt.float32r
I32 = mybir.dt.int32
U32 = mybir.dt.uint32
ACT = mybir.ActivationFunctionType
ALU = mybir.AluOpType
AX = mybir.AxisListType

P = 128
SEQ = 512
D = 1024
KT = D // P
NB = SEQ // P
HEADS = 4
DV = 256
LOWRANK = 16
CHUNK = 16
NCH = P // CHUNK
DH = 64
GROUPS = 3
DIL = 4
D_FF = 2816
FT = D_FF // P
EPS = 1e-6
NEG = -3.0e38
ROUND = 1.5 * 2.0 ** 23
TWO_PI = (6.28125, 0.0019350051879882812, 3.0199159795074593e-07)

GLA_QK = HEADS * P
COL_GQ = 0
COL_GK = COL_GQ + GLA_QK
COL_GV = COL_GK + GLA_QK
COL_GR = COL_GV + HEADS * DV
COL_LR = COL_GR + HEADS * DV
COL_AQ = COL_LR + LOWRANK
COL_AK = COL_AQ + GROUPS * HEADS * DH
COL_AV = COL_AK + GROUPS * HEADS * DH
COL_MA = COL_AV + GROUPS * HEADS * DH
COL_MB = COL_MA + D
UW = 256
UE = KT * UW

C_ID = 0
C_TRI = C_ID + P
C_KEEP = C_TRI + P + NCH + 1
C_MSK = C_KEEP + P
C_MOD = C_MSK + 3 * P
C_FRQ = C_MOD + P
C_ALL = C_FRQ + 1

V_C, V_N1, V_N2, V_FN, V_GN, V_AB = 0, 8, 16, 24, 32, 34
ROWS_A = V_AB + 6 * KT
ROWS_B = 4 * FT
V_CW0 = ROWS_A
V_CW1 = V_CW0 + 2 * FT
V_CW2 = V_CW1 + 2 * FT
V_CB = V_CW2 + 2 * FT
V_ALL = V_CB + 2 * FT
LN_EXP = "natural_log_exp_and_others"


def shape_constants():
    c = np.zeros((P, C_ALL), np.float32)
    row, col = np.arange(P)[:, None], np.arange(P)[None, :]
    c[:, C_ID:C_ID + P] = row == col
    same = row // CHUNK == col // CHUNK
    c[:, C_TRI:C_TRI + P] = np.where(same & (row <= col), -1.0 / 16.0, 0.0)
    for n in range(NCH + 1):
        c[:, C_TRI + P + n] = np.where(row[:, 0] < CHUNK * n, -1.0 / 16.0, 0.0)
    c[:, C_KEEP:C_KEEP + P] = col >= row
    c[:, C_MSK:C_MSK + P] = np.where(col >= row, 0.0, NEG)
    c[:, C_MSK + P:C_MSK + 2 * P] = np.where(col <= row, 0.0, NEG)
    c[:, C_MSK + 2 * P:C_MSK + 3 * P] = np.where(col <= row, 0.0, NEG)
    c[:, C_MOD:C_MOD + P] = np.where((col <= row) & ((row - col) % 4 == 0), 0.0, NEG)
    half = DH // 2
    freq = np.float32(10000.0) ** (-np.arange(half, dtype=np.float32) / np.float32(half))
    c[:, C_FRQ] = np.tile(freq.astype(np.float32), P // half)
    return c


UNITS = ([("v", g, 0) for g in range(GROUPS)]
         + [("qk", p, g) for p in range(2) for g in range(GROUPS)]
         + [("lr", 0, 0)]
         + [(kind, h, 0) for h in range(HEADS) for kind in ("gqk", "gv", "gr")]
         + [("ma", u, 0) for u in range(4)]
         + [("mb", u, 0) for u in range(4)]
         + [("wa", 0, 0)]
         + [("wg", u, 0) for u in range(4)]
         + [("wo", u, 0) for u in range(4)])
N_UNITS = len(UNITS)
UNIT = {u: n for n, u in enumerate(UNITS)}


def tiles_of(unit):
    return {"lr": 1, "wa": 8}.get(unit[0], 2)


TILES = []
for _u in UNITS:
    TILES += [(_u, t) for t in range(tiles_of(_u))]
    if _u == ("gqk", 0, 0):
        TILES += [("z", b) for b in range(NB)]
    if _u == ("qk", 1, 1):
        TILES += [("ada", 0)]
    if _u == ("gv", 2, 0):
        TILES += [("ada", 1)]
TILE = {t: n for n, t in enumerate(TILES)}
N_TILES = len(TILES)

RAW = []
for _n in range(N_UNITS):
    RAW.append(("w", _n))
    if _n < 16:
        RAW.append(("ada", _n))
RAW_AT = {r: q for q, r in enumerate(RAW)}
N_RAW = len(RAW)


def dmas_of(raw):
    return 2 if raw[0] == "w" and UNITS[raw[1]][0] in ("qk", "gqk") else 1


LANDED = []
_count = [0, 0]
for _q, _r in enumerate(RAW):
    _count[_q % 2] += 16 * dmas_of(_r)
    LANDED.append(_count[_q % 2])
LANDED_END = tuple(_count)
FIRST_FFN = N_RAW
DOWN_UNITS = FT // 2
SUMS = (0, 0, KT - 2)


def hybrid_block_kernel(nc, x, c, positions, ada_w, ada_b, norm1_w, w_in, gate_w2, gate_b, gla_norm_w,
                        w_gla, w_attn, w_out, norm2_w, w_up, conv_w, conv_b, w_down, final_w, consts, out):
    assert N_UNITS % 2 == 1 and N_RAW % 2 == 1
    ctx = ExitStack()
    with ctx:
        def sb(name, shape, dt=F32):
            return ctx.enter_context(nc.sbuf_tensor(name, shape, dt))

        def sem(name):
            return ctx.enter_context(nc.semaphore(name))

        x_spill = nc.dram_tensor("x_spill", [P, KT * SEQ], F32, kind="Internal").ap()

        raw = sb("raw", [P, 2, UE])
        w_hi = sb("w_hi", [P, 2, UE], F32R)
        w_lo = sb("w_lo", [P, 2, UE], F32R)
        h_hi = sb("h_hi", [P, KT, SEQ], F32R)
        h_lo = sb("h_lo", [P, KT, SEQ], F32R)
        cst = sb("cst", [P, C_ALL])
        ones = sb("ones", [P, P])
        vecs = sb("vecs", [P, V_ALL])
        rows_a = sb("rows_a", [ROWS_A, P])
        rows_b = sb("rows_b", [ROWS_B, 2, P])
        c_silu = sb("c_silu", [P, KT])
        mod = sb("mod", [P, 6 * KT])
        gain = sb("gain", [P, 2, KT])
        ada_acc = sb("ada_acc", [P, 2 * D])

        def region(*places):
            got = []
            with ExitStack() as scope:
                at = 0
                for n, (name, kb, shape, dt) in enumerate(sorted(places, key=lambda p: p[1])):
                    off = int(kb * 1024)
                    assert off >= at, name
                    if off > at:
                        scope.enter_context(nc.sbuf_tensor(f"gap_{name}", [P, (off - at) // 4], F32))
                    got.append(scope.enter_context(nc.sbuf_tensor(name, shape, dt)))
                    size = 4
                    for s in shape[1:]:
                        size *= s
                    at = off + (size + 31) // 32 * 32
            order = sorted(range(len(places)), key=lambda i: places[i][1])
            back = [None] * len(places)
            for i, t in zip(order, got):
                back[i] = t
            return back

        ada_in, x_tok, xT0, sq, rstd, ntmp, ada_in7, cs = region(
            ("ada_in", 0, [P, 7, KT, 2, P], F32), ("x_tok", 56, [P, NB, D], F32), ("xT0", 72, [P, KT, SEQ], F32),
            ("sq", 88, [P, 2, SEQ], F32), ("rstd", 94, [P, SEQ], F32),
            ("ntmp", 96, [P, 2, SEQ], F32), ("ada_in7", 100, [P, KT, 2, P], F32), ("cs", 108, [P, 2, SEQ], F32))
        xn = x_tok[:, :, :].rearrange("p b (t n) -> p (b t) n", n=SEQ)
        qk, rope, oa_hi, oa_lo, ocomb, osum, orec, oa32, rope_t, v_ext, S, PT, mx, mg, rowm, negm = region(
            ("qk", 0, [DH, GROUPS, 2, 2, SEQ], F32), ("rope", 24, [P, 2, 2, SEQ], F32),
            ("oa_hi", 32, [P, 2, SEQ], F32R), ("oa_lo", 36, [P, 2, SEQ], F32R),
            ("ocomb", 40, [P, SEQ], F32), ("osum", 42, [P, SEQ], F32), ("orec", 44, [P, SEQ], F32),
            ("oa32", 46, [P, SEQ], F32), ("rope_t", 48, [P, 2, SEQ], F32),
            ("v_ext", 56, [P, NB, GROUPS, HEADS, P], F32), ("S", 80, [P, 2, 1920], F32),
            ("PT", 95, [P, 1920], F32), ("mx", 102.5, [P, 8, 2], F32), ("mg", 102.75, [P, 2, 4], F32),
            ("rowm", 103, [2, 2, SEQ], F32), ("negm", 107, [P, 8, 2], F32))
        q_in, k_in, gv, gr, logs, za, lrT, w2b, og_hi, og_lo, kk, at_sb, kt_sb, ke, state, eb, enb, ed, qB, o_sb, osq, ors = region(
            ("q_in", 0, [P, 2, SEQ], F32), ("k_in", 4, [P, 2, SEQ], F32), ("gv_sb", 8, [P, 2, NB, DV], F32),
            ("gr_sb", 16, [P, 2, 2, SEQ], F32), ("logs", 24, [P, NB, SEQ], F32),
            ("za", 48, [P, 2, SEQ], F32), ("lrT", 52, [32, SEQ], F32), ("w2b", 54, [LOWRANK + 1, SEQ], F32),
            ("og_hi", 56, [P, KT, SEQ], F32R), ("og_lo", 72, [P, KT, SEQ], F32R),
            ("kk", 88, [P, NCH, P], F32), ("at_sb", 92, [P, 2, P], F32), ("kt_sb", 93, [P, 2, P], F32),
            ("ke", 94, [P, P], F32), ("state", 94.5, [P, DV], F32), ("eb", 95.5, [P, SEQ], F32),
            ("enb", 97.5, [P, SEQ], F32), ("ed", 99.5, [P, NB, NCH + 1], F32), ("qB", 99.75, [P, SEQ], F32),
            ("o_sb", 101.75, [P, 2, SEQ], F32), ("osq", 105.75, [P, 2, SEQ], F32), ("ors", 109.75, [P, SEQ], F32))
        mix_hi, mix_lo, sA, sB, mtmp = region(
            ("mix_hi", 0, [P, KT, SEQ], F32R), ("mix_lo", 16, [P, KT, SEQ], F32R),
            ("sA", 40, [P, KT, SEQ], F32), ("sB", 88, [P, KT, SEQ], F32), ("mtmp", 104, [P, 2, SEQ], F32))
        hid, x1, conv, sq2, sq_sum2, rstd2, ntmp2, hs_hi, hs_lo = region(
            ("hid", 0, [P, FT, SEQ], F32), ("x1", 56, [P, KT, SEQ], F32), ("conv", 72, [P, 2, 2, SEQ], F32),
            ("sq2", 80, [P, 2, SEQ], F32), ("sq_sum2", 84, [P, SEQ], F32), ("rstd2", 86, [P, SEQ], F32),
            ("ntmp2", 88, [P, 2, SEQ], F32),
            ("hs_hi", 92, [P, 2, 2, SEQ], F32R), ("hs_lo", 100, [P, 2, 2, SEQ], F32R))
        y_tok, = region(("y_tok", 0, [P, NB, D], F32))
        rstd_tok = rstd2[:, 0:NB]
        ntmp1 = conv[:, 0, :, :]
        angles = ada_in[:, 1].rearrange("p k s n -> p (k s n)")
        pos_i = angles[:, 0:SEQ].bitcast(I32)
        ang, turns, ang_abs = (angles[:, i * SEQ:(i + 1) * SEQ] for i in range(1, 4))

        bank = [ctx.enter_context(nc.psum_tensor(f"bank{i}", [P, SEQ], F32)) for i in range(8)]
        side = bank[2:]

        landed = [sem(f"raw_landed{i}") for i in range(2)]
        raw_used = sem("raw_used")
        hi_done = sem("hi_done")
        acc_ready = sem("acc_ready")
        acc_free = [sem(f"acc_free{i}") for i in range(2)]
        rows_in, conv_in, cst_in, x_in, pos_in = (sem(n) for n in ("rows_in", "conv_in", "cst_in", "x_in", "pos_in"))
        ada_landed = [sem(f"ada_landed{i}") for i in range(2 * KT)]
        w2_in = sem("w2_in")
        ones_set = sem("ones_set")
        vec_ps, vec_sb, silu_done = sem("vec_ps"), sem("vec_sb"), sem("silu_done")
        xt_ps, xt_sb, spilled, x_back = sem("xt_ps"), sem("xt_sb"), sem("spilled"), sem("x_back")
        ada_step, ada_sum = sem("ada_step"), sem("ada_sum")
        mod1_ps, mod_done, gain_done = sem("mod1_ps"), sem("mod_done"), sem("gain_done")
        sq_done, sum_done, ssq_ps, ln_done, rstd_done = (sem(n) for n in (
            "sq_done", "sum_done", "ssq_ps", "ln_done", "rstd_done"))
        xn_done, nt_done, hh_done, hl_done = (sem(n) for n in ("xn_done", "nt_done", "hh_done", "hl_done"))
        rot_dve, rot_sum, rot_act = sem("rot_dve"), sem("rot_sum"), sem("rot_act")
        v_ones = sem("v_ones")
        rope_sum, qk_in = sem("rope_sum"), [sem(f"qk_in{i}") for i in range(2)]
        sc_done, msk_done, mx1_done, mx_done = sem("sc_done"), sem("msk_done"), sem("mx1_done"), sem("mx_done")
        mxr_ps, rowmax_done, mxc_ps, negm_done = (sem(n) for n in ("mxr_ps", "rowmax_done", "mxc_ps", "negm_done"))
        exp_done, tr_ps, pt_act, pt_dve, pv_done = (sem(n) for n in ("exp_done", "tr_ps", "pt_act", "pt_dve", "pv_done"))
        perm_sb, osum_done, oln_done, orec_done, oa32_done, oahi_done, oalo_done = (sem(n) for n in (
            "perm_sb", "osum_done", "oln_done", "orec_done", "oa32_done", "oahi_done", "oalo_done"))
        lr_ones, z_abs, z_exp, z_ln, logs_done = (sem(n) for n in (
            "lr_ones", "z_abs", "z_exp", "z_ln", "logs_done"))
        b_ps, gexp_done, qg_done, qB_done, kk_step, kk_done = (sem(n) for n in (
            "b_ps", "gexp_done", "qg_done", "qB_done", "kk_step", "kk_done"))
        at_zero, at_ps, at_done, kt_done, p3_done, st_done = (sem(n) for n in (
            "at_zero", "at_ps", "at_done", "kt_done", "p3_done", "st_done"))
        o_done, osq_done, osum2_done, gssq_ps, gln_done, grstd_done, on_done, og32_done, oghi_done, oglo_done = (
            sem(n) for n in ("o_done", "osq_done", "osqsum_done", "gssq_ps", "gln_done", "grstd_done", "on_done",
                             "og32_done", "oghi_done", "oglo_done"))
        mix32_done, mixhi_done, mixlo_done = sem("mix32_done"), sem("mixhi_done"), sem("mixlo_done")
        ffn_ready, tap2_done, tap_done, gelu_done, hid_done = (sem(n) for n in (
            "ffn_ready", "tap2_done", "tap_done", "gelu_done", "hid_done"))
        sq_used = sem("sq_used")
        hs_hi_done, hs_lo_done, down_done, down_tile = (sem(n) for n in (
            "hs_hi_done", "hs_lo_done", "down_done", "down_tile"))
        x2_done, xw_done, yt_ps, yt_act, yt_dve, stored = (sem(n) for n in (
            "x2_done", "xw_done", "yt_ps", "yt_act", "yt_dve", "stored"))

        block = ctx.enter_context(nc.Block())

        def ada_first(j):
            return ada_in[:, j] if j < 7 else ada_in7

        def last_tile(n):
            return TILE[(UNITS[n], tiles_of(UNITS[n]) - 1)]

        def views(n):
            rs, ws = RAW_AT[("w", n)] % 2, n % 2
            kind = UNITS[n][0]
            if kind == "qk":
                r = raw[:, rs, :].rearrange("p (k a t f) -> p t k a f", k=KT, a=4, t=2)
                hv = w_hi[:, ws, :].rearrange("p (k t a f) -> p t k a f", k=KT, t=2, a=4)
                lv = w_lo[:, ws, :].rearrange("p (k t a f) -> p t k a f", k=KT, t=2, a=4)
                return [(r[:, t], hv[:, t], lv[:, t]) for t in range(2)]
            size = KT * LOWRANK if kind == "lr" else UE
            return [(raw[:, rs, 0:size], w_hi[:, ws, 0:size], w_lo[:, ws, 0:size])]

        def evacuated(eng, tile):
            i = TILE[tile]
            eng.wait_ge(acc_free[i % 2], i // 2 + 1)

        BANK_AT = [0, 512, 896, 1408]
        BANK_W = [512, 384, 512, 512]

        def score_blocks(bk):
            if bk == 0:
                return [(0, 2 * P, 1), (2 * P, 2 * P, 2)]
            if bk == 1:
                return [(0, 2 * P, 3), (2 * P, P, 0)]
            return [(r * P, P, NB + r) for r in range(DIL)]

        @block.sync
        def _(sp):
            sp.dma_start(rows_a[V_C:V_C + KT, :], c.rearrange("a (k p) -> (a k) p", p=P)).then_inc(rows_in, 16)
            sp.dma_start(rows_a[V_N1:V_N1 + KT, :], norm1_w.rearrange("a (k p) -> (a k) p", p=P)).then_inc(rows_in, 16)
            sp.dma_start(rows_a[V_AB:ROWS_A, :], ada_b.rearrange("a (k p) -> (a k) p", p=P)).then_inc(rows_in, 16)
            sp.dma_start(rows_a[V_N2:V_N2 + KT, :], norm2_w.rearrange("a (k p) -> (a k) p", p=P)).then_inc(rows_in, 16)
            sp.dma_start(rows_a[V_FN:V_FN + KT, :], final_w.rearrange("(k p) -> k p", p=P)).then_inc(rows_in, 16)
            sp.dma_start(rows_a[V_GN:V_GN + 2, :], gla_norm_w.rearrange("a (k p) -> (a k) p", p=P)).then_inc(rows_in, 16)
            ada_v = ada_w.rearrange("a (k p) n -> (a k) p n", p=P)
            ada_t = ada_w.rearrange("a (k p) (s n) -> p (a k) s n", p=P, n=D)

            def load_first(j):
                for half in range(2):
                    rows = slice(half * KT // 2, (half + 1) * KT // 2)
                    for s_ in range(2):
                        sp.dma_start(ada_first(j)[:, rows, s_, :],
                                     ada_t[:, rows, s_, j * P:(j + 1) * P]).then_inc(ada_landed[2 * j + half], 16)

            w_in_v = w_in.rearrange("a (k p) n -> p (a k) n", p=P)

            def cols(view, at, width=UW):
                return view[:, :, at:at + width]

            wg_v = w_gla.rearrange("a (k p) n -> p (a k) n", p=P)
            wo_v = w_out.rearrange("a (k p) n -> p (a k) n", p=P)
            wa_v = w_attn.rearrange("a (k p) n -> p (a k) n", p=P)

            def load(q):
                what, n = RAW[q]
                slot = q % 2
                done = landed[slot]
                if q >= 2:
                    sp.wait_ge(raw_used, q - 1)
                if what == "ada":
                    r, k = n // KT, n % KT
                    sp.dma_start(raw[:, slot, :], ada_v[k, :, 2 * D * (r + 1):2 * D * (r + 2)]).then_inc(done, 16)
                    return
                kind, a, b = UNITS[n]
                dst = raw[:, slot, :].rearrange("p (k n) -> p k n", k=KT)
                if kind == "qk":
                    off = b * HEADS * DH + a * 2 * DH
                    sp.dma_start(dst[:, :, 0:P], cols(w_in_v, COL_AQ + off, P)).then_inc(done, 16)
                    sp.dma_start(dst[:, :, P:UW], cols(w_in_v, COL_AK + off, P)).then_inc(done, 16)
                elif kind == "gqk":
                    sp.dma_start(dst[:, :, 0:P], cols(w_in_v, COL_GQ + a * P, P)).then_inc(done, 16)
                    sp.dma_start(dst[:, :, P:UW], cols(w_in_v, COL_GK + a * P, P)).then_inc(done, 16)
                elif kind == "lr":
                    small = raw[:, slot, 0:KT * LOWRANK].rearrange("p (k n) -> p k n", k=KT)
                    sp.dma_start(small, cols(w_in_v, COL_LR, LOWRANK)).then_inc(done, 16)
                elif kind == "wa":
                    sp.dma_start(raw[:, slot, :].rearrange("p (k n) -> p k n", k=2), wa_v).then_inc(done, 16)
                else:
                    src = {"v": cols(w_in_v, COL_AV + a * UW), "gv": cols(w_in_v, COL_GV + a * DV),
                           "gr": cols(w_in_v, COL_GR + a * DV), "ma": cols(w_in_v, COL_MA + a * UW),
                           "mb": cols(w_in_v, COL_MB + a * UW),
                           "wg": wg_v[:, :, (a % 4) * UW:(a % 4 + 1) * UW],
                           "wo": wo_v[:, :, (a % 4) * UW:(a % 4 + 1) * UW]}[kind]
                    sp.dma_start(dst, src).then_inc(done, 16)

            def shuffle(j):
                p, g = divmod(j, GROUPS)
                sp.wait_ge(rope_sum, 2 * j + 2)
                if j == GROUPS:
                    sp.wait_ge(sc_done, 8)
                for half in range(2):
                    for a in range(4):
                        sp.dma_start(qk[32 * half:32 * half + 32, g, a // 2, a % 2, :],
                                     rope[32 * a:32 * a + 32, j % 2, half, :]).then_inc(qk_in[j % 2], 16)

            for j in range(KT):
                if j == KT // 2:
                    load(0)
                load_first(j)
            sp.wait_ge(mod1_ps, 2)
            sp.dma_start(pos_i, positions.broadcast_to((P, SEQ))).then_inc(pos_in, 16)
            for q in range(N_RAW):
                if q > 0:
                    load(q)
                if q == 1:
                    sp.dma_start(rows_b[:, 0, :], conv_w[0, 0:2, :].rearrange("i (k p) -> (i k) p", p=P)).then_inc(conv_in, 16)
                    sp.dma_start(rows_b[0:2 * FT, 1, :], conv_w[0, 2:3, :].rearrange("i (k p) -> (i k) p", p=P)).then_inc(conv_in, 16)
                    sp.dma_start(rows_b[2 * FT:ROWS_B, 1, :], conv_b.rearrange("i (k p) -> (i k) p", p=P)).then_inc(conv_in, 16)
                    sp.wait_ge(xt_sb, KT)
                    sp.dma_start(x_spill, xT0[:, :, :].rearrange("p k n -> p (k n)")).then_inc(spilled, 16)
                what, n = RAW[q]
                if what == "w" and 6 <= n < 12:
                    shuffle(n - 6)
                if q == 2:
                    sp.wait_ge(mod1_ps, KT)
                    sp.dma_start(w2b[0:LOWRANK, :], gate_w2.rearrange("a r n -> (a r) n")).then_inc(w2_in, 16)
                    sp.dma_start(w2b[LOWRANK:LOWRANK + 1, :], gate_b).then_inc(w2_in, 16)
                if what == "w" and n == UNIT[("wo", 0, 0)]:
                    sp.wait_ge(spilled, 16)
                if what == "w" and n == UNIT[("wo", 1, 0)]:
                    sp.wait_ge(acc_ready, last_tile(UNIT[("wg", 3, 0)]) + 1)
                    sp.dma_start(x1[:, :, :].rearrange("p k n -> p (k n)"), x_spill).then_inc(x_back, 16)

            up_v = w_up.rearrange("a (k p) n -> p (a k) n", p=P)

            def load_up(i, s):
                slot = (s + 1) % 2
                dst = raw[:, slot, :].rearrange("p (k t n) -> p k t n", k=KT, t=2)
                sp.wait_ge(raw_used, i + (FIRST_FFN - 1))
                for t in range(2):
                    sp.dma_start(dst[:, :, t, :], up_v[:, :, bass.ds(i * P + t * D_FF, P)]).then_inc(landed[slot], 16)

            with sp.Fori(0, FT // 2) as a:
                for s in range(2):
                    load_up(2 * a + s, s)

            down_v = w_down.rearrange("a (k p) n -> p (a k) n", p=P)

            def load_down(j, s):
                slot = (s + 1) % 2
                sp.wait_ge(raw_used, j + (FIRST_FFN + FT - 1))
                for t in range(2):
                    sp.dma_start(raw[:, slot, t * D:(t + 1) * D].rearrange("p (k n) -> p k n", k=1),
                                 down_v[:, bass.ds(2 * j + t, 1), :]).then_inc(landed[slot], 16)

            with sp.Fori(0, DOWN_UNITS // 2) as a:
                for s in range(2):
                    load_down(2 * a + s, s)
            load_down(DOWN_UNITS - 1, 0)

            out_v = out.rearrange("a (b p) n -> p (a b) n", p=P)
            for i in range(8):
                half, b = divmod(i, NB)
                sp.wait_ge(yt_act if i % 2 == 0 else yt_dve, i // 2 + 1)
                sp.dma_start(out_v[:, b, half * SEQ:(half + 1) * SEQ], y_tok[:, b, half * SEQ:(half + 1) * SEQ]).then_inc(stored, 16)
            sp.wait_ge(stored, 8 * 16)

        @block.gpsimd
        def _(pool):
            pool.memset(ones[:, :], 1.0).then_inc(ones_set, 1)

            def sum_squares(part, sq_t, sum_t, tiles):
                for k in range(tiles):
                    i = SUMS[part] + k
                    pool.wait_ge(sq_done, part * KT + k + 1)
                    if k == 0:
                        pool.wait_ge(ssq_ps, part)
                    if k > 0:
                        pool.wait_ge(sum_done, i)
                    if k == 0:
                        pool.tensor_copy(sum_t[:, :], sq_t[:, k % 2, :]).then_inc(sum_done, 1)
                    else:
                        pool.tensor_tensor(sum_t[:, :], sum_t[:, :], sq_t[:, k % 2, :], ALU.add).then_inc(sum_done, 1)

            pool.wait_ge(rstd_done, 1)
            pool.wait_ge(xt_sb, KT)
            for k in range(KT):
                pool.tensor_tensor(xn[:, k, :], xT0[:, k, :], rstd[:, :], ALU.mult).then_inc(xn_done, 1)
            pool.wait_ge(xt_ps, KT)
            pool.wait_ge(hl_done, KT)
            pool.wait_ge(spilled, 16)
            for hd in range(2):
                part = v_ext[:, :, :, hd::2, (1 - hd) * DH:(2 - hd) * DH]
                pool.memset(part.rearrange("p b g h n -> p (b g) h n"), 1.0).then_inc(v_ones, 1)
            for j in range(2 * GROUPS):
                for t in range(2):
                    evacuated(pool, (("qk", *divmod(j, GROUPS)), t))
                for half, op in ((0, ALU.subtract), (1, ALU.add)):
                    dst = rope[:, j % 2, half, :]
                    pool.tensor_tensor(dst, dst, rope_t[:, half, :], op).then_inc(rope_sum, 1)
            pool.memset(lrT[:, :], 1.0).then_inc(lr_ones, 1)
            for h in range(HEADS):
                pool.wait_ge(osq_done, h + 1)
                pool.tensor_tensor(osq[:, 0, :], osq[:, 0, :], osq[:, 1, :], ALU.add).then_inc(osum2_done, 1)
            for m in range(KT):
                evacuated(pool, (("wg", m // 2, 0), m % 2))
                pool.tensor_tensor(sB[:, m, :], sB[:, m, :], mtmp[:, m % 2, :], ALU.add).then_inc(mix32_done, 1)
            sum_squares(1, sq2, sq_sum2, KT - 2)
            sum_squares(2, sq2, sq_sum2, KT - 1)

        @block.scalar
        def _(act):
            act.dma_start(cst[:, :], consts).then_inc(cst_in, 16)
            x_v = x.rearrange("a (b p) n -> p (a b) n", p=P)
            for b in range(NB):
                act.dma_start(x_tok[:, b, :], x_v[:, b, :]).then_inc(x_in, 16)

            def split_hi(n):
                if n == N_UNITS:
                    return split_hi_ffn(0, 0, acc_ready, last_tile(n - 2) + 1)
                q = RAW_AT[("w", n)]
                act.wait_ge(landed[q % 2], LANDED[q])
                if n >= 2:
                    act.wait_ge(acc_ready, last_tile(n - 2) + 1)
                for r, hv, _ in views(n):
                    last = act.activation(hv, r, ACT.Copy)
                last.then_inc(hi_done, 1)

            def split_hi_ffn(pair, odd, used, value):
                slot = 1 - odd
                act.wait_ge(landed[slot], pair * 32 + (LANDED_END[slot] + 32))
                act.wait_ge(used, value)
                act.activation(w_hi[:, slot, :], raw[:, slot, :], ACT.Copy).then_inc(hi_done, 1)

            def square(part, k, sq_t, src):
                if k >= 2 and part == 0:
                    act.wait_ge(sq_used, k - 1)
                if k >= 2 and part > 0:
                    act.wait_ge(sum_done, SUMS[part] + k - 1)
                if k < 2 and part > 1:
                    act.wait_ge(ssq_ps, part)
                act.activation(sq_t[:, k % 2, :], src[:, k, :], ACT.Square).then_inc(sq_done, 1)

            def inverse_root(part, dst, src):
                act.wait_ge(ssq_ps, part + 1)
                act.activation(dst, src, ACT.Ln, scale=1.0 / D, bias=EPS).then_inc(ln_done, 1)
                act.wait_ge(ln_done, part + 1)
                act.activation(dst, dst, ACT.Exp, scale=-0.5).then_inc(rstd_done, 1)

            def modulated(part, k, src, tmp, shift_col):
                i = part * KT + k
                act.wait_ge(gain_done, k + 1 if part == 0 else KT + 1)
                act.wait_ge(xn_done, i + 1)
                if k >= 2:
                    act.wait_ge(hl_done, i - 1)
                for dst, done in ((tmp[:, k % 2, :], nt_done), (h_hi[:, k, :], hh_done)):
                    act.activation(dst, src, ACT.Identity, scale=gain[:, part, k:k + 1],
                                   bias=mod[:, shift_col + k:shift_col + k + 1]).then_inc(done, 1)

            act.wait_ge(vec_sb, 1)
            act.activation(c_silu[:, :], vecs[:, V_C:V_C + KT], ACT.Silu).then_inc(silu_done, 1)
            act.preload_act_table_set(LN_EXP)
            for k in range(KT):
                act.wait_ge(xt_ps, k + 1)
                act.activation(xT0[:, k, :], bank[3 + k % 4][:, :], ACT.Copy).then_inc(xt_sb, 1)
                act.wait_ge(xt_sb, k + 1)
                square(0, k, sq, xT0)
            inverse_root(0, rstd[:, :], bank[0][:, :])
            split_hi(0)
            for k in range(KT):
                modulated(0, k, xn[:, k, :], ntmp, 0)

            def acc(tile):
                i = TILE[tile]
                act.wait_ge(acc_ready, i + 1)
                return bank[i % 2]

            def free(tile, ins):
                ins.then_inc(acc_free[TILE[tile] % 2], 1)

            def exps(hh):
                p, hd = divmod(hh, 2)
                act.wait_ge(negm_done, p + 1)
                for bk in range(4):
                    for col, width, i in score_blocks(bk):
                        at = BANK_AT[bk] + col
                        last = act.activation(S[:, hd, at:at + width], S[:, hd, at:at + width], ACT.Exp,
                                              bias=negm[:, i, hd:hd + 1], scale=DH ** -0.5)
                    last.then_inc(exp_done, 1)

            def attention(p, i):
                if i in (4, 5):
                    hh = 2 * p + i - 4
                    for bk in range(2):
                        act.wait_ge(tr_ps, 4 * hh + bk + 1)
                        if hh >= 1:
                            act.wait_ge(pv_done, hh)
                        at = BANK_AT[bk]
                        act.activation(PT[:, at:at + BANK_W[bk]], side[bk][:, 0:BANK_W[bk]],
                                       ACT.Copy).then_inc(pt_act, 1)
                if i in (3, 4):
                    exps(2 * p + i - 3)
                if i in (5, 6):
                    hh = 2 * p + i - 5
                    act.wait_ge(pv_done, hh + 1)
                    if hh >= 1:
                        act.wait_ge(orec_done, hh)
                    act.activation(ocomb[:, :].rearrange("p (l r) -> p r l", r=DIL),
                                   side[5][:, :].rearrange("p (r l) -> p r l", r=DIL),
                                   ACT.Copy).then_inc(perm_sb, 1)
                    num, den = (slice(0, DH), slice(DH, P)) if hh % 2 == 0 else (slice(DH, P), slice(0, DH))
                    act.wait_ge(osum_done, hh + 1)
                    if hh > 0:
                        act.wait_ge(oa32_done, hh)
                    act.activation(ocomb[den, :], osum[den, :], ACT.Ln).then_inc(oln_done, 1)
                    act.wait_ge(oln_done, hh + 1)
                    act.activation(orec[num, :], ocomb[den, :], ACT.Exp, scale=-1.0).then_inc(orec_done, 1)
                if i == 6:
                    act.wait_ge(oa32_done, 2 * p + 2)
                    act.activation(oa_hi[:, p, :], oa32[:, :], ACT.Copy).then_inc(oahi_done, 1)

            def gates():
                for b in range(NB):
                    z = acc(("z", b))
                    if b >= 2:
                        act.wait_ge(logs_done, 2 * (b - 1))
                    act.activation(za[:, b % 2, :], z[:, :], ACT.Abs).then_inc(z_abs, 1)
                    act.wait_ge(z_abs, b + 1)
                    act.activation(za[:, b % 2, :], za[:, b % 2, :], ACT.Exp, scale=-1.0).then_inc(z_exp, 1)
                    act.wait_ge(z_exp, b + 1)
                    act.activation(za[:, b % 2, :], za[:, b % 2, :], ACT.Ln, bias=1.0).then_inc(z_ln, 1)

            def gla(h, i):
                if i == 0:
                    act.wait_ge(b_ps, h + 1)
                    if h > 0:
                        act.wait_ge(kk_done, NB * h)
                        act.wait_ge(st_done, 3 * h)
                    act.activation(eb[:, :], side[0][:, :], ACT.Exp).then_inc(gexp_done, 1)
                    act.activation(enb[:, :], side[0][:, :], ACT.Exp, scale=-1.0).then_inc(gexp_done, 1)
                    act.activation(ed[:, :, :].rearrange("p b n -> p (b n)"), side[1][:, 0:NB * (NCH + 1)],
                                   ACT.Exp).then_inc(gexp_done, 1)
                if 2 <= i <= 5:
                    u = NB * h + i - 2
                    act.wait_ge(at_ps, u + 1)
                    if u >= 2:
                        act.wait_ge(p3_done, u - 1)
                    act.activation(kt_sb[:, u % 2, :], side[3][:, 0:P], ACT.Copy).then_inc(kt_done, 1)
                if i == 6:
                    act.wait_ge(o_done, 2 * h + 2)
                    if h > 0:
                        act.wait_ge(gssq_ps, h)
                    act.activation(osq[:, :, :], o_sb[:, :, :], ACT.Square).then_inc(osq_done, 1)
                if i == 8:
                    act.wait_ge(gssq_ps, h + 1)
                    if h > 0:
                        act.wait_ge(on_done, h)
                    act.activation(ors[:, :], side[0][:, :], ACT.Ln, scale=1.0 / DV, bias=EPS).then_inc(gln_done, 1)
                    act.wait_ge(gln_done, h + 1)
                    act.activation(ors[:, :], ors[:, :], ACT.Exp, scale=-0.5).then_inc(grstd_done, 1)
                if i == 9:
                    act.wait_ge(og32_done, 2 * h + 2)
                    act.activation(og_hi[:, 2 * h:2 * h + 2, :], o_sb[:, :, :], ACT.Copy).then_inc(oghi_done, 1)

            def evac(n, t):
                kind, a, _ = UNITS[n]
                tile = (UNITS[n], t)
                src = acc(tile)
                if kind == "v":
                    act.wait_ge(v_ones, 2)
                    v = src[:, :].rearrange("p (b h n) -> p b h n", b=2, h=HEADS)
                    for hd in range(2):
                        last = act.activation(v_ext[:, 2 * t:2 * t + 2, a, hd::2, hd * DH:(hd + 1) * DH],
                                              v[:, :, hd::2, :], ACT.Copy)
                    free(tile, last)
                if kind == "lr":
                    act.wait_ge(lr_ones, 1)
                    free(tile, act.activation(lrT[0:LOWRANK, :], src[0:LOWRANK, :], ACT.Copy))
                if kind == "gqk":
                    if a < 2:
                        act.wait_ge(sc_done, 16)
                    else:
                        act.wait_ge(p3_done, NB * (a - 1))
                    dst, scale = ((q_in, float(P) ** -0.5), (k_in, 1.0))[t]
                    free(tile, act.activation(dst[:, a % 2, :], src[:, :], ACT.Copy, scale=scale))
                if kind == "gv":
                    if a >= 2:
                        act.wait_ge(p3_done, NB * (a - 1))
                    free(tile, act.activation(gv[:, a % 2, 2 * t:2 * t + 2, :].rearrange("p b n -> p (b n)"),
                                              src[:, :], ACT.Copy))
                if kind == "gr":
                    if a >= 2:
                        act.wait_ge(og32_done, 2 * (a - 1))
                    free(tile, act.activation(gr[:, a % 2, t, :], src[:, :], ACT.Silu))
                    act.preload_act_table_set(LN_EXP)
                if kind == "ma":
                    if a == 0 and t == 0:
                        act.wait_ge(oalo_done, 2)
                        act.wait_ge(logs_done, 2 * NB)
                    free(tile, act.activation(sA[:, 2 * a + t, :], src[:, :], ACT.Sigmoid))
                if kind == "mb":
                    if a == 0 and t == 0:
                        act.wait_ge(p3_done, NB * HEADS)
                        act.wait_ge(st_done, 3 * HEADS)
                        act.wait_ge(o_done, 2 * HEADS)
                    if a == 3 and t == 0:
                        act.wait_ge(oglo_done, HEADS)
                    free(tile, act.activation(sB[:, 2 * a + t, :], src[:, :], ACT.Sigmoid))

            for g in range(GROUPS):
                n = UNIT[("v", g, 0)]
                split_hi(n + 1)
                for t in range(2):
                    evac(n, t)
                if g == 0:
                    act.wait_ge(rot_dve, 7)
                    act.activation(cs[:, 1, :], ang, ACT.Sin).then_inc(rot_act, 1)
                    act.activation(ang_abs, ang, ACT.Abs).then_inc(rot_act, 1)
                    act.wait_ge(rot_act, 2)
                    act.activation(cs[:, 0, :], ang_abs, ACT.Sin, scale=-1.0, bias=float(np.pi / 2)).then_inc(rot_act, 1)
                    act.preload_act_table_set(LN_EXP)
            for g in range(GROUPS):
                split_hi(UNIT[("qk", 0, g)] + 1)
            for g in range(GROUPS):
                split_hi(UNIT[("qk", 1, g)] + 1)
                for i in (2 * g - 1, 2 * g):
                    if i >= 0:
                        attention(0, i)
            split_hi(UNIT[("lr", 0, 0)] + 1)
            evac(UNIT[("lr", 0, 0)], 0)
            attention(0, 5)
            for h in range(HEADS):
                for u, kind in enumerate(("gqk", "gv", "gr")):
                    n = UNIT[(kind, h, 0)]
                    split_hi(n + 1)
                    for t in range(2):
                        i = 2 * u + t
                        if h == 0 and i == 0:
                            attention(0, 6)
                        evac(n, t)
                        if h == 0:
                            attention(1, i)
                        if h == 1 and i == 0:
                            attention(1, 6)
                        if h >= 2 and i in (0, 2, 3):
                            gla(h - 2, 6 + i)
                        if h >= 1:
                            gla(h - 1, i)
                    if kind == "gqk" and h == 0:
                        gates()
            for u in range(4):
                n = UNIT[("ma", u, 0)]
                split_hi(n + 1)
                for t in range(2):
                    i = 2 * u + t
                    evac(n, t)
                    if i in (0, 2, 3):
                        gla(2, 6 + i)
                    gla(3, i)
            for u in range(4):
                n = UNIT[("mb", u, 0)]
                split_hi(n + 1)
                for t in range(2):
                    if u == 0:
                        gla(3, 8 + t)
                    evac(n, t)
            split_hi(UNIT[("wa", 0, 0)] + 1)
            for u in range(4):
                split_hi(UNIT[("wg", u, 0)] + 1)
                for m in (2 * u, 2 * u + 1):
                    act.wait_ge(mix32_done, m + 1)
                    act.activation(mix_hi[:, m, :], sB[:, m, :], ACT.Copy).then_inc(mixhi_done, 1)
            for u in range(4):
                split_hi(UNIT[("wo", u, 0)] + 1)
                for m in (2 * u, 2 * u + 1):
                    evacuated(act, (("wo", u, 0), m % 2))
                    square(1, m, sq2, x1)
            act.preload_act_table_set(LN_EXP)
            inverse_root(1, rstd2[:, :], side[0][:, :])
            for k in range(KT):
                modulated(1, k, ntmp2[:, k % 2, :], ntmp1, 3 * KT)

            def up(a, s, used, value, first=False):
                i = 2 * a + s
                split_hi_ffn(a + s, 1 - s, used, value)
                for t in range(2):
                    act.wait_ge(ffn_ready, 2 * i + (t + 1))
                    if not first:
                        act.wait_ge(hid_done, i - 1)
                    act.activation(conv[:, s, t, :], bank[2 * s + t][:, :], ACT.Identity,
                                   scale=vecs[:, bass.ds(i + (V_CW2 + t * FT), 1)],
                                   bias=vecs[:, bass.ds(i + (V_CB + t * FT), 1)]).then_inc(tap2_done, 1)
                act.wait_ge(tap_done, 4 * i + 4)
                act.activation(conv[:, s, 1, :], conv[:, s, 1, :], ACT.Gelu).then_inc(gelu_done, 1)

            up(0, 0, acc_ready, N_TILES, first=True)
            up(0, 1, ffn_ready, 2, first=True)
            with act.Fori(1, FT // 2 - 1) as a:
                for s in range(2):
                    up(a, s, ffn_ready, 4 * a + 2 * s)

            def hidden_hi(j, s):
                act.activation(hs_hi[:, s, :, :], hid[:, bass.ds(2 * j, 2), :], ACT.Copy).then_inc(hs_hi_done, 1)

            act.wait_ge(hid_done, 2)
            hidden_hi(0, 0)
            for s in range(2):
                up(FT // 2 - 1, s, ffn_ready, 2 * FT - 4 + 2 * s)

            def down(a, s, used, value):
                j = 2 * a + s
                split_hi_ffn(a + (FT // 2 + s), 1 - s, used, value)
                act.wait_ge(hid_done, 2 * j + 4)
                hidden_hi(j + 1, 1 - s)

            down(0, 0, ffn_ready, 2 * FT)
            down(0, 1, down_done, 1)
            with act.Fori(1, DOWN_UNITS // 2) as a:
                for s in range(2):
                    down(a, s, down_done, 2 * a + s)
            act.preload_act_table_set(LN_EXP)
            for m in range(KT):
                act.wait_ge(x2_done, m + 1)
                square(2, m, sq2, x1)
                act.wait_ge(sq_done, 2 * KT + m + 1)
                act.activation(x1[:, m, :], x1[:, m, :], ACT.Copy, scale=vecs[:, V_FN + m:V_FN + m + 1]).then_inc(xw_done, 1)
            inverse_root(2, rstd_tok, bank[7][:, 0:NB])
            for i in range(0, 8, 2):
                half, b = divmod(i, NB)
                act.wait_ge(yt_ps, i + 1)
                act.wait_ge(rstd_done, 3)
                act.activation(y_tok[:, b, half * SEQ:(half + 1) * SEQ], bank[i][:, :], ACT.Copy,
                               scale=rstd_tok[:, b:b + 1]).then_inc(yt_act, 1)

        @block.vector
        def _(dve):
            dve.wait_ge(vec_ps, 1)
            dve.tensor_copy(vecs[:, 0:ROWS_A], bank[2][:, 0:ROWS_A]).then_inc(vec_sb, 1)

            def ada_sums(j):
                w = ada_first(j).rearrange("p k s n -> p k (s n)")
                for k in range(KT):
                    if k == 0:
                        dve.wait_ge(silu_done, 1)
                    if k % (KT // 2) == 0:
                        dve.wait_ge(ada_landed[2 * j + k // (KT // 2)], 32)
                    if k == 0:
                        ins = dve.tensor_scalar(w[:, 0, :], w[:, 0, :], c_silu[:, 0:1], None, ALU.mult)
                    else:
                        dve.wait_ge(ada_step, (KT - 1) * j + k)
                        ins = dve.scalar_tensor_tensor(w[:, 0, :], w[:, k, :], c_silu[:, k:k + 1], w[:, 0, :],
                                                       ALU.mult, ALU.add)
                    ins.then_inc(ada_step if k < KT - 1 else ada_sum, 1)

            mod_v = mod[:, 0:2 * KT].rearrange("p (s k) -> p s k", s=2)
            bias_v = vecs[:, V_AB:V_AB + 2 * KT].rearrange("p (s k) -> p s k", s=2)

            def shift_and_gain(j):
                dve.wait_ge(mod1_ps, j + 1)
                dve.wait_ge(vec_sb, 1)
                dve.tensor_tensor(mod_v[:, :, j], bank[6 + j % 2][:, 0:2], bias_v[:, :, j], ALU.add).then_inc(mod_done, 1)
                dve.wait_ge(mod_done, j + 1)
                dve.scalar_tensor_tensor(gain[:, 0, j:j + 1], mod[:, KT + j:KT + j + 1], 1.0,
                                         vecs[:, V_N1 + j:V_N1 + j + 1], ALU.add, ALU.mult).then_inc(gain_done, 1)

            def lower(part, k, tmp):
                dve.wait_ge(nt_done, part * KT + k + 1)
                dve.wait_ge(hh_done, part * KT + k + 1)
                dve.tensor_tensor(h_lo[:, k, :], tmp[:, k % 2, :], h_hi[:, k, :].bitcast(F32),
                                  ALU.subtract).then_inc(hl_done, 1)

            def split_lo(n, quarter=None):
                if n == N_UNITS:
                    return split_lo_ffn(0, 0)
                dve.wait_ge(hi_done, n + 1)
                for r, hv, lv in views(n):
                    if quarter is not None:
                        r, hv, lv = (v[:, quarter * UE // 4:(quarter + 1) * UE // 4] for v in (r, hv, lv))
                    last = dve.tensor_tensor(lv, r, hv.bitcast(F32), ALU.subtract)
                if quarter in (None, 3):
                    last.then_inc(raw_used, 1)

            def split_lo_ffn(pair, odd):
                slot = 1 - odd
                dve.wait_ge(hi_done, pair * 2 + (odd + N_UNITS + 1))
                dve.tensor_tensor(w_lo[:, slot, :], raw[:, slot, :], w_hi[:, slot, :].bitcast(F32),
                                  ALU.subtract).then_inc(raw_used, 1)

            def modulate(n):
                if n >= 2 * KT:
                    return
                r, k = divmod(n, KT)
                q = RAW_AT[("ada", n)]
                dve.wait_ge(landed[q % 2], LANDED[q])
                if k > 0:
                    dve.wait_ge(raw_used, RAW_AT[("ada", n - 1)] + 1)
                src = raw[:, q % 2, :]
                if k == 0:
                    if r == 1:
                        dve.wait_ge(acc_ready, TILE[("ada", 0)] + 1)
                    ins = dve.tensor_scalar(ada_acc[:, :], src, c_silu[:, 0:1], None, ALU.mult)
                else:
                    ins = dve.scalar_tensor_tensor(ada_acc[:, :], src, c_silu[:, k:k + 1], ada_acc[:, :],
                                                   ALU.mult, ALU.add)
                ins.then_inc(raw_used, 1)

            def acc(tile):
                i = TILE[tile]
                dve.wait_ge(acc_ready, i + 1)
                return bank[i % 2]

            def free(tile, ins):
                ins.then_inc(acc_free[TILE[tile] % 2], 1)

            def ada_tile(r):
                src = acc(("ada", r))
                at = 2 * KT * (r + 1)
                free(("ada", r), dve.tensor_tensor(mod[:, at:at + 2 * KT], src[:, 0:2 * KT],
                                                   vecs[:, V_AB + at:V_AB + at + 2 * KT], ALU.add))
                if r == 1:
                    evacuated(dve, ("ada", 1))
                    dve.scalar_tensor_tensor(gain[:, 1, :], mod[:, 4 * KT:5 * KT], 1.0, vecs[:, V_N2:V_N2 + KT],
                                             ALU.add, ALU.mult).then_inc(gain_done, 1)

            def rotate(j):
                p, g = divmod(j, GROUPS)
                if j > 0:
                    dve.wait_ge(rope_sum, 2 * j)
                if j > 1:
                    dve.wait_ge(qk_in[j % 2], 16 * 8 * (j // 2))
                unit = ("qk", p, g)
                first = acc((unit, 0))
                dve.tensor_tensor(rope[:, j % 2, 0, :], first[:, :], cs[:, 0, :], ALU.mult)
                free((unit, 0), dve.tensor_tensor(rope_t[:, 1, :], first[:, :], cs[:, 1, :], ALU.mult))
                second = acc((unit, 1))
                dve.tensor_tensor(rope_t[:, 0, :], second[:, :], cs[:, 1, :], ALU.mult)
                free((unit, 1), dve.tensor_tensor(rope[:, j % 2, 1, :], second[:, :], cs[:, 0, :], ALU.mult))

            def mask_and_max(hh):
                p, hd = divmod(hh, 2)
                prev_own, own = cst[:, C_MSK:C_MSK + 2 * P], cst[:, C_MSK + P:C_MSK + 2 * P]
                own4 = own.rearrange("p (a n) -> p a n", a=1).broadcast_to((P, DIL, P))
                mod4 = cst[:, C_MOD:C_MOD + P].rearrange("p (a n) -> p a n", a=1).broadcast_to((P, DIL, P))
                two = prev_own.rearrange("p (a n) -> p a n", a=1).broadcast_to((P, 2, 2 * P))
                for bk in range(4):
                    dve.wait_ge(sc_done, 4 * hh + bk + 1)
                    if hh >= 2:
                        dve.wait_ge(tr_ps, 4 * (hh - 2) + bk + 1)
                    at, w = BANK_AT[bk], BANK_W[bk]
                    dst, src = S[:, hd, at:at + w], side[bk][:, 0:w]
                    if bk == 1:
                        m = cst[:, C_MSK:C_MSK + 3 * P]
                    else:
                        m = (two, None, own4, mod4)[bk]
                        n_b = 2 if bk == 0 else DIL
                        dst, src = (v.rearrange("p (a n) -> p a n", a=n_b) for v in (dst, src))
                    dve.tensor_tensor(dst, src, m, ALU.add).then_inc(msk_done, 1)
                for bk in range(4):
                    dve.wait_ge(msk_done, 4 * hh + bk + 1)
                    at = BANK_AT[bk]
                    if hd == 0 and bk == 0 and p > 0:
                        dve.wait_ge(mxr_ps, p)
                    if bk == 0:
                        dve.tensor_reduce(mx[:, 1:3, hd], S[:, hd, 0:4 * P].rearrange("p (a n) -> p a n", a=2),
                                          AX.X, ALU.max)
                    elif bk == 1:
                        dve.tensor_reduce(mx[:, 3:4, hd], S[:, hd, at:at + 2 * P], AX.X, ALU.max)
                        dve.tensor_reduce(mx[:, 0:1, hd], S[:, hd, at + 2 * P:at + 3 * P], AX.X, ALU.max)
                    else:
                        dve.tensor_reduce(mg[:, bk - 2, :], S[:, hd, at:at + 4 * P].rearrange("p (a n) -> p a n", a=DIL),
                                          AX.X, ALU.max).then_inc(mx1_done, 1)
                dve.wait_ge(mx1_done, 2 * hh + 2)
                dve.tensor_tensor(mx[:, NB:2 * NB, hd], mg[:, 0, :], mg[:, 1, :], ALU.max).then_inc(mx_done, 1)
                dve.wait_ge(mx_done, hh + 1)

            def attention(p, i):
                if i in (0, 1):
                    mask_and_max(2 * p + i)
                if i == 2:
                    dve.wait_ge(mxr_ps, p + 1)
                    if p > 0:
                        dve.wait_ge(mxc_ps, p)
                    dve.tensor_copy(rowm[:, 0, :], side[0][0:2, :]).then_inc(rowmax_done, 1)
                    dve.wait_ge(rowmax_done, 2 * p + 1)
                    dve.tensor_tensor(rowm[:, 1, :], side[1][0:2, :], rowm[:, 0, :], ALU.max).then_inc(rowmax_done, 1)
                if i == 3:
                    dve.wait_ge(mxc_ps, p + 1)
                    if p > 0:
                        dve.wait_ge(exp_done, 8 * p)
                    dve.tensor_scalar(negm[:, :, :].rearrange("p a b -> p (a b)"), side[0][:, 0:16],
                                      -DH ** -0.5, None, ALU.mult).then_inc(negm_done, 1)
                if i in (4, 5):
                    hh = 2 * p + i - 4
                    for bk in (2, 3):
                        dve.wait_ge(tr_ps, 4 * hh + bk + 1)
                        if hh >= 1:
                            dve.wait_ge(pv_done, hh)
                        at = BANK_AT[bk]
                        dve.tensor_copy(PT[:, at:at + BANK_W[bk]], side[bk][:, 0:BANK_W[bk]]).then_inc(pt_dve, 1)
                if i in (5, 6):
                    hh = 2 * p + i - 5
                    hd = hh % 2
                    top, bottom = slice(0, DH), slice(DH, P)
                    num, den = (top, bottom) if hd == 0 else (bottom, top)
                    dve.wait_ge(perm_sb, hh + 1)
                    if hh > 0:
                        dve.wait_ge(oa32_done, hh)
                        dve.wait_ge(oln_done, hh)
                    dve.tensor_tensor(osum[:, :], side[4][:, :], ocomb[:, :], ALU.add).then_inc(osum_done, 1)
                    dve.wait_ge(osum_done, hh + 1)
                    dve.wait_ge(orec_done, hh + 1)
                    if p > 0:
                        dve.wait_ge(oalo_done, p)
                    dve.tensor_tensor(oa32[num, :], osum[num, :], orec[num, :], ALU.mult).then_inc(oa32_done, 1)
                if i == 6:
                    dve.wait_ge(oa32_done, 2 * p + 2)
                    dve.wait_ge(oahi_done, p + 1)
                    dve.tensor_tensor(oa_lo[:, p, :], oa32[:, :], oa_hi[:, p, :].bitcast(F32),
                                      ALU.subtract).then_inc(oalo_done, 1)
                    dve.wait_ge(oalo_done, p + 1)

            def gates():
                dve.wait_ge(sc_done, 16)
                for b in range(NB):
                    z = acc(("z", b))
                    dve.wait_ge(z_abs, b + 1)
                    free(("z", b), dve.tensor_scalar(logs[:, b, :], z[:, :], -1.0, 0.0, ALU.mult, ALU.max))
                    evacuated(dve, ("z", b))
                    dve.wait_ge(z_ln, b + 1)
                    dve.tensor_tensor(logs[:, b, :], logs[:, b, :], za[:, b % 2, :], ALU.add).then_inc(logs_done, 2)

            def keys(h, b):
                u = NB * h + b
                if u >= 1:
                    dve.wait_ge(at_ps, u)
                    dve.wait_ge(kk_done, u)
                own = k_in[:, h % 2, b * P:(b + 1) * P]
                dve.tensor_copy(kk[:, :, :], own.rearrange("p (a n) -> p a n", a=1).broadcast_to((P, NCH, P))).then_inc(kk_step, 1)
                for n in range(NCH):
                    w = CHUNK * (n + 1)
                    decay = eb[:, b * P + w - 1:b * P + w]
                    dve.wait_ge(kk_step, NCH * u + n + 1)
                    dst = kk[:, n + 1, 0:w] if n < NCH - 1 else ke[:, :]
                    dve.tensor_scalar(dst, kk[:, n, 0:w], decay, None,
                                      ALU.mult).then_inc(kk_step if n < NCH - 1 else kk_done, 1)

            def gla(h, i):
                if i == 0:
                    q, k = q_in[:, h % 2, :], k_in[:, h % 2, :]
                    evacuated(dve, (("gqk", h, 0), 0))
                    evacuated(dve, (("gqk", h, 0), 1))
                    dve.wait_ge(gexp_done, 3 * h + 3)
                    dve.tensor_tensor(k, k, enb[:, :], ALU.mult).then_inc(qg_done, 1)
                    dve.tensor_tensor(q, q, eb[:, :], ALU.mult).then_inc(qg_done, 1)
                    if h > 0:
                        dve.wait_ge(p3_done, NB * h)
                    dve.wait_ge(qg_done, 2 * h + 2)
                    keys(h, 0)
                    chunks = q.rearrange("p (b n c) -> p b n c", b=NB, n=NCH)
                    start = ed[:, :, 0:NCH].rearrange("p b (n o) -> p b n o", o=1).broadcast_to((P, NB, NCH, CHUNK))
                    dve.tensor_tensor(qB[:, :].rearrange("p (b n c) -> p b n c", b=NB, n=NCH), chunks, start,
                                      ALU.mult).then_inc(qB_done, 1)
                if 2 <= i <= 5:
                    b = i - 2
                    u = NB * h + b
                    dve.wait_ge(at_ps, u + 1)
                    if u >= 2:
                        dve.wait_ge(p3_done, u - 1)
                    dve.copy_predicated(at_sb[:, u % 2, :], cst[:, C_KEEP:C_KEEP + P].bitcast(U32),
                                        side[2][:, 0:P]).then_inc(at_done, 1)
                    if b + 1 < NB:
                        keys(h, b + 1)
                if 3 <= i <= 5:
                    b = i - 3
                    dve.wait_ge(p3_done, NB * h + b + 1)
                    new = side[1][:, 64:64 + DV]
                    if b == 0:
                        if h > 0:
                            dve.wait_ge(st_done, 3 * h)
                        ins = dve.tensor_copy(state[:, :], new)
                    else:
                        dve.wait_ge(st_done, 3 * h + b)
                        ins = dve.scalar_tensor_tensor(state[:, :], state[:, :], ed[:, b, NCH:NCH + 1], new,
                                                       ALU.mult, ALU.add)
                    ins.then_inc(st_done, 1)
                if i == 6:
                    dve.wait_ge(p3_done, NB * h + NB)
                    if h > 0:
                        dve.wait_ge(oglo_done, h)
                    for v in range(2):
                        dve.tensor_copy(o_sb[:, v, :], side[4 + v][:, :]).then_inc(o_done, 1)
                if i == 8:
                    dve.wait_ge(grstd_done, h + 1)
                    dve.wait_ge(osq_done, h + 1)
                    dve.tensor_tensor(o_sb[:, :, :], o_sb[:, :, :],
                                      ors[:, :].rearrange("p (a n) -> p a n", a=1).broadcast_to((P, 2, SEQ)),
                                      ALU.mult).then_inc(on_done, 1)
                    dve.wait_ge(on_done, h + 1)
                    evacuated(dve, (("gr", h, 0), 0))
                    evacuated(dve, (("gr", h, 0), 1))
                    for v in range(2):
                        dve.scalar_tensor_tensor(o_sb[:, v, :], o_sb[:, v, :], vecs[:, V_GN + v:V_GN + v + 1],
                                                 gr[:, h % 2, v, :], ALU.mult, ALU.mult).then_inc(og32_done, 1)
                if i == 9:
                    dve.wait_ge(og32_done, 2 * h + 2)
                    dve.wait_ge(oghi_done, h + 1)
                    dve.tensor_tensor(og_lo[:, 2 * h:2 * h + 2, :], o_sb[:, :, :],
                                      og_hi[:, 2 * h:2 * h + 2, :].bitcast(F32), ALU.subtract).then_inc(oglo_done, 1)

            def rotary_angles():
                dve.wait_ge(pos_in, 16)
                dve.tensor_copy(ang, pos_i).then_inc(rot_dve, 1)
                dve.wait_ge(cst_in, 16)
                dve.wait_ge(rot_dve, 1)
                dve.tensor_scalar(ang, ang, cst[:, C_FRQ:C_FRQ + 1], None, ALU.mult).then_inc(rot_dve, 1)
                dve.wait_ge(rot_dve, 2)
                dve.tensor_scalar(turns, ang, float(1.0 / (2 * np.pi)), ROUND, ALU.mult, ALU.add).then_inc(rot_dve, 1)
                dve.wait_ge(rot_dve, 3)
                dve.tensor_scalar(turns, turns, ROUND, None, ALU.subtract).then_inc(rot_dve, 1)
                for n, part in enumerate(TWO_PI):
                    dve.wait_ge(rot_dve, 4 + n)
                    last = dve.scalar_tensor_tensor(ang, turns, -part, ang, ALU.mult, ALU.add)
                    if n < 2:
                        last.then_inc(rot_dve, 1)
                    else:
                        last.then_inc(rot_sum, 1)
                dve.wait_ge(rot_sum, 1)
                dve.tensor_scalar(ang, ang, 3.1415925, -3.1415925, ALU.min, ALU.max).then_inc(rot_dve, 1)

            for j in range(KT // 2):
                ada_sums(j)
                if j > 0:
                    shift_and_gain(j - 1)
            shift_and_gain(KT // 2 - 1)
            lower(0, 0, ntmp)
            split_lo(0)
            for j in range(1, KT // 2):
                lower(0, j, ntmp)
            for j in range(KT // 2, KT):
                ada_sums(j)
                if j > KT // 2:
                    lower(0, j - 1, ntmp)
                shift_and_gain(j)
            lower(0, KT - 1, ntmp)
            for n in range(GROUPS):
                modulate(n)
                split_lo(n + 1)
                if n == 0:
                    rotary_angles()
                    dve.wait_ge(vec_ps, 3)
                    for half in range(2):
                        dve.tensor_copy(vecs[:, ROWS_A + half * ROWS_B:ROWS_A + (half + 1) * ROWS_B],
                                        bank[2][:, P * (half + 1):P * (half + 1) + ROWS_B]).then_inc(vec_sb, 1)
            dve.wait_ge(rot_act, 3)
            for p in range(2):
                for g in range(GROUPS):
                    n = UNIT[("qk", p, g)]
                    modulate(n)
                    split_lo(n + 1)
                    if p == 1 and g > 0:
                        attention(0, 2 * g - 1)
                    rotate(GROUPS * p + g)
                    if p == 1:
                        attention(0, 2 * g)
                    if (p, g) == (1, 1):
                        ada_tile(0)
            n = UNIT[("lr", 0, 0)]
            modulate(n)
            split_lo(n + 1)
            attention(0, 5)
            for h in range(HEADS):
                for u, kind in enumerate(("gqk", "gv", "gr")):
                    n = UNIT[(kind, h, 0)]
                    modulate(n)
                    split_lo(n + 1)
                    for t in range(2):
                        i = 2 * u + t
                        if h == 0 and i == 0:
                            attention(0, 6)
                        if h == 0:
                            attention(1, i)
                        if h == 1 and i == 0:
                            attention(1, 6)
                            dve.memset(at_sb[:, :, :], 0.0).then_inc(at_zero, 1)
                            dve.wait_ge(at_zero, 1)
                        if h >= 2 and i == 0:
                            gla(h - 2, 6)
                        if h >= 1:
                            gla(h - 1, i)
                        if h >= 2 and i in (2, 3):
                            gla(h - 2, 6 + i)
                    if kind == "gqk" and h == 0:
                        gates()
                    if (kind, h) == ("gv", 2):
                        ada_tile(1)
            for u in range(4):
                split_lo(UNIT[("ma", u, 0)] + 1)
                for t in range(2):
                    i = 2 * u + t
                    if i == 0:
                        gla(2, 6)
                    gla(3, i)
                    if i in (2, 3):
                        gla(2, 6 + i)
            for u in range(4):
                split_lo(UNIT[("mb", u, 0)] + 1)
                if u == 0:
                    for i in (8, 9):
                        gla(3, i)
            n = UNIT[("wa", 0, 0)]
            for m in range(KT):
                tile = (UNITS[n], m)
                evacuated(dve, (("mb", m // 2, 0), m % 2))
                free(tile, dve.tensor_tensor(sB[:, m, :], acc(tile)[:, :], sB[:, m, :], ALU.mult))
                if m < 4:
                    split_lo(n + 1, m)
            for u in range(4):
                split_lo(UNIT[("wg", u, 0)] + 1)
                for t in range(2):
                    m = 2 * u + t
                    tile = (("wg", u, 0), t)
                    if m >= 2:
                        dve.wait_ge(mix32_done, m - 1)
                    evacuated(dve, (("wa", 0, 0), m))
                    evacuated(dve, (("ma", m // 2, 0), m % 2))
                    src = acc(tile)
                    free(tile, dve.tensor_tensor(mtmp[:, m % 2, :], src[:, :], sA[:, m, :], ALU.mult))
                    dve.wait_ge(mixhi_done, m + 1)
                    dve.tensor_tensor(mix_lo[:, m, :], sB[:, m, :], mix_hi[:, m, :].bitcast(F32),
                                      ALU.subtract).then_inc(mixlo_done, 1)
            for u in range(4):
                split_lo(UNIT[("wo", u, 0)] + 1)
                for t in range(2):
                    m = 2 * u + t
                    tile = (("wo", u, 0), t)
                    dve.wait_ge(x_back, 16)
                    src = acc(tile)
                    free(tile, dve.scalar_tensor_tensor(x1[:, m, :], src[:, :], mod[:, 2 * KT + m:2 * KT + m + 1],
                                                        x1[:, m, :], ALU.mult, ALU.add))
            for t in range(2):
                evacuated(dve, (("wo", 3, 0), t))
            dve.wait_ge(rstd_done, 2)
            for k in range(KT):
                if k >= 2:
                    dve.wait_ge(hh_done, KT + k - 1)
                dve.tensor_tensor(ntmp2[:, k % 2, :], x1[:, k, :], rstd2[:, :], ALU.mult).then_inc(xn_done, 1)
                if k >= 1:
                    lower(1, k - 1, ntmp1)
            lower(1, KT - 1, ntmp1)

            def up(a, s):
                i = 2 * a + s
                split_lo_ffn(a + s, 1 - s)
                for t in range(2):
                    dve.wait_ge(tap2_done, 2 * i + (t + 1))
                    src = bank[2 * s + t]
                    for tap, col in ((1, V_CW1), (2, V_CW0)):
                        if tap == 2:
                            dve.wait_ge(tap_done, 4 * i + (2 * t + 1))
                        ins = dve.scalar_tensor_tensor(conv[:, s, t, tap:SEQ], src[:, 0:SEQ - tap],
                                                       vecs[:, bass.ds(i + (col + t * FT), 1)],
                                                       conv[:, s, t, tap:SEQ], ALU.mult, ALU.add)
                        ins.then_inc(tap_done, 1)
                dve.wait_ge(gelu_done, i + 1)
                dve.tensor_tensor(hid[:, bass.ds(i, 1), :].rearrange("p a n -> p (a n)"), conv[:, s, 0, :],
                                  conv[:, s, 1, :], ALU.mult).then_inc(hid_done, 1)

            with dve.Fori(0, FT // 2 - 1) as a:
                for s in range(2):
                    up(a, s)

            def hidden_lo(j, s):
                dve.wait_ge(hs_hi_done, j + 1)
                dve.tensor_tensor(hs_lo[:, s, :, :], hid[:, bass.ds(2 * j, 2), :], hs_hi[:, s, :, :].bitcast(F32),
                                  ALU.subtract).then_inc(hs_lo_done, 1)

            hidden_lo(0, 0)
            for s in range(2):
                up(FT // 2 - 1, s)
            with dve.Fori(0, DOWN_UNITS // 2) as a:
                for s in range(2):
                    split_lo_ffn(a + (FT // 2 + s), 1 - s)
                    hidden_lo(2 * a + s + 1, 1 - s)
            for m in range(KT):
                dve.wait_ge(down_tile, m + 1)
                dve.scalar_tensor_tensor(x1[:, m, :], bank[m][:, :], mod[:, 5 * KT + m:5 * KT + m + 1], x1[:, m, :],
                                         ALU.mult, ALU.add).then_inc(x2_done, 1)
            dve.wait_ge(sum_done, SUMS[2] + KT - 1)
            dve.wait_ge(sq_done, 3 * KT)
            dve.tensor_tensor(sq_sum2[:, :], sq_sum2[:, :], sq2[:, 1, :], ALU.add).then_inc(sum_done, 1)
            for i in range(1, 8, 2):
                half, b = divmod(i, NB)
                dve.wait_ge(yt_ps, i + 1)
                dve.wait_ge(rstd_done, 3)
                dve.tensor_scalar(y_tok[:, b, half * SEQ:(half + 1) * SEQ], bank[i][:, :], rstd_tok[:, b:b + 1],
                                  None, ALU.mult).then_inc(yt_dve, 1)

        @block.tensor
        def _(pe):
            ident = cst[:, C_ID:C_ID + P]

            def three(out_ap, w, x_, first, last):
                (wh, wl), (xh, xl) = w, x_
                pe.matmul(out_ap, wh, xh, start=first, stop=False, skip_group_check=True)
                pe.matmul(out_ap, wh, xl, start=False, stop=False, skip_group_check=True)
                return pe.matmul(out_ap, wl, xh, start=False, stop=last, skip_group_check=True)

            pe.wait_ge(cst_in, 16)
            pe.wait_ge(rows_in, 6 * 16)
            pe.transpose(bank[2][:, 0:ROWS_A], rows_a[:, :], ident[0:ROWS_A, 0:ROWS_A]).then_inc(vec_ps, 1)
            pe.wait_ge(x_in, NB * 16)
            pe.wait_ge(ones_set, 1)

            def sum_of_squares(k):
                pe.wait_ge(sq_done, k + 1)
                ins = pe.matmul(bank[0][:, :], ones[:, :], sq[:, k % 2, :], start=(k == 0), stop=(k == KT - 1))
                ins.then_inc(sq_used if k < KT - 1 else ssq_ps, 1)

            for k in range(KT):
                if k >= 4:
                    pe.wait_ge(xt_sb, k - 3)
                for b in range(NB):
                    last = pe.transpose(bank[3 + k % 4][:, b * P:(b + 1) * P], x_tok[:, b, k * P:(k + 1) * P], ident)
                last.then_inc(xt_ps, 1)
                if k >= 1:
                    sum_of_squares(k - 1)
            sum_of_squares(KT - 1)

            def shift_scale(j):
                pe.wait_ge(ada_sum, j + 1)
                if j < 2:
                    pe.wait_ge(xt_sb, KT)
                else:
                    pe.wait_ge(mod_done, j - 1)
                for s_ in range(2):
                    last = pe.matmul(bank[6 + j % 2][:, s_:s_ + 1], ada_first(j)[:, 0, s_, :], ones[:, 0:1],
                                     start=True, stop=True, skip_group_check=True)
                last.then_inc(mod1_ps, 1)

            def take(i):
                if i >= 2:
                    pe.wait_ge(acc_free[i % 2], i // 2)
                return bank[i % 2]

            def product(n, t):
                kind, a, _ = UNITS[n]
                slot = n % 2
                i = TILE[(UNITS[n], t)]
                dst = take(i)
                if t == 0:
                    pe.wait_ge(raw_used, RAW_AT[("w", n)] + 1)
                if kind in ("v", "gv"):
                    for half in range(2):
                        blk = 2 * t + half
                        tok = slice(blk * P, (blk + 1) * P) if kind == "gv" or a == 0 else slice(blk, SEQ, DIL)
                        for k in range(KT):
                            w = tuple(v[:, slot, k * UW:(k + 1) * UW] for v in (w_hi, w_lo))
                            s = tuple(v[:, k, tok] for v in (h_hi, h_lo))
                            last = three(dst[:, half * UW:(half + 1) * UW], s, w, k == 0, k == KT - 1)
                else:
                    if kind == "wa":
                        nk, width, at, src = 2, D, t * P, (oa_hi, oa_lo)
                    elif kind == "lr":
                        nk, width, at, src = KT, LOWRANK, 0, (h_hi, h_lo)
                    else:
                        nk, width, at = KT, UW, t * P
                        src = {"wg": (og_hi, og_lo), "wo": (mix_hi, mix_lo)}.get(kind, (h_hi, h_lo))
                    m = LOWRANK if kind == "lr" else P
                    if kind == "wa" and t == 0:
                        pe.wait_ge(oalo_done, 2)
                    if kind == "wg" and a == 0 and t == 0:
                        pe.wait_ge(oglo_done, HEADS)
                    for k in range(nk):
                        if kind == "wo" and a == 0 and t == 0:
                            pe.wait_ge(mixlo_done, k + 1)
                        w = tuple(v[:, slot, k * width + at:k * width + at + m] for v in (w_hi, w_lo))
                        last = three(dst[0:m, :], w, tuple(v[:, k, :] for v in src), k == 0, k == nk - 1)
                last.then_inc(acc_ready, 1)

            def ada_tile(r):
                dst = take(TILE[("ada", r)])
                pe.wait_ge(raw_used, RAW_AT[("ada", KT * (r + 1) - 1)] + 1)
                for j in range(2 * KT):
                    last = pe.matmul(dst[:, j:j + 1], ada_acc[:, j * P:(j + 1) * P], ones[:, 0:1],
                                     start=(j == 0), stop=True, skip_group_check=True)
                last.then_inc(acc_ready, 1)

            def scores(hh):
                p, hd = divmod(hh, 2)
                if hd == 0:
                    for odd in range(2):
                        pe.wait_ge(qk_in[odd], 16 * 8 * ((GROUPS * (p + 1) + 1 - odd) // 2))
                for bk in range(4):
                    if hh >= 1:
                        pe.wait_ge(msk_done, 4 * (hh - 1) + bk + 1)
                    if hd == 0 and p > 0:
                        pe.wait_ge(pt_act if bk < 2 else pt_dve, 4 * p)
                    if bk < 2:
                        blocks = [(0, 1), (2 * P, 2)] if bk == 0 else [(0, 3), (2 * P, 0)]
                        for col, b in blocks:
                            lo = max(b - 1, 0) * P
                            keys = slice(lo, (b + 1) * P)
                            last = pe.matmul(side[bk][:, col:col + (b + 1) * P - lo], qk[:, 0, 0, hd, b * P:(b + 1) * P],
                                             qk[:, 0, 1, hd, keys], start=True, stop=True, skip_group_check=True)
                    else:
                        for r in range(DIL):
                            tok = slice(r, SEQ, DIL)
                            last = pe.matmul(side[bk][:, r * P:(r + 1) * P], qk[:, bk - 1, 0, hd, tok],
                                             qk[:, bk - 1, 1, hd, tok], start=True, stop=True, skip_group_check=True)
                    last.then_inc(sc_done, 1)

            def transposes(hh):
                hd = hh % 2
                for bk in range(4):
                    pe.wait_ge(exp_done, 4 * hh + bk + 1)
                    if hd == 1:
                        pe.wait_ge(pt_act if bk < 2 else pt_dve, 2 * hh - (1 - bk % 2))
                    for col in range(0, BANK_W[bk], P):
                        last = pe.transpose(side[bk][:, col:col + P], S[:, hd, BANK_AT[bk] + col:BANK_AT[bk] + col + P], ident)
                    last.then_inc(tr_ps, 1)

            def values(hh):
                pe.wait_ge(pt_act, 2 * hh + 2)
                pe.wait_ge(pt_dve, 2 * hh + 2)
                if hh >= 1:
                    pe.wait_ge(osum_done, hh)
                if hh == 0:
                    evacuated(pe, (("v", GROUPS - 1, 0), 0))
                    evacuated(pe, (("v", GROUPS - 1, 0), 1))
                at = {1: 0, 2: 2 * P, 3: 4 * P}
                for b in range(NB):
                    dst = side[4][:, b * P:(b + 1) * P]
                    if b == 0:
                        pe.matmul(dst, v_ext[:, 0, 0, hh, :], PT[:, 6 * P:7 * P], start=True, stop=True, skip_group_check=True)
                    else:
                        for j in range(2):
                            pe.matmul(dst, v_ext[:, b - 1 + j, 0, hh, :], PT[:, at[b] + j * P:at[b] + (j + 1) * P],
                                      start=(j == 0), stop=(j == 1), skip_group_check=True)
                for r in range(DIL):
                    for g in (1, 2):
                        col = BANK_AT[g + 1] + r * P
                        last = pe.matmul(side[5][:, r * P:(r + 1) * P], v_ext[:, r, g, hh, :], PT[:, col:col + P],
                                         start=(g == 1), stop=(g == 2), skip_group_check=True)
                last.then_inc(pv_done, 1)

            def attention(p, i):
                if i in (0, 1):
                    scores(2 * p + i)
                if i == 2:
                    pe.wait_ge(mx_done, 2 * p + 2)
                    for b in range(NB):
                        pe.transpose(side[0][0:2, b * P:(b + 1) * P], mx[:, b, :], ident)
                    for r in range(DIL):
                        last = pe.transpose(side[1][0:2, r::DIL], mx[:, NB + r, :], ident)
                    last.then_inc(mxr_ps, 1)
                if i == 3:
                    pe.wait_ge(rowmax_done, 2 * p + 2)
                    for b in range(NB):
                        pe.transpose(side[0][:, 2 * b:2 * b + 2], rowm[:, 1, b * P:(b + 1) * P], ident[0:2, 0:2])
                    for r in range(DIL):
                        c0 = 2 * (NB + r)
                        last = pe.transpose(side[0][:, c0:c0 + 2], rowm[:, 1, r::DIL], ident[0:2, 0:2])
                    last.then_inc(mxc_ps, 1)
                if i == 4:
                    transposes(2 * p)
                if i == 5:
                    values(2 * p)
                    transposes(2 * p + 1)
                if i == 6:
                    values(2 * p + 1)

            def gate_tiles():
                pe.wait_ge(w2_in, 32)
                evacuated(pe, (("lr", 0, 0), 0))
                for b in range(NB):
                    dst = take(TILE[("z", b)])
                    pe.matmul(dst[:, :], lrT[0:LOWRANK + 1, b * P:(b + 1) * P], w2b[:, :],
                              start=True, stop=True).then_inc(acc_ready, 1)

            def within(h, b):
                u = NB * h + b
                pe.wait_ge(kk_done, u + 1)
                if u >= 1:
                    pe.wait_ge(at_done, u)
                    pe.wait_ge(kt_done, u)
                for n in range(NCH):
                    at = CHUNK * n
                    pe.matmul(side[2][:, at:at + CHUNK], kk[:, n, :], q_in[:, h % 2, b * P + at:b * P + at + CHUNK],
                              start=True, stop=True, skip_group_check=True)
                pe.transpose(side[3][:, 0:P], ke[:, :], ident).then_inc(at_ps, 1)

            def outputs(h, b):
                u = NB * h + b
                pe.wait_ge(at_done, u + 1)
                pe.wait_ge(kt_done, u + 1)
                if b == 0:
                    if h == 0:
                        pe.wait_ge(osum_done, 4)
                    else:
                        pe.wait_ge(o_done, 2 * h)
                    evacuated(pe, (("gv", h, 0), 0))
                    evacuated(pe, (("gv", h, 0), 1))
                else:
                    pe.wait_ge(st_done, 3 * h + b)
                    pe.wait_ge(qB_done, h + 1)
                for v in range(2):
                    dst = side[4 + v][:, b * P:(b + 1) * P]
                    last = pe.matmul(dst, gv[:, h % 2, b, v * P:(v + 1) * P], at_sb[:, u % 2, :],
                                     start=True, stop=(b == 0), skip_group_check=True)
                    if b > 0:
                        last = pe.matmul(dst, state[:, v * P:(v + 1) * P], qB[:, b * P:(b + 1) * P],
                                         start=False, stop=True, skip_group_check=True)
                if b < NB - 1:
                    last = pe.matmul(side[1][:, 64:64 + DV], kt_sb[:, u % 2, :], gv[:, h % 2, b, :],
                                     start=True, stop=True, skip_group_check=True)
                last.then_inc(p3_done, 1)

            def gla(h, i):
                if i == 0:
                    pe.wait_ge(logs_done, 2 * NB)
                    if h >= 1:
                        pe.wait_ge(gexp_done, 3 * h)
                        pe.wait_ge(st_done, 3 * h)
                    if h >= 2:
                        pe.wait_ge(gln_done, h - 1)
                    for b in range(NB):
                        g = logs[:, b, h * P:(h + 1) * P]
                        pe.matmul(side[0][:, b * P:(b + 1) * P], g, cst[:, C_TRI:C_TRI + P],
                                  start=True, stop=True, skip_group_check=True)
                        c0 = b * (NCH + 1)
                        last = pe.matmul(side[1][:, c0:c0 + NCH + 1], g, cst[:, C_TRI + P:C_TRI + P + NCH + 1],
                                         start=True, stop=True, skip_group_check=True)
                    last.then_inc(b_ps, 1)
                if 2 <= i <= 5:
                    within(h, i - 2)
                if 3 <= i <= 6:
                    outputs(h, i - 3)
                if i == 8:
                    pe.wait_ge(osum2_done, h + 1)
                    pe.wait_ge(gexp_done, 3 * min(h + 2, HEADS))
                    pe.matmul(side[0][:, :], ones[:, :], osq[:, 0, :], start=True, stop=True,
                              skip_group_check=True).then_inc(gssq_ps, 1)

            for j in range(KT // 2):
                shift_scale(j)
            pe.wait_ge(raw_used, 1)
            pe.wait_ge(rstd_done, 1)
            for k in range(KT):
                if KT // 2 <= k + 2 < KT:
                    shift_scale(k + 2)
                pe.wait_ge(hl_done, k + 1)
                w = tuple(v[:, 0, k * UW:(k + 1) * UW] for v in (w_hi, w_lo))
                for blk in range(NB):
                    s = tuple(v[:, k, blk * P:(blk + 1) * P] for v in (h_hi, h_lo))
                    last = three(bank[blk // 2][:, blk % 2 * UW:(blk % 2 + 1) * UW], s, w,
                                 k == 0 and blk % 2 == 0, k == KT - 1)
                    if k == KT - 1 and blk % 2 == 1:
                        last.then_inc(acc_ready, 1)
            pe.wait_ge(conv_in, 3 * 16)
            for half in range(2):
                pe.transpose(bank[2][:, P * (half + 1):P * (half + 1) + ROWS_B], rows_b[:, half, :],
                             ident[0:ROWS_B, 0:ROWS_B]).then_inc(vec_ps, 1)

            for n in range(1, GROUPS):
                for t in range(2):
                    product(n, t)
            for p in range(2):
                for g in range(GROUPS):
                    for t in range(2):
                        product(UNIT[("qk", p, g)], t)
                        if p == 1 and 2 * g + t > 0:
                            attention(0, 2 * g + t - 1)
                    if (p, g) == (1, 1):
                        ada_tile(0)
            product(UNIT[("lr", 0, 0)], 0)
            attention(0, 5)
            for h in range(HEADS):
                for u, kind in enumerate(("gqk", "gv", "gr")):
                    for t in range(2):
                        i = 2 * u + t
                        product(UNIT[(kind, h, 0)], t)
                        if h == 0 and i == 0:
                            attention(0, 6)
                        if h == 0:
                            attention(1, i)
                        if h == 1 and i == 0:
                            attention(1, 6)
                        if h >= 2 and i in (0, 2, 3):
                            gla(h - 2, 6 + i)
                        if h >= 1:
                            gla(h - 1, i)
                    if kind == "gqk" and h == 0:
                        gate_tiles()
                    if (kind, h) == ("gv", 2):
                        ada_tile(1)
            for u in range(4):
                for t in range(2):
                    i = 2 * u + t
                    product(UNIT[("ma", u, 0)], t)
                    if i in (0, 2, 3):
                        gla(2, 6 + i)
                    gla(3, i)
            for u in range(4):
                for t in range(2):
                    product(UNIT[("mb", u, 0)], t)
                    if u == 0:
                        gla(3, 8 + t)
            for m in range(KT):
                product(UNIT[("wa", 0, 0)], m)
            for kind in ("wg", "wo"):
                for u in range(4):
                    for t in range(2):
                        product(UNIT[(kind, u, 0)], t)
            pe.wait_ge(sum_done, SUMS[2])
            pe.matmul(side[0][:, :], ones[:, :], sq_sum2[:, :], start=True, stop=False)
            for k in (KT - 2, KT - 1):
                pe.wait_ge(sq_done, KT + k + 1)
                last = pe.matmul(side[0][:, :], ones[:, :], sq2[:, k % 2, :], start=False, stop=(k == KT - 1))
            last.then_inc(ssq_ps, 1)

            def up_tile(s, t, k):
                slot, at = 1 - s, k * UW + t * P
                w = tuple(v[:, slot, at:at + P] for v in (w_hi, w_lo))
                return three(bank[2 * s + t][:, :], w, (h_hi[:, k, :], h_lo[:, k, :]), k == 0, k == KT - 1)

            def up(a, s, first=False):
                i = 2 * a + s
                for t in range(2):
                    if not first:
                        pe.wait_ge(tap_done, 4 * i + (2 * t - 6))
                    if t == 0:
                        pe.wait_ge(raw_used, i + (N_RAW + 1))
                    for k in range(KT):
                        last = up_tile(s, t, k)
                    last.then_inc(ffn_ready, 1)

            for t in range(2):
                last_in_bank = N_TILES - 1 - (N_TILES - 1 - t) % 2
                pe.wait_ge(acc_free[t], last_in_bank // 2 + 1)
            pe.wait_ge(raw_used, N_RAW + 1)
            for k in range(KT):
                pe.wait_ge(hl_done, KT + k + 1)
                for t in range(2):
                    last = up_tile(0, t, k)
                    if k == KT - 1:
                        last.then_inc(ffn_ready, 1)
            pe.wait_ge(rstd_done, 2)
            up(0, 1, first=True)
            with pe.Fori(1, FT // 2) as a:
                for s in range(2):
                    up(a, s)

            def down(a, s, first=False, final=False):
                j = 2 * a + s
                slot = 1 - s
                pe.wait_ge(raw_used, j + (N_RAW + FT + 1))
                pe.wait_ge(hs_lo_done, j + 1)
                for m in ((4, 5, 6, 7, 0, 1, 2, 3) if first else range(KT)):
                    if first and m < 4:
                        pe.wait_ge(tap_done, 4 * FT - 6 + 2 * m)
                    for k in range(2):
                        at = k * D + m * P
                        w = tuple(v[:, slot, at:at + P] for v in (w_hi, w_lo))
                        last = three(bank[m][:, :], w, (hs_hi[:, s, k, :], hs_lo[:, s, k, :]),
                                     first and k == 0, final and k == 1)
                    if final:
                        last.then_inc(down_tile, 1)
                        if m == KT - 2:
                            for i in range(NB):
                                to_tokens(i, range(4))
                if not final:
                    last.then_inc(down_done, 1)

            def to_tokens(i, parts):
                half, b = divmod(i, NB)
                for m in parts:
                    pe.wait_ge(xw_done, 4 * half + m + 1)
                    last = pe.transpose(bank[i][:, m * P:(m + 1) * P], x1[:, 4 * half + m, b * P:(b + 1) * P], ident)
                if m == 3:
                    last.then_inc(yt_ps, 1)

            down(0, 0, first=True)
            down(0, 1)
            with pe.Fori(1, DOWN_UNITS // 2) as a:
                for s in range(2):
                    down(a, s)
            down(DOWN_UNITS // 2, 0, final=True)
            for i in range(4, 7):
                to_tokens(i, range(3))
            pe.wait_ge(sum_done, SUMS[2] + KT)
            pe.wait_ge(x2_done, KT)
            for b in range(NB):
                last = pe.matmul(bank[7][:, b:b + 1], sq_sum2[:, b * P:(b + 1) * P], ones[:, 0:1],
                                 start=True, stop=True, skip_group_check=True)
            last.then_inc(ssq_ps, 1)
            for i in range(4, 7):
                to_tokens(i, range(3, 4))
            pe.wait_ge(ln_done, 3)
            to_tokens(7, range(4))


_INS = ["x", "c", "positions", "ada_w", "ada_b", "norm1_w", "w_in", "gla_gate_w2", "gla_gate_b", "gla_norm_w",
        "w_gla_branch", "w_attn_branch", "w_out", "norm2_w", "w_up", "conv_w", "conv_b", "w_down", "final_norm_w"]


def kernel(**inputs):
    import concourse.bacc as _bacc
    from concourse.bass_utils import run_bass_kernel_spmd as _run

    nc = _bacc.Bacc("TRN2", target_bir_lowering=False, num_devices=1)
    arrays, args = {}, []
    for name in _INS + ["shape_constants"]:
        a = np.ascontiguousarray(inputs[name]) if name in inputs else shape_constants()
        arrays[f"in_{name}_dram"] = a
        args.append(nc.dram_tensor(f"in_{name}_dram", a.shape, mybir.dt.from_np(a.dtype), kind="ExternalInput").ap())
    args.append(nc.dram_tensor("out_0_dram", (1, SEQ, D), F32, kind="ExternalOutput").ap())
    hybrid_block_kernel(nc, *args)
    r = _run(nc, [arrays], core_ids=[0])
    return r.results[0]["out_0_dram"]
```

```python
from contextlib import ExitStack

import numpy as np

import concourse.bass as bass
from concourse import mybir

F32 = mybir.dt.float32
F32R = mybir.dt.float32r
I32 = mybir.dt.int32
U32 = mybir.dt.uint32
ACT = mybir.ActivationFunctionType
ALU = mybir.AluOpType
AX = mybir.AxisListType

P = 128
SEQ = 512
D = 1024
KT = D // P
NB = SEQ // P
HEADS = 4
DV = 256
LOWRANK = 16
CHUNK = 16
NCH = P // CHUNK
DH = 64
GROUPS = 3
DIL = 4
D_FF = 2816
FT = D_FF // P
EPS = 1e-6
NEG = -3.0e38
ROUND = 1.5 * 2.0 ** 23
TWO_PI = (6.28125, 0.0019350051879882812, 3.0199159795074593e-07)

GLA_QK = HEADS * P
COL_GQ = 0
COL_GK = COL_GQ + GLA_QK
COL_GV = COL_GK + GLA_QK
COL_GR = COL_GV + HEADS * DV
COL_LR = COL_GR + HEADS * DV
COL_AQ = COL_LR + LOWRANK
COL_AK = COL_AQ + GROUPS * HEADS * DH
COL_AV = COL_AK + GROUPS * HEADS * DH
COL_MA = COL_AV + GROUPS * HEADS * DH
COL_MB = COL_MA + D
UW = 256
UE = KT * UW

C_ID = 0
C_TRI = C_ID + P
C_KEEP = C_TRI + P + NCH + 1
C_MSK = C_KEEP + P
C_MOD = C_MSK + 3 * P
C_FRQ = C_MOD + P
C_ALL = C_FRQ + 1

V_C, V_N1, V_N2, V_FN, V_GN, V_AB = 0, 8, 16, 24, 32, 34
ROWS_A = V_AB + 6 * KT
ROWS_B = 4 * FT
V_CW0 = ROWS_A
V_CW1 = V_CW0 + 2 * FT
V_CW2 = V_CW1 + 2 * FT
V_CB = V_CW2 + 2 * FT
V_ALL = V_CB + 2 * FT
HALVES = (slice(0, SEQ // 2), slice(SEQ // 2, SEQ))
LN_EXP = "natural_log_exp_and_others"


def shape_constants():
    c = np.zeros((P, C_ALL), np.float32)
    row, col = np.arange(P)[:, None], np.arange(P)[None, :]
    c[:, C_ID:C_ID + P] = row == col
    same = row // CHUNK == col // CHUNK
    c[:, C_TRI:C_TRI + P] = np.where(same & (row <= col), -1.0 / 16.0, 0.0)
    for n in range(NCH + 1):
        c[:, C_TRI + P + n] = np.where(row[:, 0] < CHUNK * n, -1.0 / 16.0, 0.0)
    c[:, C_KEEP:C_KEEP + P] = col >= row
    c[:, C_MSK:C_MSK + P] = np.where(col >= row, 0.0, NEG)
    c[:, C_MSK + P:C_MSK + 2 * P] = np.where(col <= row, 0.0, NEG)
    c[:, C_MSK + 2 * P:C_MSK + 3 * P] = np.where(col <= row, 0.0, NEG)
    c[:, C_MOD:C_MOD + P] = np.where((col <= row) & ((row - col) % 4 == 0), 0.0, NEG)
    half = DH // 2
    freq = np.float32(10000.0) ** (-np.arange(half, dtype=np.float32) / np.float32(half))
    c[:, C_FRQ] = np.tile(freq.astype(np.float32), P // half)
    return c


UNITS = ([("v", g, 0) for g in range(GROUPS)]
         + [("qk", p, g) for p in range(2) for g in range(GROUPS)]
         + [("lr", 0, 0)]
         + [(kind, h, 0) for h in range(HEADS) for kind in ("gqk", "gv", "gr")]
         + [("ma", u, 0) for u in range(4)]
         + [("mb", u, 0) for u in range(4)]
         + [("wa", 0, 0)]
         + [("wg", u, 0) for u in range(4)]
         + [("wo", u, 0) for u in range(4)])
N_UNITS = len(UNITS)
UNIT = {u: n for n, u in enumerate(UNITS)}


def tiles_of(unit):
    return {"lr": 1, "wa": 8}.get(unit[0], 2)


WITH_ADA = {(("qk", 1, 2), 1): 0, (("gr", 2, 0), 1): 1}
TILES = []
for _u in UNITS:
    for _t in range(tiles_of(_u)):
        if (_u, _t) in WITH_ADA:
            TILES += [("ada", WITH_ADA[_u, _t])]
        TILES += [(_u, _t)]
    if _u == ("gqk", 0, 0):
        TILES += [("z", b) for b in range(NB)]
TILE = {t: n for n, t in enumerate(TILES)}
N_TILES = len(TILES)

RAW = []
for _n in range(N_UNITS):
    RAW.append(("w", _n))
    if 1 <= _n <= 2 * KT:
        RAW.append(("ada", _n - 1))
RAW_AT = {r: q for q, r in enumerate(RAW)}
N_RAW = len(RAW)


def dmas_of(raw):
    return 2 if raw[0] == "w" and UNITS[raw[1]][0] in ("qk", "gqk") else 1


LANDED = []
_count = [0, 0]
for _q, _r in enumerate(RAW):
    _count[_q % 2] += 16 * dmas_of(_r)
    LANDED.append(_count[_q % 2])
LANDED_END = tuple(_count)
FIRST_FFN = N_RAW
DOWN_UNITS = FT // 2
SUMS = (0, KT - 1, 2 * KT - 2)


def hybrid_block_kernel(nc, x, c, positions, ada_w, ada_b, norm1_w, w_in, gate_w2, gate_b, gla_norm_w,
                        w_gla, w_attn, w_out, norm2_w, w_up, conv_w, conv_b, w_down, final_w, consts, out):
    assert N_UNITS % 2 == 1 and N_RAW % 2 == 1
    ctx = ExitStack()
    with ctx:
        def sb(name, shape, dt=F32):
            return ctx.enter_context(nc.sbuf_tensor(name, shape, dt))

        def sem(name):
            return ctx.enter_context(nc.semaphore(name))

        x_spill = nc.dram_tensor("x_spill", [P, KT * SEQ], F32, kind="Internal").ap()

        raw = sb("raw", [P, 2, UE])
        w_hi = sb("w_hi", [P, 2, UE], F32R)
        w_lo = sb("w_lo", [P, 2, UE], F32R)
        h_hi = sb("h_hi", [P, KT, SEQ], F32R)
        h_lo = sb("h_lo", [P, KT, SEQ], F32R)
        cst = sb("cst", [P, C_ALL])
        ones = sb("ones", [P, P])
        vecs = sb("vecs", [P, V_ALL])
        rows_a = sb("rows_a", [ROWS_A, P])
        rows_b = sb("rows_b", [ROWS_B, 2, P])
        c_silu = sb("c_silu", [P, KT])
        mod = sb("mod", [P, 6 * KT])
        gain = sb("gain", [P, 2, KT])
        ada_acc = sb("ada_acc", [P, 2 * D])

        def region(*places):
            got = []
            with ExitStack() as scope:
                at = 0
                for n, (name, kb, shape, dt) in enumerate(sorted(places, key=lambda p: p[1])):
                    off = int(kb * 1024)
                    assert off >= at, name
                    if off > at:
                        scope.enter_context(nc.sbuf_tensor(f"gap_{name}", [P, (off - at) // 4], F32))
                    got.append(scope.enter_context(nc.sbuf_tensor(name, shape, dt)))
                    size = 4
                    for s in shape[1:]:
                        size *= s
                    at = off + (size + 31) // 32 * 32
            order = sorted(range(len(places)), key=lambda i: places[i][1])
            back = [None] * len(places)
            for i, t in zip(order, got):
                back[i] = t
            return back

        ada_in, x_tok, xT0, sq, sq_sum, rstd, ntmp, ada_in7, cs = region(
            ("ada_in", 0, [P, 7, KT // 2, 2, 2 * P], F32), ("x_tok", 56, [P, NB, D], F32), ("xT0", 72, [P, KT, SEQ], F32),
            ("sq", 88, [P, 2, SEQ], F32), ("sq_sum", 92, [P, SEQ], F32), ("rstd", 94, [P, SEQ], F32),
            ("ntmp", 96, [P, 2, SEQ], F32), ("ada_in7", 100, [P, KT // 2, 2, 2 * P], F32), ("cs", 108, [P, 2, SEQ], F32))
        xn = x_tok[:, :, :].rearrange("p b (t n) -> p (b t) n", n=SEQ)
        qk, rope, oa_hi, oa_lo, ocomb, osum, orec, oa32, rope_t, v_ext, S, PT, mx, mg, rowm, negm = region(
            ("qk", 0, [DH, GROUPS, 2, 2, SEQ], F32), ("rope", 24, [P, 2, 2, SEQ], F32),
            ("oa_hi", 32, [P, 2, SEQ], F32R), ("oa_lo", 36, [P, 2, SEQ], F32R),
            ("ocomb", 40, [P, SEQ], F32), ("osum", 42, [P, SEQ], F32), ("orec", 44, [P, SEQ], F32),
            ("oa32", 46, [P, SEQ], F32), ("rope_t", 48, [P, 2, SEQ], F32),
            ("v_ext", 56, [P, NB, GROUPS, HEADS, P], F32), ("S", 80, [P, 2, 1920], F32),
            ("PT", 95, [P, 1920], F32), ("mx", 102.5, [P, 8, 2], F32), ("mg", 102.75, [P, 2, 4], F32),
            ("rowm", 103, [2, 2, SEQ], F32), ("negm", 107, [P, 8, 2], F32))
        q_in, k_in, gv, gr, logs, za, lrT, w2b, og_hi, og_lo, kk, at_sb, kt_sb, ke, state, eb, enb, ed, qB, o_sb, osq, ors = region(
            ("q_in", 0, [P, 2, SEQ], F32), ("k_in", 4, [P, 2, SEQ], F32), ("gv_sb", 8, [P, 2, NB, DV], F32),
            ("gr_sb", 16, [P, 2, 2, SEQ], F32), ("logs", 24, [P, NB, SEQ], F32),
            ("za", 48, [P, 2, SEQ], F32), ("lrT", 52, [32, SEQ], F32), ("w2b", 54, [LOWRANK + 1, SEQ], F32),
            ("og_hi", 56, [P, KT, SEQ], F32R), ("og_lo", 72, [P, KT, SEQ], F32R),
            ("kk", 88, [P, NCH, P], F32), ("at_sb", 92, [P, 2, P], F32), ("kt_sb", 93, [P, 2, P], F32),
            ("ke", 94, [P, P], F32), ("state", 94.5, [P, DV], F32), ("eb", 95.5, [P, SEQ], F32),
            ("enb", 97.5, [P, SEQ], F32), ("ed", 99.5, [P, NB, NCH + 1], F32), ("qB", 99.75, [P, SEQ], F32),
            ("o_sb", 101.75, [P, 2, SEQ], F32), ("osq", 105.75, [P, 2, SEQ], F32), ("ors", 109.75, [P, SEQ], F32))
        z_abs_sb = [za[:, 0, :], za[:, 1, :], cs[:, 0, :], cs[:, 1, :]]
        mix_hi, mix_lo, sA, sB, mtmp = region(
            ("mix_hi", 0, [P, KT, SEQ], F32R), ("mix_lo", 16, [P, KT, SEQ], F32R),
            ("sA", 40, [P, KT, SEQ], F32), ("sB", 88, [P, KT, SEQ], F32), ("mtmp", 104, [P, 2, SEQ], F32))
        hid, x1, conv, sq2, sq_sum2, rstd2, ntmp2, hs_hi, hs_lo = region(
            ("hid", 0, [P, FT, SEQ], F32), ("x1", 56, [P, KT, SEQ], F32), ("conv", 72, [P, 2, 2, SEQ], F32),
            ("sq2", 80, [P, 2, SEQ], F32), ("sq_sum2", 84, [P, SEQ], F32), ("rstd2", 86, [P, SEQ], F32),
            ("ntmp2", 88, [P, 2, SEQ], F32),
            ("hs_hi", 92, [P, 2, 2, SEQ], F32R), ("hs_lo", 100, [P, 2, 2, SEQ], F32R))
        y_tok, = region(("y_tok", 0, [P, NB, D], F32))
        rstd_tok = rstd2[:, 0:NB]
        angles = ada_in[:, 1].rearrange("p k s n -> p (k s n)")
        pos_i = angles[:, 0:SEQ].bitcast(I32)
        ang, turns, ang_abs = (angles[:, i * SEQ:(i + 1) * SEQ] for i in range(1, 4))

        bank = [ctx.enter_context(nc.psum_tensor(f"bank{i}", [P, SEQ], F32)) for i in range(8)]
        side = bank[2:]

        landed = [sem(f"raw_landed{i}") for i in range(2)]
        raw_used = sem("raw_used")
        hi_done = sem("hi_done")
        acc_ready = sem("acc_ready")
        acc_free = [sem(f"acc_free{i}") for i in range(2)]
        rows_in, conv_in, cst_in, x_in, pos_in = (sem(n) for n in ("rows_in", "conv_in", "cst_in", "x_in", "pos_in"))
        ada_landed = [sem(f"ada_landed{i}") for i in range(KT)]
        w2_in = sem("w2_in")
        ones_set = sem("ones_set")
        vec_ps, vec_sb, silu_done = sem("vec_ps"), sem("vec_sb"), sem("silu_done")
        xt_ps, xt_sb, spilled, x_back = sem("xt_ps"), sem("xt_sb"), sem("spilled"), sem("x_back")
        ada_init_act, ada_init_dve, ada_step = sem("ada_init_act"), sem("ada_init_dve"), sem("ada_step")
        ada_sum, ident_in = sem("ada_sum"), sem("ident_in")
        mod1_ps, mod_done, gain_done = sem("mod1_ps"), sem("mod_done"), sem("gain_done")
        sq_done, sum_done, ssq_ps, ln_done, rstd_done = (sem(n) for n in (
            "sq_done", "sum_done", "ssq_ps", "ln_done", "rstd_done"))
        xn_done, nt_done, hh_done = (sem(n) for n in ("xn_done", "nt_done", "hh_done"))
        hl_pool, hl_done = sem("hl_pool"), sem("hl_done")
        rot_dve, rot_sum, rot_act = sem("rot_dve"), sem("rot_sum"), sem("rot_act")
        v_ones = sem("v_ones")
        rope_sum, qk_in = sem("rope_sum"), [sem(f"qk_in{i}") for i in range(2)]
        sc_done, msk_done, mx1_done, mx_done = sem("sc_done"), sem("msk_done"), sem("mx1_done"), sem("mx_done")
        mxr_ps, rowmax_done, mxc_ps, negm_done = (sem(n) for n in ("mxr_ps", "rowmax_done", "mxc_ps", "negm_done"))
        exp_done, tr_ps, pt_act, pt_dve, pv_done = (sem(n) for n in ("exp_done", "tr_ps", "pt_act", "pt_dve", "pv_done"))
        perm_sb, osum_done, oln_done, orec_done, oa32_done, oahi_done, oalo_done = (sem(n) for n in (
            "perm_sb", "osum_done", "oln_done", "orec_done", "oa32_done", "oahi_done", "oalo_done"))
        lr_ones, z_abs, z_exp, z_ln, logs_done = (sem(n) for n in (
            "lr_ones", "z_abs", "z_exp", "z_ln", "logs_done"))
        b_ps, gexp_done, qg_done, qB_done, kk_step, kk_done = (sem(n) for n in (
            "b_ps", "gexp_done", "qg_done", "qB_done", "kk_step", "kk_done"))
        at_zero, at_ps, at_done, kt_done, p3_done, st_done = (sem(n) for n in (
            "at_zero", "at_ps", "at_done", "kt_done", "p3_done", "st_done"))
        o_done, osq_done, osum2_done, gssq_ps, gln_done, grstd_done, on_done, og32_done, oghi_done, oglo_done = (
            sem(n) for n in ("o_done", "osq_done", "osqsum_done", "gssq_ps", "gln_done", "grstd_done", "on_done",
                             "og32_done", "oghi_done", "oglo_done"))
        mix32_done, mixhi_done, mixlo_done = sem("mix32_done"), sem("mixhi_done"), sem("mixlo_done")
        ffn_ready, tap2_done, tap_done, gelu_done, hid_done = (sem(n) for n in (
            "ffn_ready", "tap2_done", "tap_done", "gelu_done", "hid_done"))
        hs_hi_done, hs_lo_done, down_done, down_tile = (sem(n) for n in (
            "hs_hi_done", "hs_lo_done", "down_done", "down_tile"))
        x2_done, xw_done, yt_ps, yt_act, yt_dve, stored = (sem(n) for n in (
            "x2_done", "xw_done", "yt_ps", "yt_act", "yt_dve", "stored"))

        x1_half, sq_half, ssq_half, ln_half, rstd_half = (sem(n) for n in (
            "x1_half", "sq_half", "ssq_half", "ln_half", "rstd_half"))

        block = ctx.enter_context(nc.Block())

        def ada_first(j, half):
            return ada_in[:, 2 * j + half] if 2 * j + half < 7 else ada_in7

        def ada_rows(j, k):
            half, row = divmod(k, KT // 2)
            return ada_first(j, half)[:, row].rearrange("p s n -> p (s n)")

        def last_tile(n):
            return TILE[(UNITS[n], tiles_of(UNITS[n]) - 1)]

        def views(n):
            rs, ws = RAW_AT[("w", n)] % 2, n % 2
            kind = UNITS[n][0]
            if kind == "qk":
                r = raw[:, rs, :].rearrange("p (k a t f) -> p t k a f", k=KT, a=4, t=2)
                hv = w_hi[:, ws, :].rearrange("p (k t a f) -> p t k a f", k=KT, t=2, a=4)
                lv = w_lo[:, ws, :].rearrange("p (k t a f) -> p t k a f", k=KT, t=2, a=4)
                return [(r[:, t], hv[:, t], lv[:, t]) for t in range(2)]
            size = KT * LOWRANK if kind == "lr" else UE
            return [(raw[:, rs, 0:size], w_hi[:, ws, 0:size], w_lo[:, ws, 0:size])]

        def evacuated(eng, tile):
            i = TILE[tile]
            eng.wait_ge(acc_free[i % 2], i // 2 + 1)

        BANK_AT = [0, 512, 896, 1408]
        BANK_W = [512, 384, 512, 512]

        def score_blocks(bk):
            if bk == 0:
                return [(0, 2 * P, 1), (2 * P, 2 * P, 2)]
            if bk == 1:
                return [(0, 2 * P, 3), (2 * P, P, 0)]
            return [(r * P, P, NB + r) for r in range(DIL)]

        @block.sync
        def _(sp):
            sp.dma_start(rows_a[V_C:V_C + KT, :], c.rearrange("a (k p) -> (a k) p", p=P)).then_inc(rows_in, 16)
            sp.dma_start(rows_a[V_N1:V_N1 + KT, :], norm1_w.rearrange("a (k p) -> (a k) p", p=P)).then_inc(rows_in, 16)
            sp.dma_start(rows_a[V_AB:ROWS_A, :], ada_b.rearrange("a (k p) -> (a k) p", p=P)).then_inc(rows_in, 16)
            sp.dma_start(rows_a[V_N2:V_N2 + KT, :], norm2_w.rearrange("a (k p) -> (a k) p", p=P)).then_inc(rows_in, 16)
            sp.dma_start(rows_a[V_FN:V_FN + KT, :], final_w.rearrange("(k p) -> k p", p=P)).then_inc(rows_in, 16)
            sp.dma_start(rows_a[V_GN:V_GN + 2, :], gla_norm_w.rearrange("a (k p) -> (a k) p", p=P)).then_inc(rows_in, 16)
            ada_v = ada_w.rearrange("a (k p) n -> (a k) p n", p=P)
            ada_t = ada_w.rearrange("a (k p) (s n) -> p (a k) s n", p=P, n=D)

            def load_first(j):
                for half in range(2):
                    rows = slice(half * KT // 2, (half + 1) * KT // 2)
                    for s_ in range(2):
                        sp.dma_start(ada_first(j, half)[:, :, s_, :],
                                     ada_t[:, rows, s_, 2 * j * P:2 * (j + 1) * P]).then_inc(ada_landed[2 * j + half], 16)

            w_in_v = w_in.rearrange("a (k p) n -> p (a k) n", p=P)

            def cols(view, at, width=UW):
                return view[:, :, at:at + width]

            wg_v = w_gla.rearrange("a (k p) n -> p (a k) n", p=P)
            wo_v = w_out.rearrange("a (k p) n -> p (a k) n", p=P)
            wa_v = w_attn.rearrange("a (k p) n -> p (a k) n", p=P)

            def load(q):
                what, n = RAW[q]
                slot = q % 2
                done = landed[slot]
                if q >= 2:
                    sp.wait_ge(raw_used, q - 1)
                if what == "ada":
                    r, k = n // KT, n % KT
                    sp.dma_start(raw[:, slot, :], ada_v[k, :, 2 * D * (r + 1):2 * D * (r + 2)]).then_inc(done, 16)
                    return
                kind, a, b = UNITS[n]
                dst = raw[:, slot, :].rearrange("p (k n) -> p k n", k=KT)
                if kind == "qk":
                    off = b * HEADS * DH + a * 2 * DH
                    sp.dma_start(dst[:, :, 0:P], cols(w_in_v, COL_AQ + off, P)).then_inc(done, 16)
                    sp.dma_start(dst[:, :, P:UW], cols(w_in_v, COL_AK + off, P)).then_inc(done, 16)
                elif kind == "gqk":
                    sp.dma_start(dst[:, :, 0:P], cols(w_in_v, COL_GQ + a * P, P)).then_inc(done, 16)
                    sp.dma_start(dst[:, :, P:UW], cols(w_in_v, COL_GK + a * P, P)).then_inc(done, 16)
                elif kind == "lr":
                    small = raw[:, slot, 0:KT * LOWRANK].rearrange("p (k n) -> p k n", k=KT)
                    sp.dma_start(small, cols(w_in_v, COL_LR, LOWRANK)).then_inc(done, 16)
                elif kind == "wa":
                    sp.dma_start(raw[:, slot, :].rearrange("p (k n) -> p k n", k=2), wa_v).then_inc(done, 16)
                else:
                    src = {"v": cols(w_in_v, COL_AV + a * UW), "gv": cols(w_in_v, COL_GV + a * DV),
                           "gr": cols(w_in_v, COL_GR + a * DV), "ma": cols(w_in_v, COL_MA + a * UW),
                           "mb": cols(w_in_v, COL_MB + a * UW),
                           "wg": wg_v[:, :, (a % 4) * UW:(a % 4 + 1) * UW],
                           "wo": wo_v[:, :, (a % 4) * UW:(a % 4 + 1) * UW]}[kind]
                    sp.dma_start(dst, src).then_inc(done, 16)

            def shuffle(j):
                p, g = divmod(j, GROUPS)
                sp.wait_ge(rope_sum, 2 * j + 2)
                if j == GROUPS:
                    sp.wait_ge(sc_done, 8)
                for half in range(2):
                    for a in range(4):
                        sp.dma_start(qk[32 * half:32 * half + 32, g, a // 2, a % 2, :],
                                     rope[32 * a:32 * a + 32, j % 2, half, :]).then_inc(qk_in[j % 2], 16)

            for j in range(KT // 2):
                if j == 1:
                    load(0)
                load_first(j)
            sp.wait_ge(mod1_ps, 1)
            sp.dma_start(pos_i, positions.broadcast_to((P, SEQ))).then_inc(pos_in, 16)
            sp.dma_start(cst[:, C_TRI:C_ALL], consts[:, C_TRI:C_ALL]).then_inc(cst_in, 16)
            for q in range(N_RAW):
                what, n = RAW[q]
                if what == "w" and 6 <= n < 12:
                    shuffle(n - 6)
                if q > 0:
                    load(q)
                if q == 1:
                    sp.dma_start(rows_b[:, 0, :], conv_w[0, 0:2, :].rearrange("i (k p) -> (i k) p", p=P)).then_inc(conv_in, 16)
                    sp.dma_start(rows_b[0:2 * FT, 1, :], conv_w[0, 2:3, :].rearrange("i (k p) -> (i k) p", p=P)).then_inc(conv_in, 16)
                    sp.dma_start(rows_b[2 * FT:ROWS_B, 1, :], conv_b.rearrange("i (k p) -> (i k) p", p=P)).then_inc(conv_in, 16)
                    sp.wait_ge(xt_sb, KT)
                    sp.dma_start(x_spill, xT0[:, :, :].rearrange("p k n -> p (k n)")).then_inc(spilled, 16)
                if q == 2:
                    sp.wait_ge(mod1_ps, KT // 2)
                    sp.dma_start(w2b[0:LOWRANK, :], gate_w2.rearrange("a r n -> (a r) n")).then_inc(w2_in, 16)
                    sp.dma_start(w2b[LOWRANK:LOWRANK + 1, :], gate_b).then_inc(w2_in, 16)
                if what == "w" and n == UNIT[("wo", 0, 0)]:
                    sp.wait_ge(spilled, 16)
                if what == "w" and n == UNIT[("wo", 1, 0)]:
                    sp.wait_ge(acc_ready, last_tile(UNIT[("wg", 3, 0)]) + 1)
                    sp.dma_start(x1[:, :, :].rearrange("p k n -> p (k n)"), x_spill).then_inc(x_back, 16)

            up_v = w_up.rearrange("a (k p) n -> p (a k) n", p=P)

            def load_up(i, s):
                slot = (s + 1) % 2
                dst = raw[:, slot, :].rearrange("p (k t n) -> p k t n", k=KT, t=2)
                sp.wait_ge(raw_used, i + (FIRST_FFN - 1))
                for t in range(2):
                    sp.dma_start(dst[:, :, t, :], up_v[:, :, bass.ds(i * P + t * D_FF, P)]).then_inc(landed[slot], 16)

            with sp.Fori(0, FT // 2) as a:
                for s in range(2):
                    load_up(2 * a + s, s)

            down_v = w_down.rearrange("a (k p) n -> p (a k) n", p=P)

            def load_down(j, s):
                slot = (s + 1) % 2
                sp.wait_ge(raw_used, j + (FIRST_FFN + FT - 1))
                for t in range(2):
                    sp.dma_start(raw[:, slot, t * D:(t + 1) * D].rearrange("p (k n) -> p k n", k=1),
                                 down_v[:, bass.ds(2 * j + t, 1), :]).then_inc(landed[slot], 16)

            with sp.Fori(0, DOWN_UNITS // 2) as a:
                for s in range(2):
                    load_down(2 * a + s, s)
            load_down(DOWN_UNITS - 1, 0)

            out_v = out.rearrange("a (b p) n -> p (a b) n", p=P)
            for i in range(8):
                half, b = divmod(i, NB)
                sp.wait_ge(yt_act if i % 2 == 0 else yt_dve, i // 2 + 1)
                sp.dma_start(out_v[:, b, half * SEQ:(half + 1) * SEQ], y_tok[:, b, half * SEQ:(half + 1) * SEQ]).then_inc(stored, 16)
            sp.wait_ge(stored, 8 * 16)

        @block.gpsimd
        def _(pool):
            pool.memset(ones[:, :], 1.0).then_inc(ones_set, 1)

            def sum_squares(part, sq_t, sum_t, tiles):
                for k in range(tiles):
                    i = SUMS[part] + k
                    pool.wait_ge(sq_done, part * KT + k + 1)
                    if k == 0 and part > 0:
                        pool.wait_ge(ssq_ps, part)
                    if k > 0:
                        pool.wait_ge(sum_done, i)
                    if k == 0:
                        pool.tensor_copy(sum_t[:, :], sq_t[:, k % 2, :]).then_inc(sum_done, 1)
                    else:
                        pool.tensor_tensor(sum_t[:, :], sum_t[:, :], sq_t[:, k % 2, :], ALU.add).then_inc(sum_done, 1)

            sum_squares(0, sq, sq_sum, KT - 1)
            pool.wait_ge(rstd_done, 1)
            pool.wait_ge(xt_sb, KT)
            for k in range(KT):
                pool.tensor_tensor(xn[:, k, :], xT0[:, k, :], rstd[:, :], ALU.mult).then_inc(xn_done, 1)
                if 1 <= k <= KT // 2:
                    pool.wait_ge(nt_done, k)
                    pool.wait_ge(hh_done, k)
                    pool.tensor_tensor(h_lo[:, k - 1, :], ntmp[:, (k - 1) % 2, :], h_hi[:, k - 1, :].bitcast(F32),
                                       ALU.subtract).then_inc(hl_pool, 1)
            pool.wait_ge(xt_ps, KT)
            pool.wait_ge(hl_done, KT // 2)
            pool.wait_ge(spilled, 16)
            for hd in range(2):
                part = v_ext[:, :, :, hd::2, (1 - hd) * DH:(2 - hd) * DH]
                pool.memset(part.rearrange("p b g h n -> p (b g) h n"), 1.0).then_inc(v_ones, 1)
            for j in range(2 * GROUPS):
                for t in range(2):
                    evacuated(pool, (("qk", *divmod(j, GROUPS)), t))
                for half, op in ((0, ALU.subtract), (1, ALU.add)):
                    dst = rope[:, j % 2, half, :]
                    pool.tensor_tensor(dst, dst, rope_t[:, half, :], op).then_inc(rope_sum, 1)
            pool.memset(lrT[:, :], 1.0).then_inc(lr_ones, 1)
            for h in range(HEADS):
                pool.wait_ge(osq_done, h + 1)
                pool.tensor_tensor(osq[:, 0, :], osq[:, 0, :], osq[:, 1, :], ALU.add).then_inc(osum2_done, 1)
            for m in range(KT):
                evacuated(pool, (("wg", m // 2, 0), m % 2))
                pool.tensor_tensor(sB[:, m, :], sB[:, m, :], mtmp[:, m % 2, :], ALU.add).then_inc(mix32_done, 1)
            sum_squares(1, sq2, sq_sum2, KT - 1)
            pool.wait_ge(raw_used, N_RAW + 1)
            pool.wait_ge(hi_done, N_UNITS + 2)
            pool.tensor_tensor(w_lo[:, 0, :], raw[:, 0, :], w_hi[:, 0, :].bitcast(F32), ALU.subtract).then_inc(raw_used, 1)
            sum_squares(2, sq2, sq_sum2, KT - 1)

        @block.scalar
        def _(act):
            act.dma_start(cst[:, 0:C_TRI], consts[:, 0:C_TRI]).then_inc(ident_in, 16)
            x_v = x.rearrange("a (b p) n -> p (a b) n", p=P)
            for b in range(NB):
                act.dma_start(x_tok[:, b, :], x_v[:, b, :]).then_inc(x_in, 16)

            def split_hi(n):
                if n == N_UNITS:
                    return split_hi_ffn(0, 0, acc_ready, last_tile(n - 2) + 1)
                q = RAW_AT[("w", n)]
                act.wait_ge(landed[q % 2], LANDED[q])
                if n >= 2:
                    act.wait_ge(acc_ready, last_tile(n - 2) + 1)
                for r, hv, _ in views(n):
                    last = act.activation(hv, r, ACT.Copy)
                last.then_inc(hi_done, 1)

            def split_hi_ffn(pair, odd, used, value):
                slot = 1 - odd
                act.wait_ge(landed[slot], pair * 32 + (LANDED_END[slot] + 32))
                act.wait_ge(used, value)
                act.activation(w_hi[:, slot, :], raw[:, slot, :], ACT.Copy).then_inc(hi_done, 1)

            def square(part, k, sq_t, src):
                if k >= 2:
                    act.wait_ge(sum_done, SUMS[part] + k - 1)
                if k < 2 and part > 1:
                    act.wait_ge(ssq_ps, part)
                act.activation(sq_t[:, k % 2, :], src, ACT.Square).then_inc(sq_done, 1)

            def inverse_root(part, dst, src):
                act.wait_ge(ssq_ps, part + 1)
                act.activation(dst, src, ACT.Ln, scale=1.0 / D, bias=EPS).then_inc(ln_done, 1)
                act.wait_ge(ln_done, part + 1)
                act.activation(dst, dst, ACT.Exp, scale=-0.5).then_inc(rstd_done, 1)

            def modulated(k):
                act.wait_ge(gain_done, k // 2 + 1)
                act.wait_ge(xn_done, k + 1)
                if 2 <= k < KT // 2 + 2:
                    act.wait_ge(hl_pool, k - 1)
                elif k >= 2:
                    act.wait_ge(hl_done, k - KT // 2 - 1)
                for dst, done in ((h_hi[:, k, :], hh_done), (ntmp[:, k % 2, :], nt_done)):
                    act.activation(dst, xn[:, k, :], ACT.Identity, scale=gain[:, 0, k:k + 1],
                                   bias=mod[:, k:k + 1]).then_inc(done, 1)

            act.wait_ge(vec_sb, 1)
            act.activation(c_silu[:, :], vecs[:, V_C:V_C + KT], ACT.Silu).then_inc(silu_done, 1)

            def ada_first_rows(j):
                act.wait_ge(silu_done, 1)
                act.wait_ge(ada_landed[2 * j], 32)
                for k in range(2):
                    act.activation(ada_rows(j, k), ada_rows(j, k), ACT.Copy, scale=c_silu[:, k:k + 1]).then_inc(ada_init_act, 1)

            for k in range(KT):
                act.wait_ge(xt_ps, k + 1)
                square(0, k, sq, bank[3 + k % 4][:, :])
                act.activation(xT0[:, k, :], bank[3 + k % 4][:, :], ACT.Copy).then_inc(xt_sb, 1)
            act.preload_act_table_set(LN_EXP)
            split_hi(0)
            inverse_root(0, rstd[:, :], bank[0][:, :])
            for k in range(KT):
                if k == 0:
                    ada_first_rows(2)
                modulated(k)
                if k == 5:
                    split_hi(1)

            def acc(tile):
                i = TILE[tile]
                act.wait_ge(acc_ready, i + 1)
                return bank[i % 2]

            def free(tile, ins):
                ins.then_inc(acc_free[TILE[tile] % 2], 1)

            def exps(hh):
                p, hd = divmod(hh, 2)
                act.wait_ge(negm_done, p + 1)
                for bk in range(4):
                    for col, width, i in score_blocks(bk):
                        at = BANK_AT[bk] + col
                        last = act.activation(S[:, hd, at:at + width], S[:, hd, at:at + width], ACT.Exp,
                                              bias=negm[:, i, hd:hd + 1], scale=DH ** -0.5)
                    last.then_inc(exp_done, 1)

            def attention(p, i):
                if i in (4, 5):
                    hh = 2 * p + i - 4
                    for bk in range(2):
                        act.wait_ge(tr_ps, 4 * hh + bk + 1)
                        if hh >= 1:
                            act.wait_ge(pv_done, hh)
                        at = BANK_AT[bk]
                        act.activation(PT[:, at:at + BANK_W[bk]], side[bk][:, 0:BANK_W[bk]],
                                       ACT.Copy).then_inc(pt_act, 1)
                if i in (3, 4):
                    exps(2 * p + i - 3)
                if i in (5, 6):
                    hh = 2 * p + i - 5
                    act.wait_ge(pv_done, hh + 1)
                    if hh >= 1:
                        act.wait_ge(orec_done, hh)
                    act.activation(ocomb[:, :].rearrange("p (l r) -> p r l", r=DIL),
                                   side[5][:, :].rearrange("p (r l) -> p r l", r=DIL),
                                   ACT.Copy).then_inc(perm_sb, 1)
                    num, den = (slice(0, DH), slice(DH, P)) if hh % 2 == 0 else (slice(DH, P), slice(0, DH))
                    act.wait_ge(osum_done, hh + 1)
                    if hh > 0:
                        act.wait_ge(oa32_done, hh)
                    act.activation(ocomb[den, :], osum[den, :], ACT.Ln).then_inc(oln_done, 1)
                    act.wait_ge(oln_done, hh + 1)
                    act.activation(orec[num, :], ocomb[den, :], ACT.Exp, scale=-1.0).then_inc(orec_done, 1)
                if i == 6:
                    act.wait_ge(oa32_done, 2 * p + 2)
                    act.activation(oa_hi[:, p, :], oa32[:, :], ACT.Copy).then_inc(oahi_done, 1)

            def gates():
                evacuated(act, (("qk", 1, GROUPS - 1), 1))
                for b in range(NB):
                    z = acc(("z", b))
                    act.activation(z_abs_sb[b], z[:, :], ACT.Abs).then_inc(z_abs, 1)
                    free(("z", b), act.activation(logs[:, b, :], z[:, :], ACT.Relu, scale=-1.0))
                for b in range(NB):
                    act.wait_ge(z_abs, b + 1)
                    act.activation(z_abs_sb[b], z_abs_sb[b], ACT.Exp, scale=-1.0).then_inc(z_exp, 1)
                for b in range(NB):
                    act.wait_ge(z_exp, b + 1)
                    act.activation(z_abs_sb[b], z_abs_sb[b], ACT.Ln, bias=1.0).then_inc(z_ln, 1)

            def gla(h, i):
                if i == 0:
                    act.wait_ge(b_ps, h + 1)
                    if h > 0:
                        act.wait_ge(kk_done, NB * h)
                        act.wait_ge(st_done, 3 * h)
                    act.activation(eb[:, :], side[0][:, :], ACT.Exp).then_inc(gexp_done, 1)
                    act.activation(enb[:, :], side[0][:, :], ACT.Exp, scale=-1.0).then_inc(gexp_done, 1)
                    act.activation(ed[:, :, :].rearrange("p b n -> p (b n)"), side[1][:, 0:NB * (NCH + 1)],
                                   ACT.Exp).then_inc(gexp_done, 1)
                if 2 <= i <= 5:
                    u = NB * h + i - 2
                    act.wait_ge(at_ps, u + 1)
                    if u >= 2:
                        act.wait_ge(p3_done, u - 1)
                    act.activation(kt_sb[:, u % 2, :], side[3][:, 0:P], ACT.Copy).then_inc(kt_done, 1)
                if i == 6:
                    act.wait_ge(o_done, 2 * h + 2)
                    if h > 0:
                        act.wait_ge(gssq_ps, h)
                    act.activation(osq[:, :, :], o_sb[:, :, :], ACT.Square).then_inc(osq_done, 1)
                if i == 8:
                    act.wait_ge(gssq_ps, h + 1)
                    if h > 0:
                        act.wait_ge(on_done, h)
                    act.activation(ors[:, :], side[0][:, :], ACT.Ln, scale=1.0 / DV, bias=EPS).then_inc(gln_done, 1)
                    act.wait_ge(gln_done, h + 1)
                    act.activation(ors[:, :], ors[:, :], ACT.Exp, scale=-0.5).then_inc(grstd_done, 1)
                if i == 9:
                    act.wait_ge(og32_done, 2 * h + 2)
                    act.activation(og_hi[:, 2 * h:2 * h + 2, :], o_sb[:, :, :], ACT.Copy).then_inc(oghi_done, 1)

            def evac(n, t):
                kind, a, _ = UNITS[n]
                tile = (UNITS[n], t)
                src = acc(tile)
                if kind == "v":
                    act.wait_ge(spilled, 16)
                    act.wait_ge(nt_done, KT)
                    act.wait_ge(hh_done, KT)
                    v = src[:, :].rearrange("p (b h n) -> p b h n", b=2, h=HEADS)
                    for hd in range(2):
                        last = act.activation(v_ext[:, 2 * t:2 * t + 2, a, hd::2, hd * DH:(hd + 1) * DH],
                                              v[:, :, hd::2, :], ACT.Copy)
                    free(tile, last)
                if kind == "lr":
                    act.wait_ge(lr_ones, 1)
                    free(tile, act.activation(lrT[0:LOWRANK, :], src[0:LOWRANK, :], ACT.Copy))
                if kind == "gqk":
                    if a < 2:
                        act.wait_ge(sc_done, 16)
                    else:
                        act.wait_ge(p3_done, NB * (a - 1))
                    dst, scale = ((q_in, float(P) ** -0.5), (k_in, 1.0))[t]
                    free(tile, act.activation(dst[:, a % 2, :], src[:, :], ACT.Copy, scale=scale))
                if kind == "gv":
                    if a >= 2:
                        act.wait_ge(p3_done, NB * (a - 1))
                    free(tile, act.activation(gv[:, a % 2, 2 * t:2 * t + 2, :].rearrange("p b n -> p (b n)"),
                                              src[:, :], ACT.Copy))
                if kind == "gr":
                    if a >= 2:
                        act.wait_ge(og32_done, 2 * (a - 1))
                    free(tile, act.activation(gr[:, a % 2, t, :], src[:, :], ACT.Silu))
                    act.preload_act_table_set(LN_EXP)
                if kind == "ma":
                    if a == 0 and t == 0:
                        act.wait_ge(oalo_done, 2)
                        act.wait_ge(logs_done, NB)
                    free(tile, act.activation(sA[:, 2 * a + t, :], src[:, :], ACT.Sigmoid))
                if kind == "mb":
                    if a == 0 and t == 0:
                        act.wait_ge(p3_done, NB * HEADS)
                        act.wait_ge(st_done, 3 * HEADS)
                        act.wait_ge(o_done, 2 * HEADS)
                    if a == 3 and t == 0:
                        act.wait_ge(oglo_done, HEADS)
                    free(tile, act.activation(sB[:, 2 * a + t, :], src[:, :], ACT.Sigmoid))

            for g in range(GROUPS):
                n = UNIT[("v", g, 0)]
                if g > 0:
                    split_hi(n + 1)
                for t in range(2):
                    evac(n, t)
                if g == 1:
                    act.wait_ge(rot_dve, 7)
                    act.activation(cs[:, 1, :], ang, ACT.Sin).then_inc(rot_act, 1)
                    act.activation(ang_abs, ang, ACT.Abs).then_inc(rot_act, 1)
                    act.wait_ge(rot_act, 2)
                    act.activation(cs[:, 0, :], ang_abs, ACT.Sin, scale=-1.0, bias=float(np.pi / 2)).then_inc(rot_act, 1)
                    act.preload_act_table_set(LN_EXP)
            for g in range(GROUPS):
                split_hi(UNIT[("qk", 0, g)] + 1)
            for g in range(GROUPS):
                split_hi(UNIT[("qk", 1, g)] + 1)
                for i in (2 * g - 1, 2 * g):
                    if i >= 0:
                        attention(0, i)
            split_hi(UNIT[("lr", 0, 0)] + 1)
            evac(UNIT[("lr", 0, 0)], 0)
            attention(0, 5)
            for h in range(HEADS):
                for u, kind in enumerate(("gqk", "gv", "gr")):
                    n = UNIT[(kind, h, 0)]
                    split_hi(n + 1)
                    for t in range(2):
                        i = 2 * u + t
                        if h == 0 and i == 0:
                            attention(0, 6)
                        evac(n, t)
                        if h == 0:
                            attention(1, i)
                        if h == 1 and i == 0:
                            attention(1, 6)
                        if h >= 2 and i in (0, 2, 3):
                            gla(h - 2, 6 + i)
                        if h >= 1:
                            gla(h - 1, i)
                    if h == 0 and kind == "gqk":
                        gates()
            for u in range(4):
                n = UNIT[("ma", u, 0)]
                split_hi(n + 1)
                for t in range(2):
                    i = 2 * u + t
                    evac(n, t)
                    if i in (0, 2, 3):
                        gla(2, 6 + i)
                    gla(3, i)
            for u in range(4):
                n = UNIT[("mb", u, 0)]
                split_hi(n + 1)
                for t in range(2):
                    if u == 0:
                        gla(3, 8 + t)
                    evac(n, t)
            split_hi(UNIT[("wa", 0, 0)] + 1)
            for u in range(4):
                split_hi(UNIT[("wg", u, 0)] + 1)
                for m in (2 * u, 2 * u + 1):
                    act.wait_ge(mix32_done, m + 1)
                    act.activation(mix_hi[:, m, :], sB[:, m, :], ACT.Copy).then_inc(mixhi_done, 1)
            act.preload_act_table_set(LN_EXP)
            for u in range(4):
                split_hi(UNIT[("wo", u, 0)] + 1)
                for m in (2 * u, 2 * u + 1):
                    if m < KT - 1:
                        evacuated(act, (("wo", u, 0), m % 2))
                        square(1, m, sq2, x1[:, m, :])
            act.wait_ge(sum_done, SUMS[1] + KT - 2)
            act.wait_ge(x1_half, 1)
            act.activation(sq2[:, 1, HALVES[0]], x1[:, KT - 1, HALVES[0]], ACT.Square).then_inc(sq_half, 1)
            evacuated(act, (("wo", 3, 0), 1))
            act.activation(sq2[:, 1, HALVES[1]], x1[:, KT - 1, HALVES[1]], ACT.Square).then_inc(sq_done, 1)
            act.wait_ge(ssq_half, 1)
            act.activation(rstd2[:, HALVES[0]], side[0][:, HALVES[0]], ACT.Ln, scale=1.0 / D, bias=EPS).then_inc(ln_half, 1)
            act.wait_ge(ln_half, 1)
            act.activation(rstd2[:, HALVES[0]], rstd2[:, HALVES[0]], ACT.Exp, scale=-0.5).then_inc(rstd_half, 1)
            inverse_root(1, rstd2[:, HALVES[1]], side[1][:, HALVES[1]])
            for k in range(KT):
                act.wait_ge(nt_done, KT + k + 1)
                act.activation(h_hi[:, k, :], ntmp2[:, k % 2, :], ACT.Identity,
                               bias=mod[:, 3 * KT + k:3 * KT + k + 1]).then_inc(hh_done, 1)
                if k == 1:
                    split_hi_ffn(0, 1, acc_ready, N_TILES)
            act.preload_act_table(ACT.Gelu)

            def up(a, s, used, value, first=False):
                i = 2 * a + s
                if not (first and s == 0):
                    split_hi_ffn(a + s, 1 - s, used, value)
                for t in range(2):
                    act.wait_ge(ffn_ready, 2 * i + (t + 1))
                    if not first:
                        act.wait_ge(hid_done, i - 1)
                    act.activation(conv[:, s, t, :], bank[2 * s + t][:, :], ACT.Identity,
                                   scale=vecs[:, bass.ds(i + (V_CW2 + t * FT), 1)],
                                   bias=vecs[:, bass.ds(i + (V_CB + t * FT), 1)]).then_inc(tap2_done, 1)
                act.wait_ge(tap_done, 4 * i + 4)
                act.activation(conv[:, s, 1, :], conv[:, s, 1, :], ACT.Gelu).then_inc(gelu_done, 1)

            up(0, 0, acc_ready, N_TILES, first=True)
            up(0, 1, ffn_ready, 2, first=True)
            with act.Fori(1, FT // 2 - 1) as a:
                for s in range(2):
                    up(a, s, ffn_ready, 4 * a + 2 * s)

            def hidden_hi(j, s):
                act.activation(hs_hi[:, s, :, :], hid[:, bass.ds(2 * j, 2), :], ACT.Copy).then_inc(hs_hi_done, 1)

            act.wait_ge(hid_done, 2)
            hidden_hi(0, 0)
            for s in range(2):
                up(FT // 2 - 1, s, ffn_ready, 2 * FT - 4 + 2 * s)

            def down(a, s, used, value):
                j = 2 * a + s
                split_hi_ffn(a + (FT // 2 + s), 1 - s, used, value)
                act.wait_ge(hid_done, 2 * j + 4)
                hidden_hi(j + 1, 1 - s)

            down(0, 0, ffn_ready, 2 * FT)
            down(0, 1, down_done, 1)
            with act.Fori(1, DOWN_UNITS // 2) as a:
                for s in range(2):
                    down(a, s, down_done, 2 * a + s)
            act.preload_act_table_set(LN_EXP)
            for m in range(KT):
                act.wait_ge(x2_done, m + 1)
                square(2, m, sq2, x1[:, m, :])
                act.wait_ge(sq_done, 2 * KT + m + 1)
                act.activation(x1[:, m, :], x1[:, m, :], ACT.Copy, scale=vecs[:, V_FN + m:V_FN + m + 1]).then_inc(xw_done, 1)
            inverse_root(2, rstd_tok, bank[7][:, 0:NB])
            for i in range(0, 8, 2):
                half, b = divmod(i, NB)
                act.wait_ge(yt_ps, i + 1)
                act.wait_ge(rstd_done, 3)
                act.activation(y_tok[:, b, half * SEQ:(half + 1) * SEQ], bank[i][:, :], ACT.Copy,
                               scale=rstd_tok[:, b:b + 1]).then_inc(yt_act, 1)

        @block.vector
        def _(dve):
            dve.wait_ge(vec_ps, 1)
            dve.tensor_copy(vecs[:, 0:ROWS_A], bank[2][:, 0:ROWS_A]).then_inc(vec_sb, 1)

            def ada_sums(j, half):
                dve.wait_ge(silu_done, 1)
                dve.wait_ge(ada_landed[2 * j + half], 32)
                for k in range(half * KT // 2, (half + 1) * KT // 2):
                    total = ada_rows(j, k % 2)
                    if k < 2 and j != 2:
                        dve.tensor_scalar(total, total, c_silu[:, k:k + 1], None, ALU.mult).then_inc(ada_init_dve, 1)
                    if k < 2:
                        continue
                    if k >= 4:
                        dve.wait_ge(ada_step, (KT - 2) * j + k - 3)
                    elif j == 2:
                        dve.wait_ge(ada_init_act, k - 1)
                    else:
                        dve.wait_ge(ada_init_dve, 2 * min(j, 2) + k - 1)
                    dve.scalar_tensor_tensor(total, ada_rows(j, k), c_silu[:, k:k + 1], total,
                                             ALU.mult, ALU.add).then_inc(ada_step, 1)
                if half == 1:
                    dve.wait_ge(ada_step, (KT - 2) * (j + 1))
                    dve.tensor_tensor(ada_rows(j, 0), ada_rows(j, 0), ada_rows(j, 1), ALU.add).then_inc(ada_sum, 1)

            mod_v = mod[:, 0:2 * KT].rearrange("p (s k) -> p s k", s=2)
            bias_v = vecs[:, V_AB:V_AB + 2 * KT].rearrange("p (s k) -> p s k", s=2)

            def shift_and_gain(j):
                two = slice(2 * j, 2 * j + 2)
                dve.wait_ge(mod1_ps, j + 1)
                dve.wait_ge(vec_sb, 1)
                dve.tensor_tensor(mod_v[:, :, two], bank[7 - j % 2][:, 0:4].rearrange("p (s k) -> p s k", s=2),
                                  bias_v[:, :, two], ALU.add).then_inc(mod_done, 1)
                dve.wait_ge(mod_done, j + 1)
                dve.scalar_tensor_tensor(gain[:, 0, two], mod_v[:, 1, two], 1.0, vecs[:, V_N1 + 2 * j:V_N1 + 2 * j + 2],
                                         ALU.add, ALU.mult).then_inc(gain_done, 1)

            def lower(k):
                dve.wait_ge(nt_done, k + 1)
                dve.wait_ge(hh_done, k + 1)
                dve.tensor_tensor(h_lo[:, k, :], ntmp[:, k % 2, :], h_hi[:, k, :].bitcast(F32),
                                  ALU.subtract).then_inc(hl_done, 1)

            def split_lo(n, quarter=None):
                if n == N_UNITS:
                    return split_lo_ffn(0, 0)
                dve.wait_ge(hi_done, n + 1)
                for r, hv, lv in views(n):
                    if quarter is not None:
                        r, hv, lv = (v[:, quarter * UE // 4:(quarter + 1) * UE // 4] for v in (r, hv, lv))
                    last = dve.tensor_tensor(lv, r, hv.bitcast(F32), ALU.subtract)
                if quarter in (None, 3):
                    last.then_inc(raw_used, 1)

            def split_lo_ffn(pair, odd):
                slot = 1 - odd
                dve.wait_ge(hi_done, pair * 2 + (odd + N_UNITS + 1))
                dve.tensor_tensor(w_lo[:, slot, :], raw[:, slot, :], w_hi[:, slot, :].bitcast(F32),
                                  ALU.subtract).then_inc(raw_used, 1)

            def modulate(n):
                if n >= 2 * KT:
                    return
                r, k = divmod(n, KT)
                q = RAW_AT[("ada", n)]
                dve.wait_ge(landed[q % 2], LANDED[q])
                if k > 0:
                    dve.wait_ge(raw_used, RAW_AT[("ada", n - 1)] + 1)
                src = raw[:, q % 2, :]
                if k == 0:
                    if r == 1:
                        dve.wait_ge(acc_ready, TILE[("ada", 0)] + 1)
                    ins = dve.tensor_scalar(ada_acc[:, :], src, c_silu[:, 0:1], None, ALU.mult)
                else:
                    ins = dve.scalar_tensor_tensor(ada_acc[:, :], src, c_silu[:, k:k + 1], ada_acc[:, :],
                                                   ALU.mult, ALU.add)
                ins.then_inc(raw_used, 1)

            def acc(tile):
                i = TILE[tile]
                dve.wait_ge(acc_ready, i + 1)
                return bank[i % 2]

            def free(tile, ins):
                ins.then_inc(acc_free[TILE[tile] % 2], 1)

            def ada_tile(r):
                src = acc(("ada", r))
                at = 2 * KT * (r + 1)
                free(("ada", r), dve.tensor_tensor(mod[:, at:at + 2 * KT], src[:, 0:2 * KT],
                                                   vecs[:, V_AB + at:V_AB + at + 2 * KT], ALU.add))
                if r == 1:
                    evacuated(dve, ("ada", 1))
                    dve.scalar_tensor_tensor(gain[:, 1, :], mod[:, 4 * KT:5 * KT], 1.0, vecs[:, V_N2:V_N2 + KT],
                                             ALU.add, ALU.mult).then_inc(gain_done, 1)

            def rotate(j, t):
                p, g = divmod(j, GROUPS)
                if t == 0 and j > 0:
                    dve.wait_ge(rope_sum, 2 * j)
                if t == 0 and j > 1:
                    dve.wait_ge(qk_in[j % 2], 16 * 8 * (j // 2))
                tile = (("qk", p, g), t)
                src = acc(tile)
                dve.tensor_tensor(rope[:, j % 2, t, :], src[:, :], cs[:, 0, :], ALU.mult)
                free(tile, dve.tensor_tensor(rope_t[:, 1 - t, :], src[:, :], cs[:, 1, :], ALU.mult))

            def mask_and_max(hh, banks=range(4)):
                p, hd = divmod(hh, 2)
                prev_own, own = cst[:, C_MSK:C_MSK + 2 * P], cst[:, C_MSK + P:C_MSK + 2 * P]
                own4 = own.rearrange("p (a n) -> p a n", a=1).broadcast_to((P, DIL, P))
                mod4 = cst[:, C_MOD:C_MOD + P].rearrange("p (a n) -> p a n", a=1).broadcast_to((P, DIL, P))
                two = prev_own.rearrange("p (a n) -> p a n", a=1).broadcast_to((P, 2, 2 * P))
                for bk in banks:
                    dve.wait_ge(sc_done, 4 * hh + bk + 1)
                    if hh >= 2:
                        dve.wait_ge(tr_ps, 4 * (hh - 2) + bk + 1)
                    at, w = BANK_AT[bk], BANK_W[bk]
                    dst, src = S[:, hd, at:at + w], side[bk][:, 0:w]
                    if bk == 1:
                        m = cst[:, C_MSK:C_MSK + 3 * P]
                    else:
                        m = (two, None, own4, mod4)[bk]
                        n_b = 2 if bk == 0 else DIL
                        dst, src = (v.rearrange("p (a n) -> p a n", a=n_b) for v in (dst, src))
                    dve.tensor_tensor(dst, src, m, ALU.add).then_inc(msk_done, 1)
                for bk in banks:
                    dve.wait_ge(msk_done, 4 * hh + bk + 1)
                    at = BANK_AT[bk]
                    if hd == 0 and bk == 0 and p > 0:
                        dve.wait_ge(mxr_ps, p)
                    if bk == 0:
                        dve.tensor_reduce(mx[:, 1:3, hd], S[:, hd, 0:4 * P].rearrange("p (a n) -> p a n", a=2),
                                          AX.X, ALU.max)
                    elif bk == 1:
                        dve.tensor_reduce(mx[:, 3:4, hd], S[:, hd, at:at + 2 * P], AX.X, ALU.max)
                        dve.tensor_reduce(mx[:, 0:1, hd], S[:, hd, at + 2 * P:at + 3 * P], AX.X, ALU.max)
                    else:
                        dve.tensor_reduce(mg[:, bk - 2, :], S[:, hd, at:at + 4 * P].rearrange("p (a n) -> p a n", a=DIL),
                                          AX.X, ALU.max).then_inc(mx1_done, 1)
                if 3 not in banks:
                    return
                dve.wait_ge(mx1_done, 2 * hh + 2)
                dve.tensor_tensor(mx[:, NB:2 * NB, hd], mg[:, 0, :], mg[:, 1, :], ALU.max).then_inc(mx_done, 1)
                dve.wait_ge(mx_done, hh + 1)

            def attention(p, i):
                if (p, i) == (0, 0):
                    mask_and_max(0, range(3))
                elif i in (0, 1):
                    if (p, i) == (0, 1):
                        mask_and_max(0, range(3, 4))
                    mask_and_max(2 * p + i)
                if i == 2:
                    dve.wait_ge(mxr_ps, p + 1)
                    if p > 0:
                        dve.wait_ge(mxc_ps, p)
                    dve.tensor_copy(rowm[:, 0, :], side[0][0:2, :]).then_inc(rowmax_done, 1)
                    dve.wait_ge(rowmax_done, 2 * p + 1)
                    dve.tensor_tensor(rowm[:, 1, :], side[1][0:2, :], rowm[:, 0, :], ALU.max).then_inc(rowmax_done, 1)
                if i == 3:
                    dve.wait_ge(mxc_ps, p + 1)
                    if p > 0:
                        dve.wait_ge(exp_done, 8 * p)
                    dve.tensor_scalar(negm[:, :, :].rearrange("p a b -> p (a b)"), side[0][:, 0:16],
                                      -DH ** -0.5, None, ALU.mult).then_inc(negm_done, 1)
                if i in (4, 5):
                    hh = 2 * p + i - 4
                    for bk in (2, 3):
                        dve.wait_ge(tr_ps, 4 * hh + bk + 1)
                        if hh >= 1:
                            dve.wait_ge(pv_done, hh)
                        at = BANK_AT[bk]
                        dve.tensor_copy(PT[:, at:at + BANK_W[bk]], side[bk][:, 0:BANK_W[bk]]).then_inc(pt_dve, 1)
                if i in (5, 6):
                    hh = 2 * p + i - 5
                    hd = hh % 2
                    top, bottom = slice(0, DH), slice(DH, P)
                    num, den = (top, bottom) if hd == 0 else (bottom, top)
                    dve.wait_ge(perm_sb, hh + 1)
                    if hh > 0:
                        dve.wait_ge(oa32_done, hh)
                        dve.wait_ge(oln_done, hh)
                    dve.tensor_tensor(osum[:, :], side[4][:, :], ocomb[:, :], ALU.add).then_inc(osum_done, 1)
                    dve.wait_ge(osum_done, hh + 1)
                    dve.wait_ge(orec_done, hh + 1)
                    if p > 0:
                        dve.wait_ge(oalo_done, p)
                    dve.tensor_tensor(oa32[num, :], osum[num, :], orec[num, :], ALU.mult).then_inc(oa32_done, 1)
                if i == 6:
                    dve.wait_ge(oa32_done, 2 * p + 2)
                    dve.wait_ge(oahi_done, p + 1)
                    dve.tensor_tensor(oa_lo[:, p, :], oa32[:, :], oa_hi[:, p, :].bitcast(F32),
                                      ALU.subtract).then_inc(oalo_done, 1)
                    dve.wait_ge(oalo_done, p + 1)

            def gates():
                for b in range(NB):
                    evacuated(dve, ("z", b))
                    dve.wait_ge(z_ln, b + 1)
                    dve.tensor_tensor(logs[:, b, :], logs[:, b, :], z_abs_sb[b], ALU.add).then_inc(logs_done, 1)

            def keys(h, b):
                u = NB * h + b
                if u >= 1:
                    dve.wait_ge(at_ps, u)
                    dve.wait_ge(kk_done, u)
                own = k_in[:, h % 2, b * P:(b + 1) * P]
                dve.tensor_copy(kk[:, :, :], own.rearrange("p (a n) -> p a n", a=1).broadcast_to((P, NCH, P))).then_inc(kk_step, 1)
                for n in range(NCH):
                    w = CHUNK * (n + 1)
                    decay = eb[:, b * P + w - 1:b * P + w]
                    dve.wait_ge(kk_step, NCH * u + n + 1)
                    dst = kk[:, n + 1, 0:w] if n < NCH - 1 else ke[:, :]
                    dve.tensor_scalar(dst, kk[:, n, 0:w], decay, None,
                                      ALU.mult).then_inc(kk_step if n < NCH - 1 else kk_done, 1)

            def gla(h, i):
                if i == 0:
                    q, k = q_in[:, h % 2, :], k_in[:, h % 2, :]
                    evacuated(dve, (("gqk", h, 0), 0))
                    evacuated(dve, (("gqk", h, 0), 1))
                    dve.wait_ge(gexp_done, 3 * h + 3)
                    dve.tensor_tensor(k, k, enb[:, :], ALU.mult).then_inc(qg_done, 1)
                    dve.tensor_tensor(q, q, eb[:, :], ALU.mult).then_inc(qg_done, 1)
                    if h > 0:
                        dve.wait_ge(p3_done, NB * h)
                    dve.wait_ge(qg_done, 2 * h + 2)
                    keys(h, 0)
                    chunks = q.rearrange("p (b n c) -> p b n c", b=NB, n=NCH)
                    start = ed[:, :, 0:NCH].rearrange("p b (n o) -> p b n o", o=1).broadcast_to((P, NB, NCH, CHUNK))
                    dve.tensor_tensor(qB[:, :].rearrange("p (b n c) -> p b n c", b=NB, n=NCH), chunks, start,
                                      ALU.mult).then_inc(qB_done, 1)
                if 2 <= i <= 5:
                    b = i - 2
                    u = NB * h + b
                    dve.wait_ge(at_ps, u + 1)
                    if u >= 2:
                        dve.wait_ge(p3_done, u - 1)
                    dve.copy_predicated(at_sb[:, u % 2, :], cst[:, C_KEEP:C_KEEP + P].bitcast(U32),
                                        side[2][:, 0:P]).then_inc(at_done, 1)
                    if b + 1 < NB:
                        keys(h, b + 1)
                if 3 <= i <= 5:
                    b = i - 3
                    dve.wait_ge(p3_done, NB * h + b + 1)
                    new = side[1][:, 64:64 + DV]
                    if b == 0:
                        if h > 0:
                            dve.wait_ge(st_done, 3 * h)
                        ins = dve.tensor_copy(state[:, :], new)
                    else:
                        dve.wait_ge(st_done, 3 * h + b)
                        ins = dve.scalar_tensor_tensor(state[:, :], state[:, :], ed[:, b, NCH:NCH + 1], new,
                                                       ALU.mult, ALU.add)
                    ins.then_inc(st_done, 1)
                if i == 6:
                    dve.wait_ge(p3_done, NB * h + NB)
                    if h > 0:
                        dve.wait_ge(oglo_done, h)
                    for v in range(2):
                        dve.tensor_copy(o_sb[:, v, :], side[4 + v][:, :]).then_inc(o_done, 1)
                if i == 8:
                    dve.wait_ge(grstd_done, h + 1)
                    dve.wait_ge(osq_done, h + 1)
                    dve.tensor_tensor(o_sb[:, :, :], o_sb[:, :, :],
                                      ors[:, :].rearrange("p (a n) -> p a n", a=1).broadcast_to((P, 2, SEQ)),
                                      ALU.mult).then_inc(on_done, 1)
                    dve.wait_ge(on_done, h + 1)
                    evacuated(dve, (("gr", h, 0), 0))
                    evacuated(dve, (("gr", h, 0), 1))
                    for v in range(2):
                        dve.scalar_tensor_tensor(o_sb[:, v, :], o_sb[:, v, :], vecs[:, V_GN + v:V_GN + v + 1],
                                                 gr[:, h % 2, v, :], ALU.mult, ALU.mult).then_inc(og32_done, 1)
                if i == 9:
                    dve.wait_ge(og32_done, 2 * h + 2)
                    dve.wait_ge(oghi_done, h + 1)
                    dve.tensor_tensor(og_lo[:, 2 * h:2 * h + 2, :], o_sb[:, :, :],
                                      og_hi[:, 2 * h:2 * h + 2, :].bitcast(F32), ALU.subtract).then_inc(oglo_done, 1)

            def rotary_angles():
                dve.wait_ge(pos_in, 16)
                dve.tensor_copy(ang, pos_i).then_inc(rot_dve, 1)
                dve.wait_ge(cst_in, 16)
                dve.wait_ge(rot_dve, 1)
                dve.tensor_scalar(ang, ang, cst[:, C_FRQ:C_FRQ + 1], None, ALU.mult).then_inc(rot_dve, 1)
                dve.wait_ge(rot_dve, 2)
                dve.tensor_scalar(turns, ang, float(1.0 / (2 * np.pi)), ROUND, ALU.mult, ALU.add).then_inc(rot_dve, 1)
                dve.wait_ge(rot_dve, 3)
                dve.tensor_scalar(turns, turns, ROUND, None, ALU.subtract).then_inc(rot_dve, 1)
                for n, part in enumerate(TWO_PI):
                    dve.wait_ge(rot_dve, 4 + n)
                    last = dve.scalar_tensor_tensor(ang, turns, -part, ang, ALU.mult, ALU.add)
                    if n < 2:
                        last.then_inc(rot_dve, 1)
                    else:
                        last.then_inc(rot_sum, 1)
                dve.wait_ge(rot_sum, 1)
                dve.tensor_scalar(ang, ang, 3.1415925, -3.1415925, ALU.min, ALU.max).then_inc(rot_dve, 1)

            for j in range(2):
                for half in range(2):
                    ada_sums(j, half)
            shift_and_gain(0)
            split_lo(0)
            shift_and_gain(1)
            ada_sums(2, 0)
            ada_sums(2, 1)
            ada_sums(3, 0)
            shift_and_gain(2)
            ada_sums(3, 1)
            for k in (4, 5):
                lower(k)
            shift_and_gain(3)
            split_lo(1)
            for k in (6, 7):
                lower(k)
            for n in range(GROUPS):
                if n > 0:
                    split_lo(n + 1)
                modulate(n)
                if n == 0:
                    rotary_angles()
                    dve.wait_ge(vec_ps, 3)
                    for half in range(2):
                        dve.tensor_copy(vecs[:, ROWS_A + half * ROWS_B:ROWS_A + (half + 1) * ROWS_B],
                                        bank[2][:, P * (half + 1):P * (half + 1) + ROWS_B]).then_inc(vec_sb, 1)
            dve.wait_ge(rot_act, 3)
            for p in range(2):
                for g in range(GROUPS):
                    n = UNIT[("qk", p, g)]
                    if p == 0 or g == 0:
                        rotate(GROUPS * p + g, 0)
                        split_lo(n + 1)
                        rotate(GROUPS * p + g, 1)
                        modulate(n)
                        if p == 1:
                            attention(0, 0)
                    else:
                        split_lo(n + 1)
                        if g == 1:
                            attention(0, 1)
                            rotate(GROUPS + g, 0)
                            modulate(n)
                        else:
                            rotate(GROUPS + g, 0)
                            attention(0, 3)
                            ada_tile(0)
                        rotate(GROUPS + g, 1)
                        if g == 2:
                            modulate(n)
                        attention(0, 2 * g)
            n = UNIT[("lr", 0, 0)]
            split_lo(n + 1)
            modulate(n)
            attention(0, 5)
            for h in range(HEADS):
                for u, kind in enumerate(("gqk", "gv", "gr")):
                    n = UNIT[(kind, h, 0)]
                    split_lo(n + 1)
                    modulate(n)
                    for t in range(2):
                        i = 2 * u + t
                        if h == 0 and i == 0:
                            attention(0, 6)
                        if h == 0:
                            attention(1, i)
                        if h == 1 and i == 0:
                            attention(1, 6)
                            dve.memset(at_sb[:, :, :], 0.0).then_inc(at_zero, 1)
                            dve.wait_ge(at_zero, 1)
                        if h >= 2 and i == 0:
                            gla(h - 2, 6)
                        if h >= 1:
                            gla(h - 1, i)
                        if h >= 2 and i in (2, 3):
                            gla(h - 2, 6 + i)
                    if h == 0 and kind == "gqk":
                        gates()
                    if (kind, h) == ("gr", 2):
                        ada_tile(1)
            for u in range(4):
                split_lo(UNIT[("ma", u, 0)] + 1)
                for t in range(2):
                    i = 2 * u + t
                    if i == 0:
                        gla(2, 6)
                    gla(3, i)
                    if i in (2, 3):
                        gla(2, 6 + i)
            for u in range(4):
                split_lo(UNIT[("mb", u, 0)] + 1)
                if u == 0:
                    for i in (8, 9):
                        gla(3, i)
            n = UNIT[("wa", 0, 0)]
            for m in range(KT):
                tile = (UNITS[n], m)
                evacuated(dve, (("mb", m // 2, 0), m % 2))
                free(tile, dve.tensor_tensor(sB[:, m, :], acc(tile)[:, :], sB[:, m, :], ALU.mult))
                if m < 4:
                    split_lo(n + 1, m)
            for u in range(4):
                split_lo(UNIT[("wg", u, 0)] + 1)
                for t in range(2):
                    m = 2 * u + t
                    tile = (("wg", u, 0), t)
                    if m >= 2:
                        dve.wait_ge(mix32_done, m - 1)
                    evacuated(dve, (("wa", 0, 0), m))
                    evacuated(dve, (("ma", m // 2, 0), m % 2))
                    src = acc(tile)
                    free(tile, dve.tensor_tensor(mtmp[:, m % 2, :], src[:, :], sA[:, m, :], ALU.mult))
                    dve.wait_ge(mixhi_done, m + 1)
                    dve.tensor_tensor(mix_lo[:, m, :], sB[:, m, :], mix_hi[:, m, :].bitcast(F32),
                                      ALU.subtract).then_inc(mixlo_done, 1)
            for u in range(4):
                split_lo(UNIT[("wo", u, 0)] + 1)
                for t in range(2):
                    m = 2 * u + t
                    tile = (("wo", u, 0), t)
                    dve.wait_ge(x_back, 16)
                    src = acc(tile)
                    for tok in HALVES if m == KT - 1 else (slice(0, SEQ),):
                        last = dve.scalar_tensor_tensor(x1[:, m, tok], src[:, tok], mod[:, 2 * KT + m:2 * KT + m + 1],
                                                        x1[:, m, tok], ALU.mult, ALU.add)
                        if tok == HALVES[0]:
                            last.then_inc(x1_half, 1)
                    free(tile, last)
            for t in range(2):
                evacuated(dve, (("wo", 3, 0), t))
            dve.wait_ge(rstd_half, 1)
            dve.wait_ge(rstd_done, 2)
            dve.wait_ge(gain_done, KT // 2 + 1)

            def lower_second(k):
                dve.wait_ge(hh_done, KT + k + 1)
                dve.scalar_tensor_tensor(h_lo[:, k, :], ntmp2[:, k % 2, :], mod[:, 3 * KT + k:3 * KT + k + 1],
                                         h_hi[:, k, :].bitcast(F32), ALU.add, ALU.subtract).then_inc(hl_done, 1)

            for k in range(KT):
                if k >= 2:
                    dve.wait_ge(hh_done, KT + k - 1)
                    dve.wait_ge(hl_done, KT // 2 + k - 1)
                dve.scalar_tensor_tensor(ntmp2[:, k % 2, :], x1[:, k, :], gain[:, 1, k:k + 1], rstd2[:, :],
                                         ALU.mult, ALU.mult).then_inc(nt_done, 1)
                if k >= 1:
                    lower_second(k - 1)
            lower_second(KT - 1)

            def up(a, s, split=True):
                i = 2 * a + s
                if split:
                    split_lo_ffn(a + s, 1 - s)
                else:
                    dve.wait_ge(raw_used, N_RAW + 2)
                for t in range(2):
                    dve.wait_ge(tap2_done, 2 * i + (t + 1))
                    src = bank[2 * s + t]
                    for tap, col in ((1, V_CW1), (2, V_CW0)):
                        if tap == 2:
                            dve.wait_ge(tap_done, 4 * i + (2 * t + 1))
                        ins = dve.scalar_tensor_tensor(conv[:, s, t, tap:SEQ], src[:, 0:SEQ - tap],
                                                       vecs[:, bass.ds(i + (col + t * FT), 1)],
                                                       conv[:, s, t, tap:SEQ], ALU.mult, ALU.add)
                        ins.then_inc(tap_done, 1)
                dve.wait_ge(gelu_done, i + 1)
                dve.tensor_tensor(hid[:, bass.ds(i, 1), :].rearrange("p a n -> p (a n)"), conv[:, s, 0, :],
                                  conv[:, s, 1, :], ALU.mult).then_inc(hid_done, 1)

            up(0, 0, split=False)
            up(0, 1)
            with dve.Fori(1, FT // 2 - 1) as a:
                for s in range(2):
                    up(a, s)

            def hidden_lo(j, s):
                dve.wait_ge(hs_hi_done, j + 1)
                dve.tensor_tensor(hs_lo[:, s, :, :], hid[:, bass.ds(2 * j, 2), :], hs_hi[:, s, :, :].bitcast(F32),
                                  ALU.subtract).then_inc(hs_lo_done, 1)

            hidden_lo(0, 0)
            for s in range(2):
                up(FT // 2 - 1, s)
            with dve.Fori(0, DOWN_UNITS // 2) as a:
                for s in range(2):
                    split_lo_ffn(a + (FT // 2 + s), 1 - s)
                    hidden_lo(2 * a + s + 1, 1 - s)
            for m in range(KT):
                dve.wait_ge(down_tile, m + 1)
                dve.scalar_tensor_tensor(x1[:, m, :], bank[m][:, :], mod[:, 5 * KT + m:5 * KT + m + 1], x1[:, m, :],
                                         ALU.mult, ALU.add).then_inc(x2_done, 1)
            for i in range(1, 8, 2):
                half, b = divmod(i, NB)
                dve.wait_ge(yt_ps, i + 1)
                dve.wait_ge(rstd_done, 3)
                dve.tensor_scalar(y_tok[:, b, half * SEQ:(half + 1) * SEQ], bank[i][:, :], rstd_tok[:, b:b + 1],
                                  None, ALU.mult).then_inc(yt_dve, 1)

        @block.tensor
        def _(pe):
            ident = cst[:, C_ID:C_ID + P]

            def three(out_ap, w, x_, first, last):
                (wh, wl), (xh, xl) = w, x_
                pe.matmul(out_ap, wh, xh, start=first, stop=False, skip_group_check=True)
                pe.matmul(out_ap, wh, xl, start=False, stop=False, skip_group_check=True)
                return pe.matmul(out_ap, wl, xh, start=False, stop=last, skip_group_check=True)

            pe.wait_ge(ident_in, 16)
            pe.wait_ge(rows_in, 6 * 16)
            pe.transpose(bank[2][:, 0:ROWS_A], rows_a[:, :], ident[0:ROWS_A, 0:ROWS_A]).then_inc(vec_ps, 1)
            pe.wait_ge(x_in, NB * 16)
            pe.wait_ge(ones_set, 1)

            for k in range(KT):
                if k >= 4:
                    pe.wait_ge(xt_sb, k - 3)
                for b in range(NB):
                    last = pe.transpose(bank[3 + k % 4][:, b * P:(b + 1) * P], x_tok[:, b, k * P:(k + 1) * P], ident)
                last.then_inc(xt_ps, 1)

            def shift_scale(j):
                pe.wait_ge(ada_sum, j + 1)
                if j == 1:
                    pe.wait_ge(xt_sb, KT)
                if j > 1:
                    pe.wait_ge(mod_done, j - 1)
                for n in range(4):
                    last = pe.matmul(bank[7 - j % 2][:, n:n + 1], ada_rows(j, 0)[:, n * P:(n + 1) * P], ones[:, 0:1],
                                     start=True, stop=True, skip_group_check=True)
                last.then_inc(mod1_ps, 1)

            def take(i):
                if i >= 2:
                    pe.wait_ge(acc_free[i % 2], i // 2)
                return bank[i % 2]

            def product(n, t):
                kind, a, _ = UNITS[n]
                slot = n % 2
                i = TILE[(UNITS[n], t)]
                ada = WITH_ADA.get((UNITS[n], t))
                if ada is not None:
                    take(i - 1)
                    pe.wait_ge(raw_used, RAW_AT[("ada", KT * (ada + 1) - 1)] + 1)
                dst = take(i)
                if t == 0:
                    pe.wait_ge(raw_used, RAW_AT[("w", n)] + 1)
                if kind in ("v", "gv"):
                    for half in range(2):
                        blk = 2 * t + half
                        tok = slice(blk * P, (blk + 1) * P) if kind == "gv" or a == 0 else slice(blk, SEQ, DIL)
                        for k in range(KT):
                            w = tuple(v[:, slot, k * UW:(k + 1) * UW] for v in (w_hi, w_lo))
                            s = tuple(v[:, k, tok] for v in (h_hi, h_lo))
                            last = three(dst[:, half * UW:(half + 1) * UW], s, w, k == 0, k == KT - 1)
                else:
                    if kind == "wa":
                        nk, width, at, src = 2, D, t * P, (oa_hi, oa_lo)
                    elif kind == "lr":
                        nk, width, at, src = KT, LOWRANK, 0, (h_hi, h_lo)
                    else:
                        nk, width, at = KT, UW, t * P
                        src = {"wg": (og_hi, og_lo), "wo": (mix_hi, mix_lo)}.get(kind, (h_hi, h_lo))
                    m = LOWRANK if kind == "lr" else P
                    if kind == "wa" and t == 0:
                        pe.wait_ge(oalo_done, 2)
                    if kind == "wg" and a == 0 and t == 0:
                        pe.wait_ge(oglo_done, HEADS)
                    for k in range(nk):
                        if kind == "wo" and a == 0 and t == 0:
                            pe.wait_ge(mixlo_done, k + 1)
                        w = tuple(v[:, slot, k * width + at:k * width + at + m] for v in (w_hi, w_lo))
                        last = three(dst[0:m, :], w, tuple(v[:, k, :] for v in src), k == 0, k == nk - 1)
                        if ada is not None and k < nk - 1:
                            ada_part(ada, k)
                last.then_inc(acc_ready, 1)

            def ada_part(r, k):
                dst = bank[TILE[("ada", r)] % 2]
                for j in range(3 * k, min(3 * k + 3, 2 * KT)):
                    last = pe.matmul(dst[:, j:j + 1], ada_acc[:, j * P:(j + 1) * P], ones[:, 0:1],
                                     start=(j == 0), stop=True, skip_group_check=True)
                    if j == 2 * KT - 1:
                        last.then_inc(acc_ready, 1)

            def scores(hh, banks=range(4)):
                p, hd = divmod(hh, 2)
                for bk in banks:
                    if hh >= 1:
                        pe.wait_ge(msk_done, 4 * (hh - 1) + bk + 1)
                    if hd == 0:
                        j = GROUPS * p + max(bk - 1, 0)
                        pe.wait_ge(qk_in[j % 2], 16 * 8 * (j // 2 + 1))
                    if hd == 0 and p > 0:
                        pe.wait_ge(pt_act if bk < 2 else pt_dve, 4 * p)
                    if bk < 2:
                        blocks = [(0, 1), (2 * P, 2)] if bk == 0 else [(0, 3), (2 * P, 0)]
                        for col, b in blocks:
                            lo = max(b - 1, 0) * P
                            keys = slice(lo, (b + 1) * P)
                            last = pe.matmul(side[bk][:, col:col + (b + 1) * P - lo], qk[:, 0, 0, hd, b * P:(b + 1) * P],
                                             qk[:, 0, 1, hd, keys], start=True, stop=True, skip_group_check=True)
                    else:
                        for r in range(DIL):
                            tok = slice(r, SEQ, DIL)
                            last = pe.matmul(side[bk][:, r * P:(r + 1) * P], qk[:, bk - 1, 0, hd, tok],
                                             qk[:, bk - 1, 1, hd, tok], start=True, stop=True, skip_group_check=True)
                    last.then_inc(sc_done, 1)

            def transposes(hh):
                hd = hh % 2
                for bk in range(4):
                    pe.wait_ge(exp_done, 4 * hh + bk + 1)
                    if hd == 1:
                        pe.wait_ge(pt_act if bk < 2 else pt_dve, 2 * hh - (1 - bk % 2))
                    for col in range(0, BANK_W[bk], P):
                        last = pe.transpose(side[bk][:, col:col + P], S[:, hd, BANK_AT[bk] + col:BANK_AT[bk] + col + P], ident)
                    last.then_inc(tr_ps, 1)

            def values(hh):
                pe.wait_ge(pt_act, 2 * hh + 2)
                pe.wait_ge(pt_dve, 2 * hh + 2)
                if hh >= 1:
                    pe.wait_ge(osum_done, hh)
                if hh == 0:
                    pe.wait_ge(v_ones, 2)
                    evacuated(pe, (("v", GROUPS - 1, 0), 0))
                    evacuated(pe, (("v", GROUPS - 1, 0), 1))
                at = {1: 0, 2: 2 * P, 3: 4 * P}
                for b in range(NB):
                    dst = side[4][:, b * P:(b + 1) * P]
                    if b == 0:
                        pe.matmul(dst, v_ext[:, 0, 0, hh, :], PT[:, 6 * P:7 * P], start=True, stop=True, skip_group_check=True)
                    else:
                        for j in range(2):
                            pe.matmul(dst, v_ext[:, b - 1 + j, 0, hh, :], PT[:, at[b] + j * P:at[b] + (j + 1) * P],
                                      start=(j == 0), stop=(j == 1), skip_group_check=True)
                for r in range(DIL):
                    for g in (1, 2):
                        col = BANK_AT[g + 1] + r * P
                        last = pe.matmul(side[5][:, r * P:(r + 1) * P], v_ext[:, r, g, hh, :], PT[:, col:col + P],
                                         start=(g == 1), stop=(g == 2), skip_group_check=True)
                last.then_inc(pv_done, 1)

            def attention(p, i):
                if (p, i) == (0, 0):
                    scores(0, range(3))
                elif (p, i) == (0, 1):
                    scores(0, range(3, 4))
                    scores(1)
                elif i in (0, 1):
                    scores(2 * p + i)
                if i == 2:
                    pe.wait_ge(mx_done, 2 * p + 2)
                    for b in range(NB):
                        pe.transpose(side[0][0:2, b * P:(b + 1) * P], mx[:, b, :], ident)
                    for r in range(DIL):
                        last = pe.transpose(side[1][0:2, r::DIL], mx[:, NB + r, :], ident)
                    last.then_inc(mxr_ps, 1)
                if i == 3:
                    pe.wait_ge(rowmax_done, 2 * p + 2)
                    for b in range(NB):
                        pe.transpose(side[0][:, 2 * b:2 * b + 2], rowm[:, 1, b * P:(b + 1) * P], ident[0:2, 0:2])
                    for r in range(DIL):
                        c0 = 2 * (NB + r)
                        last = pe.transpose(side[0][:, c0:c0 + 2], rowm[:, 1, r::DIL], ident[0:2, 0:2])
                    last.then_inc(mxc_ps, 1)
                if i == 4:
                    transposes(2 * p)
                if i == 5:
                    values(2 * p)
                    transposes(2 * p + 1)
                if i == 6:
                    values(2 * p + 1)

            def gate_tiles():
                pe.wait_ge(w2_in, 32)
                evacuated(pe, (("lr", 0, 0), 0))
                for b in range(NB):
                    dst = take(TILE[("z", b)])
                    pe.matmul(dst[:, :], lrT[0:LOWRANK + 1, b * P:(b + 1) * P], w2b[:, :],
                              start=True, stop=True).then_inc(acc_ready, 1)

            def within(h, b):
                u = NB * h + b
                pe.wait_ge(kk_done, u + 1)
                if u >= 1:
                    pe.wait_ge(at_done, u)
                    pe.wait_ge(kt_done, u)
                for n in range(NCH):
                    at = CHUNK * n
                    m = (at + CHUNK + 31) // 32 * 32
                    pe.matmul(side[2][0:m, at:at + CHUNK], kk[:, n, 0:m], q_in[:, h % 2, b * P + at:b * P + at + CHUNK],
                              start=True, stop=True, skip_group_check=True)
                pe.transpose(side[3][:, 0:P], ke[:, :], ident).then_inc(at_ps, 1)

            def outputs(h, b):
                u = NB * h + b
                pe.wait_ge(at_done, u + 1)
                pe.wait_ge(kt_done, u + 1)
                if b == 0:
                    if h == 0:
                        pe.wait_ge(osum_done, 4)
                    else:
                        pe.wait_ge(o_done, 2 * h)
                    evacuated(pe, (("gv", h, 0), 0))
                    evacuated(pe, (("gv", h, 0), 1))
                else:
                    pe.wait_ge(st_done, 3 * h + b)
                    pe.wait_ge(qB_done, h + 1)
                for v in range(2):
                    dst = side[4 + v][:, b * P:(b + 1) * P]
                    last = pe.matmul(dst, gv[:, h % 2, b, v * P:(v + 1) * P], at_sb[:, u % 2, :],
                                     start=True, stop=(b == 0), skip_group_check=True)
                    if b > 0:
                        last = pe.matmul(dst, state[:, v * P:(v + 1) * P], qB[:, b * P:(b + 1) * P],
                                         start=False, stop=True, skip_group_check=True)
                if b < NB - 1:
                    last = pe.matmul(side[1][:, 64:64 + DV], kt_sb[:, u % 2, :], gv[:, h % 2, b, :],
                                     start=True, stop=True, skip_group_check=True)
                last.then_inc(p3_done, 1)

            def gla(h, i):
                if i == 0:
                    pe.wait_ge(logs_done, NB)
                    if h >= 1:
                        pe.wait_ge(gexp_done, 3 * h)
                        pe.wait_ge(st_done, 3 * h)
                    if h >= 2:
                        pe.wait_ge(gln_done, h - 1)
                    for b in range(NB):
                        g = logs[:, b, h * P:(h + 1) * P]
                        pe.matmul(side[0][:, b * P:(b + 1) * P], g, cst[:, C_TRI:C_TRI + P],
                                  start=True, stop=True, skip_group_check=True)
                        c0 = b * (NCH + 1)
                        last = pe.matmul(side[1][:, c0:c0 + NCH + 1], g, cst[:, C_TRI + P:C_TRI + P + NCH + 1],
                                         start=True, stop=True, skip_group_check=True)
                    last.then_inc(b_ps, 1)
                if 2 <= i <= 5:
                    within(h, i - 2)
                if 3 <= i <= 6:
                    outputs(h, i - 3)
                if i == 8:
                    pe.wait_ge(osum2_done, h + 1)
                    pe.wait_ge(gexp_done, 3 * min(h + 2, HEADS))
                    pe.matmul(side[0][:, :], ones[:, :], osq[:, 0, :], start=True, stop=True,
                              skip_group_check=True).then_inc(gssq_ps, 1)

            shift_scale(0)
            pe.wait_ge(sum_done, SUMS[0] + KT - 1)
            pe.matmul(bank[0][:, :], ones[:, :], sq_sum[:, :], start=True, stop=False)
            pe.wait_ge(sq_done, KT)
            pe.matmul(bank[0][:, :], ones[:, :], sq[:, (KT - 1) % 2, :], start=False, stop=True).then_inc(ssq_ps, 1)
            shift_scale(1)
            pe.wait_ge(raw_used, 1)
            pe.wait_ge(rstd_done, 1)
            for k in range(KT):
                if k in (2, 5):
                    shift_scale(2 + k // 4)
                w = [v[:, 0, k * UW:(k + 1) * UW] for v in (w_hi, w_lo)]
                pe.wait_ge(hh_done, k + 1)
                for blk in range(NB):
                    dst = bank[blk // 2][:, blk % 2 * UW:(blk % 2 + 1) * UW]
                    for part in range(2):
                        pe.matmul(dst, h_hi[:, k, blk * P:(blk + 1) * P], w[part],
                                  start=(k == 0 and blk % 2 == 0 and part == 0), stop=False, skip_group_check=True)
                if k < KT // 2:
                    pe.wait_ge(hl_pool, k + 1)
                else:
                    pe.wait_ge(hl_done, k + 1 - KT // 2)
                for blk in range(NB):
                    dst = bank[blk // 2][:, blk % 2 * UW:(blk % 2 + 1) * UW]
                    last = pe.matmul(dst, h_lo[:, k, blk * P:(blk + 1) * P], w[0],
                                     start=False, stop=(k == KT - 1), skip_group_check=True)
                    if k == KT - 1 and blk % 2 == 1:
                        last.then_inc(acc_ready, 1)
            pe.wait_ge(cst_in, 16)
            pe.wait_ge(conv_in, 3 * 16)
            for half in range(2):
                pe.transpose(bank[2][:, P * (half + 1):P * (half + 1) + ROWS_B], rows_b[:, half, :],
                             ident[0:ROWS_B, 0:ROWS_B]).then_inc(vec_ps, 1)

            for n in range(1, GROUPS):
                for t in range(2):
                    product(n, t)
            for p in range(2):
                for g in range(GROUPS):
                    for t in range(2):
                        product(UNIT[("qk", p, g)], t)
                        if p == 1 and 2 * g + t > 0:
                            attention(0, 2 * g + t - 1)
            product(UNIT[("lr", 0, 0)], 0)
            attention(0, 5)
            for h in range(HEADS):
                for u, kind in enumerate(("gqk", "gv", "gr")):
                    for t in range(2):
                        i = 2 * u + t
                        product(UNIT[(kind, h, 0)], t)
                        if h == 0 and i == 0:
                            attention(0, 6)
                        if h == 0:
                            attention(1, i)
                        if h == 1 and i == 0:
                            attention(1, 6)
                        if h >= 2 and i in (0, 2, 3):
                            gla(h - 2, 6 + i)
                        if h >= 1:
                            gla(h - 1, i)
                    if h == 0 and kind == "gqk":
                        gate_tiles()
            for u in range(4):
                for t in range(2):
                    i = 2 * u + t
                    product(UNIT[("ma", u, 0)], t)
                    if i in (0, 2, 3):
                        gla(2, 6 + i)
                    gla(3, i)
            for u in range(4):
                for t in range(2):
                    product(UNIT[("mb", u, 0)], t)
                    if u == 0:
                        gla(3, 8 + t)
            for m in range(KT):
                product(UNIT[("wa", 0, 0)], m)
            for kind in ("wg", "wo"):
                for u in range(4):
                    for t in range(2):
                        product(UNIT[(kind, u, 0)], t)
            pe.wait_ge(sum_done, SUMS[1] + KT - 1)
            for half, tok in enumerate(HALVES):
                pe.matmul(side[half][:, tok], ones[:, :], sq_sum2[:, tok], start=True, stop=False)
            for half, tok in enumerate(HALVES):
                pe.wait_ge(sq_half if half == 0 else sq_done, 1 if half == 0 else 2 * KT)
                pe.matmul(side[half][:, tok], ones[:, :], sq2[:, 1, tok],
                          start=False, stop=True).then_inc(ssq_half if half == 0 else ssq_ps, 1)

            def up_tile(s, t, k):
                slot, at = 1 - s, k * UW + t * P
                w = tuple(v[:, slot, at:at + P] for v in (w_hi, w_lo))
                return three(bank[2 * s + t][:, :], w, (h_hi[:, k, :], h_lo[:, k, :]), k == 0, k == KT - 1)

            def up(a, s, first=False):
                i = 2 * a + s
                for t in range(2):
                    if not first:
                        pe.wait_ge(tap_done, 4 * i + (2 * t - 6))
                    if t == 0:
                        pe.wait_ge(raw_used, i + (N_RAW + 1))
                    for k in range(KT):
                        last = up_tile(s, t, k)
                    last.then_inc(ffn_ready, 1)

            for t in range(2):
                last_in_bank = N_TILES - 1 - (N_TILES - 1 - t) % 2
                pe.wait_ge(acc_free[t], last_in_bank // 2 + 1)
            pe.wait_ge(raw_used, N_RAW + 1)
            for k in range(KT):
                for h_half, ready, before, halves in ((h_hi, hh_done, KT, (w_hi, w_lo)), (h_lo, hl_done, KT // 2, (w_hi,))):
                    pe.wait_ge(ready, before + k + 1)
                    for t in range(2):
                        at = k * UW + t * P
                        for w in halves:
                            final = k == KT - 1 and h_half is h_lo
                            last = pe.matmul(bank[t][:, :], w[:, 1, at:at + P], h_half[:, k, :],
                                             start=(k == 0 and h_half is h_hi and w is w_hi), stop=final,
                                             skip_group_check=True)
                        if final:
                            last.then_inc(ffn_ready, 1)
            pe.wait_ge(rstd_half, 1)
            pe.wait_ge(rstd_done, 2)
            up(0, 1, first=True)
            with pe.Fori(1, FT // 2) as a:
                for s in range(2):
                    up(a, s)

            def down(a, s, first=False, final=False):
                j = 2 * a + s
                slot = 1 - s
                pe.wait_ge(raw_used, j + (N_RAW + FT + 1))
                pe.wait_ge(hs_lo_done, j + 1)
                for m in ((4, 5, 6, 7, 0, 1, 2, 3) if first else range(KT)):
                    if first and m < 4:
                        pe.wait_ge(tap_done, 4 * FT - 6 + 2 * m)
                    for k in range(2):
                        at = k * D + m * P
                        w = tuple(v[:, slot, at:at + P] for v in (w_hi, w_lo))
                        last = three(bank[m][:, :], w, (hs_hi[:, s, k, :], hs_lo[:, s, k, :]),
                                     first and k == 0, final and k == 1)
                    if final:
                        last.then_inc(down_tile, 1)
                        if m == KT - 2:
                            for i in range(NB):
                                to_tokens(i, range(4))
                if not final:
                    last.then_inc(down_done, 1)

            def to_tokens(i, parts):
                half, b = divmod(i, NB)
                for m in parts:
                    pe.wait_ge(xw_done, 4 * half + m + 1)
                    last = pe.transpose(bank[i][:, m * P:(m + 1) * P], x1[:, 4 * half + m, b * P:(b + 1) * P], ident)
                if m == 3:
                    last.then_inc(yt_ps, 1)

            down(0, 0, first=True)
            down(0, 1)
            with pe.Fori(1, DOWN_UNITS // 2) as a:
                for s in range(2):
                    down(a, s)
            down(DOWN_UNITS // 2, 0, final=True)
            for i in range(4, 7):
                to_tokens(i, range(3))
            pe.wait_ge(sum_done, SUMS[2] + KT - 1)
            pe.wait_ge(x2_done, KT)
            for b in range(NB):
                pe.matmul(bank[7][:, b:b + 1], sq_sum2[:, b * P:(b + 1) * P], ones[:, 0:1],
                          start=(b == 0), stop=False, skip_group_check=True)
            pe.wait_ge(sq_done, 3 * KT)
            for b in range(NB):
                last = pe.matmul(bank[7][:, b:b + 1], sq2[:, (KT - 1) % 2, b * P:(b + 1) * P], ones[:, 0:1],
                                 start=False, stop=True, skip_group_check=True)
            last.then_inc(ssq_ps, 1)
            for i in range(4, 7):
                to_tokens(i, range(3, 4))
            pe.wait_ge(ln_done, 3)
            to_tokens(7, range(4))


_INS = ["x", "c", "positions", "ada_w", "ada_b", "norm1_w", "w_in", "gla_gate_w2", "gla_gate_b", "gla_norm_w",
        "w_gla_branch", "w_attn_branch", "w_out", "norm2_w", "w_up", "conv_w", "conv_b", "w_down", "final_norm_w"]


def kernel(**inputs):
    import concourse.bacc as _bacc
    from concourse.bass_utils import run_bass_kernel_spmd as _run

    nc = _bacc.Bacc("TRN2", target_bir_lowering=False, num_devices=1)
    arrays, args = {}, []
    for name in _INS + ["shape_constants"]:
        a = np.ascontiguousarray(inputs[name]) if name in inputs else shape_constants()
        arrays[f"in_{name}_dram"] = a
        args.append(nc.dram_tensor(f"in_{name}_dram", a.shape, mybir.dt.from_np(a.dtype), kind="ExternalInput").ap())
    args.append(nc.dram_tensor("out_0_dram", (1, SEQ, D), F32, kind="ExternalOutput").ap())
    hybrid_block_kernel(nc, *args)
    r = _run(nc, [arrays], core_ids=[0])
    return r.results[0]["out_0_dram"]
```
